# Optimizing a Trainium2 kernel written in Bass

```python
import jax, jax.numpy as jnp
from jax import lax
import numpy as np

D_MODEL = 1024
BATCH = 1
SEQ = 2048
DEPTH = 1

D_MIX = D_MODEL
D_CONV = D_MIX // 2
CONV_KERNEL = 31
D_GLA_V = D_MIX - D_CONV
D_GLA_K = D_GLA_V // 2
GLA_HEADS = 4
HEAD_K = D_GLA_K // GLA_HEADS
HEAD_V = D_GLA_V // GLA_HEADS
GATE_RANK = 16
GATE_TAU = 16.0
CHUNK = 64
D_FF = ((8 * D_MODEL + 3 * 256 - 1) // (3 * 256)) * 256
D_IN = 2 * D_CONV + 2 * D_GLA_K + 2 * D_GLA_V + GATE_RANK
EPS = 1e-6

kernel_name = "hybrid_conv_gla_adaln_block"

def rms_norm(x, g):
    xf = x.astype(jnp.float32)
    y = xf * lax.rsqrt(jnp.mean(xf * xf, axis=-1, keepdims=True) + EPS)
    return (y * g.astype(jnp.float32)).astype(x.dtype)

def layer_norm(x, g, b):
    xf = x.astype(jnp.float32)
    mu = jnp.mean(xf, axis=-1, keepdims=True)
    var = jnp.mean(jnp.square(xf - mu), axis=-1, keepdims=True)
    y = (xf - mu) * lax.rsqrt(var + EPS)
    return (y * g.astype(jnp.float32) + b.astype(jnp.float32)).astype(x.dtype)

def causal_depthwise_conv(u, w, bias):
    k = w.shape[0]
    out = lax.conv_general_dilated(
        u, w[:, None, :], window_strides=(1,), padding=[(k - 1, 0)],
        dimension_numbers=('NWC', 'WIO', 'NWC'), feature_group_count=u.shape[-1])
    return out + bias

def gla_chunked(q, k, v, log_a):
    out_dtype = v.dtype
    b_sz, t_len, n_h, dk = q.shape
    dv = v.shape[-1]
    n_chunks = t_len // CHUNK

    def to_chunks(t):
        return t.astype(jnp.float32).reshape(b_sz, n_chunks, CHUNK, n_h, t.shape[-1]).transpose(1, 0, 3, 2, 4)

    qc, kc, vc, ac = to_chunks(q), to_chunks(k), to_chunks(v), to_chunks(log_a)
    causal = jnp.tril(jnp.ones((CHUNK, CHUNK), dtype=bool))[:, :, None]

    def step(state, inp):
        qi, ki, vi, ai = inp
        cum = jnp.cumsum(ai, axis=2)
        o_inter = jnp.einsum('bhld,bhde->bhle', qi * jnp.exp(cum), state)
        diff = cum[:, :, :, None, :] - cum[:, :, None, :, :]
        decay = jnp.exp(jnp.where(causal, diff, -jnp.inf))
        scores = jnp.einsum('bhid,bhijd,bhjd->bhij', qi, decay, ki)
        o_intra = jnp.einsum('bhij,bhje->bhie', scores, vi)
        cum_last = cum[:, :, -1:, :]
        new_state = jnp.exp(cum_last[:, :, 0, :, None]) * state + jnp.einsum(
            'bhld,bhle->bhde', ki * jnp.exp(cum_last - cum), vi)
        return new_state, o_inter + o_intra

    s0 = jnp.zeros((b_sz, n_h, dk, dv), jnp.float32)
    _, o = lax.scan(step, s0, (qc, kc, vc, ac))
    return o.transpose(1, 0, 3, 2, 4).reshape(b_sz, t_len, n_h, dv).astype(out_dtype)

def setup_inputs(seed: int = 0) -> dict:
    key = jax.random.key(seed)
    ks = jax.random.split(key, 20)
    f32 = jnp.float32

    def nrm(k, shape, scale):
        return jax.random.normal(k, shape, f32) * scale

    return {
        "x": nrm(ks[0], (BATCH, SEQ, D_MODEL), 1.0),
        "c": nrm(ks[1], (BATCH, D_MODEL), 1.0),
        "w_ada": nrm(ks[2], (DEPTH, D_MODEL, 6 * D_MODEL), D_MODEL ** -0.5),
        "b_ada": nrm(ks[3], (DEPTH, 6 * D_MODEL), 0.02),
        "g_mix": 1.0 + nrm(ks[4], (DEPTH, D_MODEL), 0.02),
        "w_in": nrm(ks[5], (DEPTH, D_MODEL, D_IN), D_MODEL ** -0.5),
        "conv_w": nrm(ks[6], (DEPTH, CONV_KERNEL, D_CONV), CONV_KERNEL ** -0.5),
        "conv_b": nrm(ks[7], (DEPTH, D_CONV), 0.02),
        "ln_g": 1.0 + nrm(ks[8], (DEPTH, D_CONV), 0.02),
        "ln_b": nrm(ks[9], (DEPTH, D_CONV), 0.02),
        "w_a2": nrm(ks[10], (DEPTH, GATE_RANK, D_GLA_K), GATE_RANK ** -0.5),
        "b_a2": nrm(ks[11], (DEPTH, D_GLA_K), 0.02),
        "gla_norm_g": 1.0 + nrm(ks[12], (DEPTH, HEAD_V), 0.02),
        "w_out": nrm(ks[13], (DEPTH, D_MIX, D_MODEL), D_MIX ** -0.5),
        "g_ffn": 1.0 + nrm(ks[14], (DEPTH, D_MODEL), 0.02),
        "w_ffn_in": nrm(ks[15], (DEPTH, D_MODEL, 2 * D_FF), D_MODEL ** -0.5),
        "w_ffn_out": nrm(ks[16], (DEPTH, D_FF, D_MODEL), D_FF ** -0.5),
        "w_ada_final": nrm(ks[17], (D_MODEL, 2 * D_MODEL), D_MODEL ** -0.5),
        "b_ada_final": nrm(ks[18], (2 * D_MODEL,), 0.02),
        "g_final": 1.0 + nrm(ks[19], (D_MODEL,), 0.02),
    }

def reference(x, c, w_ada, b_ada, g_mix, w_in, conv_w, conv_b, ln_g, ln_b, w_a2, b_a2,
              gla_norm_g, w_out, g_ffn, w_ffn_in, w_ffn_out, w_ada_final, b_ada_final, g_final):
    b_sz, t_len, _ = x.shape
    c_act = jax.nn.silu(c)
    split_pts = [D_CONV, 2 * D_CONV, 2 * D_CONV + D_GLA_K, 2 * D_CONV + 2 * D_GLA_K,
                 2 * D_CONV + 2 * D_GLA_K + D_GLA_V, 2 * D_CONV + 2 * D_GLA_K + 2 * D_GLA_V]

    for l in range(DEPTH):
        mod = (c_act @ w_ada[l] + b_ada[l])[:, None, :]
        sh1, sc1, gt1, sh2, sc2, gt2 = jnp.split(mod, 6, axis=-1)

        h = rms_norm(x, g_mix[l]) * (1.0 + sc1) + sh1
        proj = h @ w_in[l]
        cv, cg, q, k, v, og, a_low = jnp.split(proj, split_pts, axis=-1)

        u = cv * jax.nn.sigmoid(cg)
        u = causal_depthwise_conv(u, conv_w[l], conv_b[l])
        y_conv = jax.nn.silu(layer_norm(u, ln_g[l], ln_b[l]))

        log_a = jax.nn.log_sigmoid(a_low @ w_a2[l] + b_a2[l]) / GATE_TAU
        qh = q.reshape(b_sz, t_len, GLA_HEADS, HEAD_K) * (HEAD_K ** -0.5)
        kh = k.reshape(b_sz, t_len, GLA_HEADS, HEAD_K)
        vh = v.reshape(b_sz, t_len, GLA_HEADS, HEAD_V)
        ah = log_a.reshape(b_sz, t_len, GLA_HEADS, HEAD_K)
        o = gla_chunked(qh, kh, vh, ah)
        o = rms_norm(o, gla_norm_g[l]).reshape(b_sz, t_len, D_GLA_V)
        y_gla = o * jax.nn.silu(og)

        mix = jnp.concatenate([y_conv, y_gla], axis=-1) @ w_out[l]
        x = x + gt1 * mix

        h = rms_norm(x, g_ffn[l]) * (1.0 + sc2) + sh2
        gate, up = jnp.split(h @ w_ffn_in[l], 2, axis=-1)
        x = x + gt2 * ((jax.nn.silu(gate) * up) @ w_ffn_out[l])

    fmod = (c_act @ w_ada_final + b_ada_final)[:, None, :]
    shf, scf = jnp.split(fmod, 2, axis=-1)
    return rms_norm(x, g_final) * (1.0 + scf) + shf


_drawn_inputs = setup_inputs


def setup_inputs(seed=0):
    import zlib

    import numpy as np

    out = dict(_drawn_inputs(seed))
    spreads = {}
    factors = {'g_mix': 4.868,
     'conv_b': 48.919,
     'ln_g': 64.0,
     'ln_b': 64.0,
     'b_a2': 8.0,
     'gla_norm_g': 8.0,
     'g_ffn': 15.584,
     'g_final': 9.499,
     'b_ada_final': 3.147}
    for name, (base, spread) in spreads.items():
        noise = np.random.default_rng([zlib.crc32(name.encode()), seed]).standard_normal(out[name].shape)
        drawn = base * np.exp(spread * noise) if base else spread * noise
        out[name] = __import__('jax').numpy.asarray(drawn.astype(out[name].dtype))
    for name, factor in factors.items():
        out[name] = (out[name] * factor).astype(out[name].dtype)
    return out
```

```python
from contextlib import ExitStack

import numpy as np

import concourse.bass as bass
from concourse import mybir

ALU = mybir.AluOpType
ACT = mybir.ActivationFunctionType
F32 = mybir.dt.float32
F32R = mybir.dt.float32r
U8 = mybir.dt.uint8

P = 128
EPS = 1e-6
RING = 3
NT = 512
GATE_TAU = 16.0
C = 128
LEVELS = [64, 32, 16, 8, 4, 2, 1]


class Line:

    def __init__(self, sem, names, ahead=0):
        self.sem, self.names, self.next, self.ahead = sem, list(names), 0, ahead

    def begin(self, engine):
        engine.sem_inc(self.sem, self.ahead * len(self.names))

    def value(self, unit, name):
        return unit * len(self.names) + (self.ahead * len(self.names) + self.names.index(name) + 1)

    def done(self, instruction, name):
        assert self.names[self.next] == name, (self.names[self.next], name)
        self.next = (self.next + 1) % len(self.names)
        instruction.then_inc(self.sem, 1)

    def wait(self, engine, unit, name):
        engine.wait_ge(self.sem, self.value(unit, name))


class Place:

    def __init__(self, base, step, loop, per_loop):
        self.slot = (base + step) % RING
        self.uses = loop * per_loop + (base + step) // RING
        self.number = loop * (RING * per_loop) + (base + step)


def tiles(engine, count, body):
    with engine.Fori(0, count // RING) as i:
        for s in range(RING):
            body(i, s)
    for s in range(count % RING):
        body(count // RING, s)


def block_kernel(nc, x, c, w_ada, b_ada, g_mix, w_in, conv_w, conv_b, ln_g, ln_b, w_a2, b_a2,
                 gla_norm_g, w_out, g_ffn, w_ffn_in, w_ffn_out, w_ada_final, b_ada_final, g_final,
                 identity, level_masks, out):
    T, D = x.shape[1], x.shape[2]
    KD = D // P
    TB = T // 2
    HB = TB // NT
    G = T // NT
    TAPS, DC = conv_w.shape[1], conv_w.shape[2]
    CT = DC // P
    RANK, DK = w_a2.shape[1], w_a2.shape[2]
    KT = DK // P
    DV = gla_norm_g.shape[1]
    HV = D - DC
    VT = HV // P
    HEADS = HV // DV
    HEAD_K = DK // HEADS
    DF = w_ffn_out.shape[1]
    FT = DF // P
    CHUNKS = T // C
    PAD = TAPS - 1
    CV, CG, Q = 0, CT, 2 * CT
    K, V = Q + KT, Q + 2 * KT
    OG = V + VT
    NA = OG + VT
    LA = NA
    assert DV == P and HEAD_K * 2 == P and KD == 8 and VT == HEADS and FT % 2 == 0 and TB % NT == 0

    x2 = x.rearrange("a t d -> (a t) d")
    out2 = out.rearrange("a t d -> (a t) d")
    wada = w_ada.rearrange("a k m -> (a k) m")
    win = w_in.rearrange("a (k p) m -> p (a k) m", p=P)
    wout = w_out.rearrange("a (k p) m -> p (a k) m", p=P)
    wfi = w_ffn_in.rearrange("a (k p) m -> p (a k) m", p=P)
    wfo = w_ffn_out.rearrange("a f m -> (a f) m")

    with ExitStack() as ctx:
        def sem(name):
            return ctx.enter_context(nc.semaphore(name))

        base = (nc.sbuf_base + 63) // 64 * 64
        room = nc.sbuf_usable_end - base - 64
        arena = ctx.enter_context(nc.sbuf_tensor("arena", [P, room // 4], F32))

        def at(name, offset, shape, dtype=F32):
            return nc.alloc_sbuf_tensor_at(name, [P, *shape], dtype, offset=base + offset)

        KB = 1024
        ident = at("ident", 0, [P])
        ones = at("ones", 512, [P])
        pvec = at("pvec", 1024, [112])
        taps = at("taps", 1472, [TAPS * CT])
        modv = at("modv", 1984, [64])
        gain1 = at("gain1", 2240, [KD])
        gain2 = at("gain2", 2272, [KD])
        gainf = at("gainf", 2304, [KD])
        eps = at("eps", 2336, [1])
        cact = at("cact", 2368, [KD])
        ssq4 = at("ssq4", 2432, [2, 4])
        rstd4 = at("rstd4", 2464, [2, 4])
        a2 = at("a2", 2560, [DK])
        WO = 2560 + 4 * DK
        w_raw = at("w_raw", WO, [RING, KD, P])
        w_hi = at("w_hi", WO + 12 * KB, [RING, KD, P], F32R)
        w_lo = at("w_lo", WO + 24 * KB, [RING, KD, P], F32R)
        HO = WO + 36 * KB
        h_hi = at("h_hi", HO, [KD, T], F32R)
        h_lo = at("h_lo", HO + 64 * KB, [KD, T], F32R)
        RO = HO + 128 * KB
        rows = at("rows", RO + 24 * KB, [2, P])
        m_raw = at("m_raw", RO, [4, KD * P])
        m_acc = at("m_acc", RO + 16 * KB, [KD * P])
        xnat = at("xnat", RO, [2, 4, D])
        p_tmp = at("p_tmp", RO + 32 * KB, [2, NT])
        p_junk = at("p_junk", RO + 36 * KB, [D], mybir.dt.bfloat16)
        stage = at("stage", RO + 20 * KB, [RING, NT])
        al_raw = at("al_raw", RO, [KD, RANK])
        al_hi = at("al_hi", RO + 1 * KB, [KD, P], F32R)
        al_lo = at("al_lo", RO + 5 * KB, [KD, P], F32R)
        alow = at("alow", RO + 9 * KB, [NT])
        zt = at("zt", RO + 11 * KB, [KT, NT])
        zm = at("zm", RO + 15 * KB, [KT, NT])
        cvb = at("cvb", HO, [T])
        cgb = at("cgb", HO + 8 * KB, [T])
        ub = at("ub", HO + 16 * KB, [PAD + T + 2])
        acc_a = at("acc_a", HO + 26 * KB, [T])
        acc_b = at("acc_b", HO + 34 * KB, [T])
        GO = HO + 64 * KB
        g_qk = at("g_qk", GO, [2 * KT, C])
        g_la = at("g_la", GO + 2 * KB, [KT, C])
        g_vt = at("g_vt", GO + 3 * KB, [VT, C])
        g_lev = at("g_lev", GO + 5 * KB, [len(LEVELS), KT * C])
        g_cum = at("g_cum", GO + 12 * KB, [KT, C])
        g_ecum = at("g_ecum", GO + 13 * KB, [KT, C])
        g_qd = at("g_qd", GO + 32 * KB, [KT, 2, C])
        g_qb = at("g_qb", GO + 34 * KB, [KT, 2, C])
        g_ql = at("g_ql", GO + 36 * KB, [len(LEVELS), KT, 2, C // 2])
        g_kd = at("g_kd", GO + 15 * KB, [KT, C])
        g_kn = at("g_kn", GO + 16 * KB, [KT * P])
        g_vn = at("g_vn", GO + 17 * KB, [VT * P])
        g_st = at("g_st", GO + 19 * KB, [HEADS, C])
        g_state = at("g_state", GO + 21 * KB, [KT, DV])
        g_sq = at("g_sq", GO + 22 * KB, [HEADS * C])
        g_rs = at("g_rs", GO + 24 * KB, [HEADS * C])
        g_on = at("g_on", GO + 26 * KB, [HEADS, C])
        g_one = at("g_one", GO + 28 * KB, [C])
        MASKS = (len(LEVELS) + 2) * HEADS * C // 2
        g_mask = at("g_mask", RO + 38 * KB, [MASKS], U8)
        mask_f = at("mask_f", HO, [MASKS])
        y_hi = at("y_hi", HO, [KD, TB], F32R)
        y_lo = at("y_lo", HO + 32 * KB, [KD, TB], F32R)
        h2_hi = at("h2_hi", HO + 64 * KB, [KD, TB], F32R)
        h2_lo = at("h2_lo", HO + 96 * KB, [KD, TB], F32R)
        cin = at("cin", HO + 64 * KB, [CT, TB])
        oin = at("oin", HO + 80 * KB, [VT, TB])
        ogin = at("ogin", HO + 96 * KB, [VT, TB])
        xin = at("xin", HO + 112 * KB, [4, D])
        ln_sum = at("ln_sum", RO, [TB])
        ln_sq = at("ln_sq", RO + 4 * KB, [2, TB])
        ln_rs = at("ln_rs", RO + 12 * KB, [TB])
        xacc = at("xacc", RO, [KD, TB])
        ssq = at("ssq", RO + 32 * KB, [TB])
        c_sq = at("c_sq", HO + 64 * KB, [2, NT])
        n_rs = at("n_rs", HO, [TB])
        n_t = at("n_t", HO + 4 * KB, [2, TB])
        act_hi = at("act_hi", HO, [2, TB], F32R)
        act_lo = at("act_lo", HO + 8 * KB, [2, TB], F32R)
        sil = at("sil", HO + 16 * KB, [2, NT])
        af = at("af", HO + 20 * KB, [2, NT])
        e_sq = at("e_sq", HO + 24 * KB, [2, TB])
        e_rs = at("e_rs", HO + 32 * KB, [TB])
        e_out = at("e_out", HO + 36 * KB, [2, D])
        assert RO + 38 * KB + MASKS <= room, (RO, room)

        banks = [ctx.enter_context(nc.psum_tensor(f"bank{b}", [P, NT], F32)) for b in range(RING)]
        side = ctx.enter_context(nc.psum_tensor("side", [P, 8 - RING, NT], F32))

        proj = nc.dram_tensor("proj", [NA + KT, P, T], F32, kind="Internal").ap()
        convd = nc.dram_tensor("convd", [CT, P, T], F32, kind="Internal").ap()
        od = nc.dram_tensor("od", [VT, P, T], F32, kind="Internal").ap()

        names = [("b_ada", b_ada.rearrange("a (r p) -> (a r) p", p=P)),
                 ("b_fin", b_ada_final.rearrange("(r p) -> r p", p=P)),
                 ("g_mix", g_mix.rearrange("a (r p) -> (a r) p", p=P)),
                 ("g_ffn", g_ffn.rearrange("a (r p) -> (a r) p", p=P)),
                 ("g_fin", g_final.rearrange("(r p) -> r p", p=P)),
                 ("c", c.rearrange("a (r p) -> (a r) p", p=P)),
                 ("conv_b", conv_b.rearrange("a (r p) -> (a r) p", p=P)),
                 ("ln_g", ln_g.rearrange("a (r p) -> (a r) p", p=P)),
                 ("ln_b", ln_b.rearrange("a (r p) -> (a r) p", p=P)),
                 ("b_a2", b_a2.rearrange("a (r p) -> (a r) p", p=P)),
                 ("gla_g", gla_norm_g)]
        col, ncol = {}, 0
        for name, rows_of in names:
            col[name] = ncol
            ncol += rows_of.shape[0]
        assert ncol <= P

        def vec(name, j=0):
            return pvec[:, col[name] + j:col[name] + j + 1]

        def mod(m, j):
            return modv[:, m * KD + j:m * KD + j + 1]

        const_in = sem("const_in")
        setup_p = Line(sem("setup_p"), ["rows", "taps"])
        setup_v = Line(sem("setup_v"), ["ones", "eps", "pvec", "taps", "mask", "pad", "al_hi", "al_lo"])
        setup_a = Line(sem("setup_a"), ["cact"])
        w_loaded = [sem(f"w_loaded{s}") for s in range(RING)]
        w_high = sem("w_high")
        w_low = sem("w_low")
        product = sem("product")
        m_loaded = [sem(f"m_loaded{s}") for s in range(4)]
        mod_v = Line(sem("mod_v"), [f"k{k}" for k in range(KD)] + ["vec"], ahead=1)
        mod_p = Line(sem("mod_p"), ["sum"])
        gains_v = Line(sem("gains_v"), ["g1", "g2", "gf"])
        x_loaded = [sem(f"x_loaded{s}") for s in range(2)]
        prep_a = Line(sem("prep_a"), [f"sq{t}" for t in range(4)] + ["ln", "rstd"] + [f"hi{k}" for k in range(KD)], ahead=1)
        prep_v = Line(sem("prep_v"), [f"xn{t}" for t in range(4)] + [f"{s}{k}" for k in range(KD) for s in ("t", "lo")], ahead=1)
        prep_p = Line(sem("prep_p"), [f"k{k}" for k in range(KD)])
        al_loaded = sem("al_loaded")
        al_v = Line(sem("al_v"), ["hi", "lo"])
        z_p = Line(sem("z_p"), ["alow", "z0", "z1"])
        z_a = Line(sem("z_a"), ["alow", "zb0", "zb1", "abs", "exp", "ln"], ahead=1)
        z_v = Line(sem("z_v"), ["min", "la"])
        z_stored = sem("z_stored")
        staged = Line(sem("staged"), ["copy"], ahead=RING)
        stored = [sem(f"stored{b}") for b in range(RING)]
        cv_loaded = sem("cv_loaded")
        cv_a = Line(sem("cv_a"), ["sig"])
        cv_v = Line(sem("cv_v"), ["u"] + [f"tap{k}" for k in range(TAPS)] + ["sum"], ahead=1)
        cv_stored = sem("cv_stored")
        picks = sem("picks")
        g_zero = Line(sem("g_zero"), ["st", "state", "qd", "qb", "ql", "one"])
        g_loaded = sem("g_loaded")
        g_stored = sem("g_stored")
        L = range(len(LEVELS))
        gla_v = Line(sem("gla_v"), ["cum0", "cum1"] + [f"sub{l}" for l in L] + ["qd0", "qd1", "kd"]
                     + [f"{s}{l}" for l in L for s in ("qa", "qb", "k")]
                     + [f"pick{l}" for l in L] + ["pickd", "st0", "st1", "gain", "on"], ahead=1)
        gla_a = Line(sem("gla_a"), ["qb0", "qb1", "abs", "exp", "ecum", "kdec0", "kdec1", "vn", "kn", "sq", "ln", "rstd"])
        gla_p = Line(sem("gla_p"), ["vn", "kn", "lev", "diag", "o", "state", "ss"], ahead=1)
        c_loaded = sem("c_loaded")
        x2_loaded = sem("x2_loaded")
        ln_v = Line(sem("ln_v"), ["s1", "s2", "s3"] + [f"d{j}" for j in range(CT)] + [f"q{j}" for j in range(1, CT)]
                    + [f"n{j}" for j in range(CT)] + [f"lo{j}" for j in range(CT)]
                    + [f"m{j}" for j in range(VT)] + [f"olo{j}" for j in range(VT)])
        ln_p = Line(sem("ln_p"), ["mean", "var"])
        ln_a = Line(sem("ln_a"), [f"q{j}" for j in range(CT)] + ["ln", "rstd"] + [f"y{j}" for j in range(CT)]
                    + [f"hi{j}" for j in range(CT)] + [f"s{j}" for j in range(VT)] + [f"ohi{j}" for j in range(VT)])
        turns = [f"g{g}k{k}" for g in range(HB) for k in range(KD)]
        xt_p = Line(sem("xt_p"), turns)
        xt_a = Line(sem("xt_a"), turns)
        res_v = Line(sem("res_v"), ["x", "ss"], ahead=RING)
        res_a = Line(sem("res_a"), ["sq"])
        zero_v = Line(sem("zero_v"), ["c", "e"])
        n_p = Line(sem("n_p"), ["ss"])
        n_a = Line(sem("n_a"), ["ln", "rstd"] + [f"hi{k}" for k in range(KD)])
        n_v = Line(sem("n_v"), [f"{s}{k}" for k in range(KD) for s in ("t", "lo")])
        f_a = Line(sem("f_a"), ["silu", "hi"], ahead=2)
        f_v = Line(sem("f_v"), ["a", "lo"], ahead=2)
        OUTS = KD * HB
        f_o = Line(sem("f_o"), [f"o{q}" for q in range(OUTS)], ahead=1)
        e_a = Line(sem("e_a"), [f"sq{k}" for k in range(KD)] + ["ln", "rstd"] + [f"b{k}" for k in range(KD)])
        e_v = Line(sem("e_v"), [f"ss{k}" for k in range(KD)] + [f"t{k}" for k in range(KD)])
        e_p = Line(sem("e_p"), ["ss"] + [f"t{t}" for t in range(TB // P)])
        e_c = Line(sem("e_c"), [f"t{t}" for t in range(TB // P)])
        out_stored = [sem(f"out_stored{s}") for s in range(2)]

        FI = FT // 2
        NC0, GC0 = NA, NA * G
        NH, GH = KD + 6 * FI, KD * HB + (4 * HB + OUTS) * FI
        PAIRS = 2 * HB

        block = ctx.enter_context(nc.Block())

        def half(h):
            return slice(h * NT, (h + 1) * NT)

        def pairs(ap, s):
            return ap.rearrange("p (r w) -> p r w", w=2 * s)

        @block.sync
        def _(sp):
            def load(place, source):
                sp.wait_ge(w_low, place.number + 1)
                sp.dma_start(w_raw[:, place.slot], source).then_inc(w_loaded[place.slot], 16)

            sp.dma_start(ident[:], identity).then_inc(const_in, 16)
            for name, rows_of in names:
                n = rows_of.shape[0]
                sp.dma_start(rows[col[name]:col[name] + n, 0, :], rows_of).then_inc(const_in, 16)
            for t in range(TAPS):
                sp.dma_start(rows[t * CT:(t + 1) * CT, 1, :],
                             conv_w[0, t:t + 1, :].rearrange("t (j p) -> (t j) p", p=P)).then_inc(const_in, 16)
            sp.dma_start(mask_f[:], level_masks).then_inc(const_in, 16)
            sp.dma_start(a2[0:RANK, :], w_a2.rearrange("a r d -> (a r) d")).then_inc(const_in, 16)

            tiles(sp, NA, lambda i, s: load(Place(0, s, i, 1), win[:, :, bass.ds((i * RING + s) * P, P)]))
            for b in range(2):
                n0 = NC0 + b * NH
                tiles(sp, KD, lambda i, s: load(Place(n0, s, i, 1), wout[:, :, bass.ds((i * RING + s) * P, P)]))
                with sp.Fori(0, FI) as i:
                    for f in range(2):
                        for u in range(2):
                            load(Place(n0 + KD, 2 * f + u, i, 2),
                                 wfi[:, :, bass.ds(i * (2 * P) + (f * P + u * DF), P)])
                    for f in range(2):
                        load(Place(n0 + KD, 4 + f, i, 2),
                             wfo[bass.ds(i * (2 * P) + f * P, P), :].rearrange("p (k m) -> p k m", k=KD))

        @block.gpsimd
        def _(pool):
            def mod_rows(m, source):
                for k in range(KD):
                    mod_v.wait(pool, m if k >= 4 else m - 1, f"k{k - 4 if k >= 4 else k + 4}")
                    pool.dma_start(m_raw[:, k % 4], source[k * P:(k + 1) * P, :]).then_inc(m_loaded[k % 4], 16)

            for m in range(2):
                mod_rows(m, wada[:, m * D:(m + 1) * D])
            mod_v.wait(pool, 1, "k7")
            mod_p.wait(pool, 1, "sum")
            for g in range(G):
                if g >= 2:
                    prep_p.wait(pool, g - 2, f"k{KD - 1}")
                pool.dma_start(xnat[:, g % 2], x2[g * NT:(g + 1) * NT, :].rearrange("(t p) d -> p t d", p=P)).then_inc(x_loaded[g % 2], 16)
            prep_p.wait(pool, G - 1, f"k{KD - 1}")
            pool.dma_start(al_raw[:], win[:, :, NA * P:NA * P + RANK]).then_inc(al_loaded, 16)
            pool.wait_ge(z_stored, 16 * (G + 1))
            with pool.Fori(0, 4) as i:
                mod_rows(i + 2, wada[:, bass.ds(i * D + 2 * D, D)])
            with pool.Fori(0, 2) as i:
                mod_rows(i + 6, w_ada_final[:, bass.ds(i * D, D)])

            for b in range(RING):
                pool.wait_ge(stored[b], 16 * (1 + (NA * G - b + RING - 1) // RING))
            pool.wait_ge(product, NA * G)
            with pool.Fori(0, CT) as j:
                cv_v.wait(pool, j - 1, "u")
                pool.dma_start(cvb[:], proj[bass.ds(j + CV, 1)].rearrange("a p t -> p (a t)")).then_inc(cv_loaded, 16)
                pool.dma_start(cgb[:], proj[bass.ds(j + CG, 1)].rearrange("a p t -> p (a t)")).then_inc(cv_loaded, 16)
            with pool.Fori(0, CHUNKS) as n:
                gla_p.wait(pool, n - 1, "diag")
                gla_v.wait(pool, n - 1, f"k{L[-1]}")
                tok = bass.ds(n * C, C)
                pool.dma_start(g_qk[:], proj[Q:Q + 2 * KT, :, tok].rearrange("a p t -> p a t")).then_inc(g_loaded, 16)
                pool.dma_start(g_vt[:], proj[V:V + VT, :, tok].rearrange("a p t -> p a t")).then_inc(g_loaded, 16)
                pool.dma_start(g_la[:], proj[LA:LA + KT, :, tok].rearrange("a p t -> p a t")).then_inc(g_loaded, 16)
            pool.wait_ge(cv_stored, 16 * (CT + 1))
            pool.wait_ge(g_stored, 16 * (CHUNKS + 1))
            for b in range(2):
                tok = slice(b * TB, (b + 1) * TB)
                if b:
                    pool.wait_ge(product, GC0 + GH)
                pool.dma_start(cin[:], convd[:, :, tok].rearrange("a p t -> p a t")).then_inc(c_loaded, 16)
                pool.dma_start(oin[:], od[:, :, tok].rearrange("a p t -> p a t")).then_inc(c_loaded, 16)
                pool.dma_start(ogin[:], proj[OG:OG + VT, :, tok].rearrange("a p t -> p a t")).then_inc(c_loaded, 16)
                for g in range(HB):
                    if g:
                        xt_p.wait(pool, b, f"g{g - 1}k{KD - 1}")
                    r0 = b * TB + g * NT
                    pool.dma_start(xin[:], x2[r0:r0 + NT, :].rearrange("(t p) d -> p t d", p=P)).then_inc(x2_loaded, 16)
                for t in range(TB // P):
                    e_c.wait(pool, b, f"t{t}")
                    r0 = b * TB + t * P
                    pool.dma_start(out2[r0:r0 + P, :], e_out[:, t % 2]).then_inc(out_stored[t % 2], 16)
            for s in range(2):
                pool.wait_ge(out_stored[s], 16 * TB // P)

        @block.scalar
        def _(act):
            for line in (prep_a, z_a, staged, f_a):
                line.begin(act)
            for s in (z_stored, *stored, cv_stored, g_stored):
                act.sem_inc(s, 16)

            def high(place, used):
                act.wait_ge(w_loaded[place.slot], place.uses * 16 + 16)
                if used is not None:
                    act.wait_ge(product, used)
                act.activation(w_hi[:, place.slot], w_raw[:, place.slot], ACT.Copy).then_inc(w_high, 1)

            for s in range(RING):
                high(Place(0, s, 0, 1), None)
            setup_v.wait(act, 0, "pvec")
            setup_a.done(act.activation(cact[:], pvec[:, col["c"]:col["c"] + KD], ACT.Silu), "cact")
            setup_v.wait(act, 0, "eps")

            with act.Fori(0, G // 2) as i:
                for s in range(2):
                    g = i * 2 + s
                    act.wait_ge(x_loaded[s], i * 16 + 16)
                    for t in range(4):
                        if t:
                            prep_a.wait(act, g, f"sq{t - 1}")
                        prep_a.done(act.activation(p_junk[:], xnat[:, s, t], ACT.Square,
                                                   accum_out=ssq4[:, s, t:t + 1]), f"sq{t}")
                    prep_a.wait(act, g, "sq3")
                    prep_a.done(act.activation(rstd4[:, s], ssq4[:, s], ACT.Ln, scale=1.0 / D, bias=eps[:]), "ln")
                    prep_a.wait(act, g, "ln")
                    prep_a.done(act.activation(rstd4[:, s], rstd4[:, s], ACT.Exp, scale=-0.5), "rstd")
                    for k in range(KD):
                        prep_v.wait(act, g, f"t{k}")
                        prep_a.done(act.activation(h_hi[:, k, bass.ds(g * NT, NT)], p_tmp[:, k % 2], ACT.Copy), f"hi{k}")

            with act.Fori(0, G) as g:
                z_p.wait(act, g, "alow")
                z_a.done(act.activation(alow[0:RANK, :], side[0:RANK, 0], ACT.Copy), "alow")
                act.wait_ge(z_stored, g * 16 + 16)
                for f in range(KT):
                    z_p.wait(act, g, f"z{f}")
                    z_a.done(act.activation(zt[:, f], side[:, 1 + f], ACT.Identity, bias=vec("b_a2", f)), f"zb{f}")
                z_v.wait(act, g, "min")
                z_a.done(act.activation(zt[:], zt[:], ACT.Abs), "abs")
                z_a.wait(act, g, "abs")
                z_a.done(act.activation(zt[:], zt[:], ACT.Exp, scale=-1.0), "exp")
                z_a.wait(act, g, "exp")
                z_a.done(act.activation(zt[:], zt[:], ACT.Ln, bias=ones[:, 0:1]), "ln")
                z_v.wait(act, g, "la")
                act.dma_start(proj[LA:LA + KT, :, bass.ds(g * NT, NT)].rearrange("a p t -> p a t"), zm[:]).then_inc(z_stored, 16)

            def in_proj(i, s):
                for h in range(G):
                    p = Place(0, s * G + h, i, G)
                    act.wait_ge(product, p.number + 1)
                    act.wait_ge(stored[p.slot], p.uses * 16 + 16)
                    staged.done(act.activation(stage[:, p.slot], banks[p.slot][:], ACT.Copy), "copy")
                    staged.wait(act, p.number, "copy")
                    act.dma_start(proj[bass.ds(i * RING + s, 1), :, h * NT:(h + 1) * NT].rearrange("a p t -> p (a t)"),
                                  stage[:, p.slot]).then_inc(stored[p.slot], 16)
                high(Place(RING, s, i, 1), i * (RING * G) + (s + 1) * G)

            tiles(act, NA, in_proj)

            with act.Fori(0, CT) as j:
                act.wait_ge(cv_loaded, j * 32 + 32)
                cv_a.done(act.activation(cgb[:], cgb[:], ACT.Sigmoid), "sig")
                cv_v.wait(act, j, "sum")
                act.dma_start(convd[bass.ds(j, 1)].rearrange("a p t -> p (a t)"), acc_a[:]).then_inc(cv_stored, 16)

            g_zero.wait(act, 0, "one")
            with act.Fori(0, CHUNKS) as n:
                act.wait_ge(g_loaded, n * 48 + 48)
                for e in range(2):
                    r = slice(e * HEAD_K, (e + 1) * HEAD_K)
                    gla_a.done(act.activation(g_qb[r, :, e], g_qk[r, 0:KT], ACT.Copy), f"qb{e}")
                gla_v.wait(act, n, f"sub{L[-1]}")
                gla_a.done(act.activation(g_lev[:], g_lev[:], ACT.Abs), "abs")
                gla_a.wait(act, n, "abs")
                gla_a.done(act.activation(g_lev[:], g_lev[:], ACT.Exp, scale=-1.0), "exp")
                gla_a.done(act.activation(g_ecum[:], g_cum[:], ACT.Exp), "ecum")
                for f in range(KT):
                    gla_a.done(act.activation(g_kd[:, f], g_cum[:, f], ACT.Exp, scale=-1.0,
                                              bias=g_cum[:, f, C - 1:C]), f"kdec{f}")
                gla_p.wait(act, n, "vn")
                gla_a.done(act.activation(g_vn[:], side[:, 0], ACT.Copy), "vn")
                gla_p.wait(act, n, "kn")
                gla_a.done(act.activation(g_kn[:], side[:, 1, 0:KT * P], ACT.Copy), "kn")
                gla_p.wait(act, n, "o")
                gla_a.done(act.activation(g_sq[:], side[:, 0], ACT.Square), "sq")
                gla_p.wait(act, n, "ss")
                gla_a.done(act.activation(g_rs[:], side[:, 2], ACT.Ln, scale=1.0 / (DV * HEAD_K), bias=eps[:]), "ln")
                gla_a.wait(act, n, "ln")
                gla_a.done(act.activation(g_rs[:], g_rs[:], ACT.Exp, scale=-0.5), "rstd")
                gla_v.wait(act, n, "on")
                act.dma_start(od[:, :, bass.ds(n * C, C)].rearrange("a p t -> p a t"), g_on[:]).then_inc(g_stored, 16)

            for b in range(2):
                n0, g0 = NC0 + b * NH, GC0 + b * GH
                for j in range(CT):
                    ln_v.wait(act, b, f"d{j}")
                    if j >= 2:
                        ln_v.wait(act, b, f"q{j - 1}")
                    ln_a.done(act.activation(ln_sq[:, j % 2], cin[:, j], ACT.Square), f"q{j}")
                ln_p.wait(act, b, "var")
                ln_a.done(act.activation(ln_rs[:], side[:, 2:4], ACT.Ln, scale=1.0 / DC, bias=eps[:]), "ln")
                ln_a.wait(act, b, "ln")
                ln_a.done(act.activation(ln_rs[:], ln_rs[:], ACT.Exp, scale=-0.5), "rstd")
                for j in range(CT):
                    ln_v.wait(act, b, f"n{j}")
                    ln_a.done(act.activation(cin[:, j], cin[:, j], ACT.Silu, scale=vec("ln_g", j), bias=vec("ln_b", j)), f"y{j}")
                for j in range(CT):
                    ln_a.wait(act, b, f"y{j}")
                    ln_a.done(act.activation(y_hi[:, j], cin[:, j], ACT.Copy), f"hi{j}")
                act.wait_ge(c_loaded, 48 * (b + 1))
                for j in range(VT):
                    ln_a.done(act.activation(ogin[:, j], ogin[:, j], ACT.Silu), f"s{j}")
                for j in range(VT):
                    ln_v.wait(act, b, f"m{j}")
                    ln_a.done(act.activation(y_hi[:, CT + j], oin[:, j], ACT.Copy), f"ohi{j}")
                for g in range(HB):
                    for k in range(KD):
                        xt_p.wait(act, b, f"g{g}k{k}")
                        xt_a.done(act.activation(xacc[:, k, half(g)], side[:, k % 4], ACT.Copy), f"g{g}k{k}")

                def squares(i, s):
                    for h in range(HB):
                        u = i * (RING * HB) + (b * KD * HB + s * HB + h)
                        res_v.wait(act, u - 2, "ss")
                        res_v.wait(act, u, "x")
                        res_a.done(act.activation(c_sq[:, h], xacc[:, bass.ds(i * RING + s, 1), half(h)]
                                                  .rearrange("p a t -> p (a t)"), ACT.Square), "sq")
                    high(Place(n0 + RING, s, i, 1), i * (RING * HB) + (g0 + (s + 1) * HB))

                tiles(act, KD, squares)
                n_p.wait(act, b, "ss")
                n_a.done(act.activation(n_rs[:], side[:, 0:HB], ACT.Ln, scale=1.0 / D, bias=eps[:]), "ln")
                n_a.wait(act, b, "ln")
                n_a.done(act.activation(n_rs[:], n_rs[:], ACT.Exp, scale=-0.5), "rstd")
                for k in range(KD):
                    n_v.wait(act, b, f"t{k}")
                    n_a.done(act.activation(h2_hi[:, k], n_t[:, k % 2], ACT.Identity, bias=mod(3, k)), f"hi{k}")

                nf, gf = n0 + KD, g0 + KD * HB

                def ffn(i, last):
                    i0 = i * (4 * HB + OUTS) + gf
                    for f in range(2):
                        for h in range(HB):
                            u = i * PAIRS + (b * FI * PAIRS + f * HB + h)
                            pg = Place(gf, 2 * (f * HB + h), i, (4 * HB + OUTS) // RING)
                            act.wait_ge(product, pg.number + 1)
                            f_v.wait(act, u - 2, "a")
                            f_a.done(act.activation(sil[:, h], banks[pg.slot][:], ACT.Silu), "silu")
                            if (f, h) == (1, HB - 1):
                                high(Place(nf + RING, 2, i, 2), i0 + (4 * HB - 1))
                            f_v.wait(act, u, "a")
                            f_a.done(act.activation(act_hi[:, f, half(h)], af[:, h], ACT.Copy), "hi")
                        if f == 0:
                            high(Place(nf + RING, 0, i, 2), i0 + 2 * HB)
                            high(Place(nf + RING, 1, i, 2), i0 + 2 * HB)
                    if not last:
                        high(Place(nf + RING, 3, i, 2), i0 + 4 * HB)
                        high(Place(nf + RING, 4, i, 2), i0 + (4 * HB + OUTS))
                        high(Place(nf + RING, 5, i, 2), i0 + (4 * HB + OUTS))

                with act.Fori(0, FI - b) as i:
                    ffn(i, False)
                if b:
                    ffn(FI - 1, True)

                f_o.wait(act, (b + 1) * FI - 1, f"o{OUTS - 1}")
                for k in range(KD):
                    if k >= 2:
                        e_v.wait(act, b, f"ss{k - 2}")
                    e_a.done(act.activation(e_sq[:, k % 2], xacc[:, k], ACT.Square), f"sq{k}")
                e_p.wait(act, b, "ss")
                e_a.done(act.activation(e_rs[:], side[:, 0:HB], ACT.Ln, scale=1.0 / D, bias=eps[:]), "ln")
                e_a.wait(act, b, "ln")
                e_a.done(act.activation(e_rs[:], e_rs[:], ACT.Exp, scale=-0.5), "rstd")
                for k in range(KD):
                    e_v.wait(act, b, f"t{k}")
                    e_a.done(act.activation(xacc[:, k], xacc[:, k], ACT.Identity, bias=mod(6, k)), f"b{k}")
                for t in range(TB // P):
                    e_p.wait(act, b, f"t{t}")
                    if t >= 2:
                        act.wait_ge(out_stored[t % 2], 16 * (b * TB // P // 2 + t // 2))
                    e_c.done(act.activation(e_out[:, t % 2], side[:, 2 * (t % 2):2 * (t % 2) + 2], ACT.Copy), f"t{t}")

        @block.vector
        def _(dve):
            dve.sem_inc(w_low, RING)
            for line in (mod_v, prep_v, cv_v, gla_v, res_v, f_v, f_o):
                line.begin(dve)

            def low(place):
                dve.wait_ge(w_high, place.number + 1)
                dve.tensor_tensor(w_lo[:, place.slot], w_raw[:, place.slot], w_hi[:, place.slot].bitcast(F32),
                                  ALU.subtract).then_inc(w_low, 1)

            setup_v.done(dve.memset(ones[:], 1.0), "ones")
            setup_v.done(dve.memset(eps[:], EPS), "eps")
            setup_p.wait(dve, 0, "rows")
            setup_v.done(dve.tensor_copy(pvec[:, 0:ncol], side[:, 0, 0:ncol]), "pvec")
            setup_p.wait(dve, 0, "taps")
            setup_v.done(dve.tensor_copy(taps[:], side[:, 1, 0:TAPS * CT]), "taps")
            setup_v.done(dve.tensor_copy(g_mask[:], mask_f[:]), "mask")

            def mod_block(m, loop):
                for k in range(KD):
                    dve.wait_ge(m_loaded[k % 4], loop * 32 + 16 * (k // 4 + 1))
                    if k == 0:
                        ins = dve.tensor_scalar(m_acc[:], m_raw[:, 0], cact[:, 0:1], None, ALU.mult)
                    else:
                        mod_v.wait(dve, m, f"k{k - 1}")
                        ins = dve.scalar_tensor_tensor(m_acc[:], m_raw[:, k % 4], cact[:, k:k + 1], m_acc[:],
                                                       ALU.mult, ALU.add)
                    mod_v.done(ins, f"k{k}")
                mod_p.wait(dve, m, "sum")
                mod_v.done(dve.tensor_tensor(modv[:, bass.ds(m * KD, KD)], side[:, 4, 0:KD],
                                             pvec[:, bass.ds(m * KD, KD)], ALU.add), "vec")

            setup_a.wait(dve, 0, "cact")
            for m in range(2):
                mod_block(m, m)
            mod_v.wait(dve, 1, "vec")
            gains_v.done(dve.scalar_tensor_tensor(gain1[:], modv[:, KD:2 * KD], 1.0,
                                                  pvec[:, col["g_mix"]:col["g_mix"] + KD], ALU.add, ALU.mult), "g1")
            for s in range(RING):
                low(Place(0, s, 0, 1))
            gains_v.wait(dve, 0, "g1")

            with dve.Fori(0, G // 2) as i:
                for s in range(2):
                    g = i * 2 + s
                    prep_a.wait(dve, g, "rstd")
                    for t in range(4):
                        prep_v.done(dve.tensor_scalar(xnat[:, s, t], xnat[:, s, t], rstd4[:, s, t:t + 1], None,
                                                      ALU.mult), f"xn{t}")
                    for k in range(KD):
                        prep_p.wait(dve, g, f"k{k}")
                        prep_a.wait(dve, g if k >= 2 else g - 1, f"hi{(k - 2) % KD}")
                        prep_v.done(dve.tensor_scalar(p_tmp[:, k % 2], side[:, k % 4], gain1[:, k:k + 1], mod(0, k),
                                                      ALU.mult, ALU.add), f"t{k}")
                        prep_a.wait(dve, g, f"hi{k}")
                        prep_v.done(dve.tensor_tensor(h_lo[:, k, bass.ds(g * NT, NT)], p_tmp[:, k % 2],
                                                      h_hi[:, k, bass.ds(g * NT, NT)].bitcast(F32), ALU.subtract), f"lo{k}")

            dve.memset(al_hi[:].bitcast(F32), 0.0)
            setup_v.done(dve.memset(al_lo[:].bitcast(F32), 0.0), "pad")
            setup_v.wait(dve, 0, "pad")
            dve.wait_ge(al_loaded, 16)
            setup_v.done(dve.tensor_copy(al_hi[:, :, 0:RANK], al_raw[:]), "al_hi")
            setup_v.wait(dve, 0, "al_hi")
            setup_v.done(dve.tensor_tensor(al_lo[:, :, 0:RANK], al_raw[:], al_hi[:, :, 0:RANK].bitcast(F32),
                                           ALU.subtract), "al_lo")
            with dve.Fori(0, G) as g:
                z_a.wait(dve, g, "zb1")
                z_v.done(dve.tensor_scalar(zm[:], zt[:], 0.0, 1.0 / GATE_TAU, ALU.min, ALU.mult), "min")
                z_a.wait(dve, g, "ln")
                z_v.wait(dve, g, "min")
                z_v.done(dve.scalar_tensor_tensor(zm[:], zt[:], -1.0 / GATE_TAU, zm[:], ALU.mult, ALU.add), "la")

            def in_proj(i, s):
                low(Place(RING, s, i, 1))
                if s == 0 and not isinstance(i, int):
                    mod_block(i + 2, i + 2)

            tiles(dve, NA, in_proj)
            mod_v.wait(dve, 7, "vec")
            gains_v.done(dve.scalar_tensor_tensor(gain2[:], modv[:, 4 * KD:5 * KD], 1.0,
                                                  pvec[:, col["g_ffn"]:col["g_ffn"] + KD], ALU.add, ALU.mult), "g2")
            gains_v.done(dve.scalar_tensor_tensor(gainf[:], modv[:, 7 * KD:8 * KD], 1.0,
                                                  pvec[:, col["g_fin"]:col["g_fin"] + KD], ALU.add, ALU.mult), "gf")

            dve.wait_ge(product, NA * G)
            dve.memset(ub[:, 0:PAD], 0.0)
            with dve.Fori(0, CT) as j:
                def tap(k):
                    return taps[:, bass.ds(j + k * CT, 1)]

                dve.wait_ge(cv_loaded, j * 32 + 32)
                cv_a.wait(dve, j, "sig")
                cv_v.wait(dve, j - 1, "sum")
                cv_v.done(dve.tensor_tensor(ub[:, PAD:PAD + T], cvb[:], cgb[:], ALU.mult), "u")
                dve.wait_ge(cv_stored, j * 16 + 16)
                for k in range(TAPS):
                    a = (acc_a, acc_b)[k % 2]
                    cv_v.wait(dve, j, f"tap{k - 2}" if k >= 2 else "u")
                    if k == 0:
                        ins = dve.tensor_scalar(a[:], ub[:, 0:T], tap(0), pvec[:, bass.ds(j + col["conv_b"], 1)],
                                                ALU.mult, ALU.add)
                    elif k == 1:
                        ins = dve.tensor_scalar(a[:], ub[:, 1:1 + T], tap(1), None, ALU.mult)
                    else:
                        ins = dve.scalar_tensor_tensor(a[:], ub[:, k:k + T], tap(k), a[:], ALU.mult, ALU.add)
                    cv_v.done(ins, f"tap{k}")
                cv_v.wait(dve, j, f"tap{TAPS - 1}")
                cv_v.done(dve.tensor_tensor(acc_a[:], acc_a[:], acc_b[:], ALU.add), "sum")

            g_zero.done(dve.memset(g_st[:], 0.0), "st")
            g_zero.done(dve.memset(g_state[:], 0.0), "state")
            g_zero.done(dve.memset(g_qd[:], 0.0), "qd")
            g_zero.done(dve.memset(g_qb[:], 0.0), "qb")
            g_zero.done(dve.memset(g_ql[:], 0.0), "ql")
            g_zero.done(dve.memset(g_one[:], 1.0), "one")
            g_zero.wait(dve, 0, "one")

            with dve.Fori(0, CHUNKS) as n:
                k_all = g_qk[:, KT:2 * KT].rearrange("p a t -> p (a t)")
                cum_all = g_cum[:].rearrange("p a t -> p (a t)")
                dve.wait_ge(g_loaded, n * 48 + 48)
                for f in range(KT):
                    gla_v.done(dve.tensor_tensor_scan(g_cum[:, f], g_one[:], g_la[:, f], 0.0, ALU.mult, ALU.add), f"cum{f}")
                gla_v.wait(dve, n, "cum1")
                for l, s in enumerate(LEVELS):
                    c3 = pairs(cum_all, s)
                    gla_v.done(dve.tensor_tensor(pairs(g_lev[:, l], s), c3,
                                                 c3[:, :, s - 1:s].to_broadcast([P, KT * C // (2 * s), 2 * s]),
                                                 ALU.subtract), f"sub{l}")
                gla_a.wait(dve, n, "kdec1")
                for e in range(2):
                    r = slice(e * HEAD_K, (e + 1) * HEAD_K)
                    gla_v.done(dve.tensor_tensor(g_qd[r, :, e], g_ecum[r], g_qk[r, 0:KT], ALU.mult), f"qd{e}")
                gla_v.done(dve.tensor_tensor(g_kd[:], g_kd[:], g_qk[:, KT:2 * KT], ALU.mult), "kd")
                for l, s in enumerate(LEVELS):
                    e3 = pairs(g_lev[:, l], s)
                    for e in range(2):
                        r = slice(e * HEAD_K, (e + 1) * HEAD_K)
                        gla_v.done(dve.tensor_tensor(
                            g_ql[r, l, :, e].rearrange("p a (r w) -> p a r w", w=s),
                            g_lev[r, l].rearrange("p (a r w) -> p a r w", a=KT, w=2 * s)[:, :, :, s:2 * s],
                            g_qk[r, 0:KT].rearrange("p a (r w) -> p a r w", w=2 * s)[:, :, :, s:2 * s],
                            ALU.mult), f"q{'ab'[e]}{l}")
                    gla_v.done(dve.tensor_tensor(e3[:, :, 0:s], e3[:, :, 0:s], pairs(k_all, s)[:, :, 0:s],
                                                 ALU.mult), f"k{l}")
                gla_p.wait(dve, n, "lev")
                st_all = g_st[:].rearrange("p h t -> p (h t)")
                for l, s in enumerate(LEVELS):
                    w = HEADS * C // 2
                    if l:
                        gla_v.wait(dve, n, f"pick{l - 1}")
                    dve.sem_inc(picks, 1)
                    data = side[:, l // 2, (l % 2) * w:(l % 2 + 1) * w]
                    gla_v.done(dve.copy_predicated(pairs(st_all, s)[:, :, s:2 * s],
                                                   g_mask[:, l * w:(l + 1) * w].rearrange("p (r w) -> p r w", w=s),
                                                   data.rearrange("p (r w) -> p r w", w=s)), f"pick{l}")
                gla_p.wait(dve, n, "diag")
                gla_v.wait(dve, n, f"pick{L[-1]}")
                dve.sem_inc(picks, 1)
                gla_v.done(dve.copy_predicated(st_all, g_mask[:, len(LEVELS) * HEADS * C // 2:], side[:, 4]), "pickd")
                gla_p.wait(dve, n, "state")
                for f in range(KT):
                    gla_v.done(dve.scalar_tensor_tensor(g_state[:, f], g_state[:, f], g_ecum[:, f, C - 1:C],
                                                        side[:, 1, f * DV:(f + 1) * DV], ALU.mult, ALU.add), f"st{f}")
                gla_a.wait(dve, n, "rstd")
                dve.wait_ge(g_stored, n * 16 + 16)
                on_all = g_on[:].rearrange("p h t -> p (h t)")
                gla_v.done(dve.tensor_scalar(g_rs[:], g_rs[:], vec("gla_g"), HEAD_K ** -0.5, ALU.mult, ALU.mult), "gain")
                gla_v.wait(dve, n, "gain")
                gla_v.done(dve.tensor_tensor(on_all, side[:, 0], g_rs[:], ALU.mult), "on")

            for b in range(2):
                n0 = NC0 + b * NH
                dve.wait_ge(c_loaded, 48 * (b + 1))
                if b:
                    e_p.wait(dve, 0, f"t{TB // P - 1}")
                for j in range(1, CT):
                    if j >= 2:
                        ln_v.wait(dve, b, f"s{j - 1}")
                    ln_v.done(dve.tensor_tensor(ln_sum[:], cin[:, 0] if j == 1 else ln_sum[:], cin[:, j], ALU.add), f"s{j}")
                ln_p.wait(dve, b, "mean")
                for j in range(CT):
                    ln_v.done(dve.scalar_tensor_tensor(cin[:, j], side[:, 0:HB].rearrange("p h t -> p (h t)"), -1.0 / DC,
                                                       cin[:, j], ALU.mult, ALU.add), f"d{j}")
                for j in range(1, CT):
                    ln_a.wait(dve, b, f"q{j}")
                    if j >= 2:
                        ln_v.wait(dve, b, f"q{j - 1}")
                    ln_v.done(dve.tensor_tensor(ln_sum[:], ln_sq[:, 0] if j == 1 else ln_sum[:], ln_sq[:, j % 2],
                                                ALU.add), f"q{j}")
                ln_a.wait(dve, b, "rstd")
                for j in range(CT):
                    ln_v.done(dve.tensor_tensor(cin[:, j], cin[:, j], ln_rs[:], ALU.mult), f"n{j}")
                if b:
                    for s in range(2):
                        dve.wait_ge(out_stored[s], 16 * (TB // P) // 2)
                for j in range(CT):
                    ln_a.wait(dve, b, f"hi{j}")
                    ln_v.done(dve.tensor_tensor(y_lo[:, j], cin[:, j], y_hi[:, j].bitcast(F32), ALU.subtract), f"lo{j}")
                for j in range(VT):
                    ln_a.wait(dve, b, f"s{j}")
                    ln_v.done(dve.tensor_tensor(oin[:, j], oin[:, j], ogin[:, j], ALU.mult), f"m{j}")
                for j in range(VT):
                    ln_a.wait(dve, b, f"ohi{j}")
                    ln_v.done(dve.tensor_tensor(y_lo[:, CT + j], oin[:, j], y_hi[:, CT + j].bitcast(F32),
                                                ALU.subtract), f"olo{j}")
                zero_v.done(dve.memset(ssq[:], 0.0), "c")
                xt_a.wait(dve, b, turns[-1])

                def residual(i, s):
                    for h in range(HB):
                        p = Place(GC0 + b * GH, s * HB + h, i, HB)
                        u = i * (RING * HB) + (b * KD * HB + s * HB + h)
                        dve.wait_ge(product, p.number + 1)
                        xa = xacc[:, bass.ds(i * RING + s, 1), half(h)].rearrange("p a t -> p (a t)")
                        res_v.done(dve.scalar_tensor_tensor(xa, banks[p.slot][:], modv[:, bass.ds(i * RING + (2 * KD + s), 1)],
                                                            xa, ALU.mult, ALU.add), "x")
                        res_a.wait(dve, u, "sq")
                        res_v.done(dve.tensor_tensor(ssq[:, half(h)], ssq[:, half(h)], c_sq[:, h], ALU.add), "ss")
                    low(Place(n0 + RING, s, i, 1))

                zero_v.wait(dve, b, "c")
                tiles(dve, KD, residual)

                n_a.wait(dve, b, "rstd")
                for k in range(KD):
                    if k >= 2:
                        n_a.wait(dve, b, f"hi{k - 2}")
                    n_v.done(dve.scalar_tensor_tensor(n_t[:, k % 2], xacc[:, k], gain2[:, k:k + 1], n_rs[:],
                                                      ALU.mult, ALU.mult), f"t{k}")
                    n_a.wait(dve, b, f"hi{k}")
                    n_v.done(dve.scalar_tensor_tensor(h2_lo[:, k], n_t[:, k % 2], mod(3, k), h2_hi[:, k].bitcast(F32),
                                                      ALU.add, ALU.subtract), f"lo{k}")

                nf, gf = n0 + KD, GC0 + b * GH + KD * HB

                def ffn(i, last):
                    for f in range(2):
                        for h in range(HB):
                            u = i * PAIRS + (b * FI * PAIRS + f * HB + h)
                            pu = Place(gf, 2 * (f * HB + h) + 1, i, (4 * HB + OUTS) // RING)
                            f_a.wait(dve, u, "silu")
                            f_a.wait(dve, u - 2, "hi")
                            if (f, h) == (1, HB - 1):
                                low(Place(nf + RING, 2, i, 2))
                            dve.wait_ge(product, pu.number + 1)
                            f_v.done(dve.tensor_tensor(af[:, h], banks[pu.slot][:], sil[:, h], ALU.mult), "a")
                            f_a.wait(dve, u, "hi")
                            f_v.done(dve.tensor_tensor(act_lo[:, f, half(h)], af[:, h],
                                                       act_hi[:, f, half(h)].bitcast(F32), ALU.subtract), "lo")
                        if f == 0:
                            low(Place(nf + RING, 0, i, 2))
                            low(Place(nf + RING, 1, i, 2))
                    if not last:
                        low(Place(nf + RING, 3, i, 2))
                    for q in range(OUTS):
                        po = Place(gf, 4 * HB + q, i, (4 * HB + OUTS) // RING)
                        k, h = q % KD, q // KD
                        dve.wait_ge(product, po.number + 1)
                        f_o.done(dve.scalar_tensor_tensor(xacc[:, k, half(h)], banks[po.slot][:], mod(5, k),
                                                          xacc[:, k, half(h)], ALU.mult, ALU.add), f"o{q}")
                    if not last:
                        low(Place(nf + RING, 4, i, 2))
                        low(Place(nf + RING, 5, i, 2))

                with dve.Fori(0, FI - b) as i:
                    ffn(i, False)
                if b:
                    ffn(FI - 1, True)

                zero_v.done(dve.memset(ssq[:], 0.0), "e")
                zero_v.wait(dve, b, "e")
                for k in range(KD):
                    e_a.wait(dve, b, f"sq{k}")
                    if k:
                        e_v.wait(dve, b, f"ss{k - 1}")
                    e_v.done(dve.tensor_tensor(ssq[:], ssq[:], e_sq[:, k % 2], ALU.add), f"ss{k}")
                e_a.wait(dve, b, "rstd")
                for k in range(KD):
                    e_v.done(dve.scalar_tensor_tensor(xacc[:, k], xacc[:, k], gainf[:, k:k + 1], e_rs[:],
                                                      ALU.mult, ALU.mult), f"t{k}")

        @block.tensor
        def _(pe):
            gla_p.begin(pe)

            def parts(out_ap, terms):
                for n, (w1, w2, r1, r2) in enumerate(terms):
                    pe.matmul(out_ap, w1, r1, start=(n == 0), stop=False)
                    pe.matmul(out_ap, w1, r2, start=False, stop=False)
                    mm = pe.matmul(out_ap, w2, r1, start=False, stop=(n == len(terms) - 1))
                return mm

            def low_made(place):
                pe.wait_ge(w_low, place.number + (RING + 1))

            pe.wait_ge(const_in, 16 * (1 + len(names) + TAPS + 2))
            setup_p.done(pe.transpose(side[:, 0, 0:ncol], rows[0:ncol, 0, :], ident[0:ncol, 0:ncol]), "rows")
            setup_p.done(pe.transpose(side[:, 1, 0:TAPS * CT], rows[0:TAPS * CT, 1, :],
                                      ident[0:TAPS * CT, 0:TAPS * CT]), "taps")

            def mod_block(m):
                mod_v.wait(pe, m, f"k{KD - 1}")
                mod_v.wait(pe, m - 1, "vec")
                for j in range(KD):
                    mm = pe.matmul(side[:, 4, j:j + 1], m_acc[:, j * P:(j + 1) * P], ones[:, 0:1], start=True, stop=True)
                mod_p.done(mm, "sum")

            setup_v.wait(pe, 0, "ones")
            for m in range(2):
                mod_block(m)

            setup_v.wait(pe, 0, "taps")
            with pe.Fori(0, G // 2) as i:
                for s in range(2):
                    g = i * 2 + s
                    prep_v.wait(pe, g, "xn3")
                    for k in range(KD):
                        prep_v.wait(pe, g if k >= 4 else g - 1, f"t{(k - 4) % KD}")
                        for t in range(4):
                            mm = pe.transpose(side[:, k % 4, t * P:(t + 1) * P], xnat[:, s, t, k * P:(k + 1) * P], ident[:])
                        prep_p.done(mm, f"k{k}")

            setup_v.wait(pe, 0, "al_lo")
            prep_v.wait(pe, G - 1, f"lo{KD - 1}")
            with pe.Fori(0, G) as g:
                z_a.wait(pe, g - 1, "alow")
                mm = parts(side[:, 0], [(al_hi[:, k], al_lo[:, k], h_hi[:, k, bass.ds(g * NT, NT)],
                                         h_lo[:, k, bass.ds(g * NT, NT)]) for k in range(KD)])
                z_p.done(mm, "alow")
                z_a.wait(pe, g, "alow")
                for f in range(KT):
                    z_a.wait(pe, g - 1, f"zb{f}")
                    z_p.done(pe.matmul(side[:, 1 + f], a2[0:RANK, f * P:(f + 1) * P], alow[0:RANK, :],
                                       start=True, stop=True), f"z{f}")

            def in_proj(i, s):
                low_made(Place(0, s, i, 1))
                if s == 1 and not isinstance(i, int):
                    mod_block(i + 2)
                w = Place(0, s, i, 1).slot
                for h in range(G):
                    p = Place(0, s * G + h, i, G)
                    staged.wait(pe, p.number - RING, "copy")
                    parts(banks[p.slot][:], [(w_hi[:, w, k], w_lo[:, w, k], h_hi[:, k, half(h)], h_lo[:, k, half(h)])
                                             for k in range(KD)]).then_inc(product, 1)

            tiles(pe, NA, in_proj)

            g_zero.wait(pe, 0, "one")
            z_a.wait(pe, G - 1, "zb1")
            with pe.Fori(0, CHUNKS) as n:
                w = HEADS * C // 2
                pe.wait_ge(g_loaded, n * 48 + 48)
                gla_v.wait(pe, n - 1, "on")
                for h in range(HEADS):
                    mm = pe.transpose(side[:, 0, h * C:(h + 1) * C], g_vt[:, h], ident[:])
                gla_p.done(mm, "vn")
                gla_v.wait(pe, n, "kd")
                for f in range(KT):
                    mm = pe.transpose(side[:, 1, f * P:(f + 1) * P], g_kd[:, f], ident[:])
                gla_p.done(mm, "kn")
                gla_v.wait(pe, n, f"k{L[-1]}")
                gla_a.wait(pe, n, "kn")
                for l in L:
                    for f in range(KT):
                        o = (l % 2) * w + f * C
                        mm = pe.matmul(side[:, l // 2, o:o + C], g_lev[:, l, f * C:(f + 1) * C],
                                       g_ql[:, l, f].rearrange("p e t -> p (e t)"), start=True, stop=True)
                gla_p.done(mm, "lev")
                for f in range(KT):
                    mm = pe.matmul(side[:, 4, f * 2 * C:(f + 1) * 2 * C], g_qk[:, KT + f],
                                   g_qb[:, f].rearrange("p e t -> p (e t)"), start=True, stop=True)
                gla_p.done(mm, "diag")
                gla_v.wait(pe, n, "pickd")
                gla_v.wait(pe, n - 1, "st1")
                for f in range(KT):
                    pe.matmul(side[:, 0, f * 2 * C:(f + 1) * 2 * C], g_state[:, f],
                              g_qd[:, f].rearrange("p e t -> p (e t)"), start=True, stop=True, skip_group_check=True)
                    for h in range(2 * f, 2 * f + 2):
                        mm = pe.matmul(side[:, 0, h * C:(h + 1) * C], g_vn[:, h * DV:(h + 1) * DV], g_st[:, h],
                                       start=False, stop=True, skip_group_check=True)
                gla_p.done(mm, "o")
                for h in range(HEADS):
                    f, r = h // 2, slice((h % 2) * HEAD_K, (h % 2 + 1) * HEAD_K)
                    mm = pe.matmul(side[r, 1, f * DV:(f + 1) * DV], g_kn[:, h * HEAD_K:(h + 1) * HEAD_K],
                                   g_vn[:, h * DV:(h + 1) * DV], start=True, stop=True)
                gla_p.done(mm, "state")
                gla_a.wait(pe, n, "sq")
                gla_p.done(pe.matmul(side[:, 2], ones[:], g_sq[:], start=True, stop=True), "ss")

            for b in range(2):
                n0, g0 = NC0 + b * NH, GC0 + b * GH
                if b == 0:
                    gla_v.wait(pe, CHUNKS - 1, "on")
                else:
                    e_c.wait(pe, 0, f"t{TB // P - 1}")
                ln_v.wait(pe, b, f"s{CT - 1}")
                for h in range(HB):
                    mm = pe.matmul(side[:, h], ones[:], ln_sum[:, half(h)], start=True, stop=True)
                ln_p.done(mm, "mean")
                ln_v.wait(pe, b, f"q{CT - 1}")
                for h in range(HB):
                    mm = pe.matmul(side[:, 2 + h], ones[:], ln_sum[:, half(h)], start=True, stop=True)
                ln_p.done(mm, "var")
                ln_v.wait(pe, b, "n0")
                for g in range(HB):
                    pe.wait_ge(x2_loaded, 16 * (b * HB + g + 1))
                    for k in range(KD):
                        if g or k >= 4:
                            xt_a.wait(pe, b, f"g{g if k >= 4 else g - 1}k{(k - 4) % KD}")
                        for t in range(4):
                            mm = pe.transpose(side[:, k % 4, t * P:(t + 1) * P], xin[:, t, k * P:(k + 1) * P], ident[:])
                        xt_p.done(mm, f"g{g}k{k}")
                ln_v.wait(pe, b, f"olo{VT - 1}")
                if b == 0:
                    staged.wait(pe, NA * G - 1, "copy")
                else:
                    f_o.wait(pe, FI - 1, f"o{OUTS - 1}")

                def out_proj(i, s):
                    p = Place(n0, s, i, 1)
                    low_made(p)
                    for h in range(HB):
                        pb = Place(g0, s * HB + h, i, HB)
                        u = i * (RING * HB) + (b * KD * HB + s * HB + h)
                        res_v.wait(pe, u - RING, "x")
                        parts(banks[pb.slot][:], [(w_hi[:, p.slot, k], w_lo[:, p.slot, k], y_hi[:, k, half(h)],
                                                   y_lo[:, k, half(h)]) for k in range(KD)]).then_inc(product, 1)

                tiles(pe, KD, out_proj)
                xt_a.wait(pe, b, turns[-1])
                res_v.wait(pe, (b + 1) * KD * HB - 1, "ss")
                for h in range(HB):
                    mm = pe.matmul(side[:, h], ones[:], ssq[:, half(h)], start=True, stop=True)
                n_p.done(mm, "ss")
                n_v.wait(pe, b, f"lo{KD - 1}")

                nf, gf = n0 + KD, g0 + KD * HB
                per = (4 * HB + OUTS) // RING
                with pe.Fori(0, FI) as i:
                    it = i + b * FI
                    for f in range(2):
                        for h in range(HB):
                            x_ = f * HB + h
                            u = i * PAIRS + (b * FI * PAIRS + x_)
                            for up in range(2):
                                w = Place(nf, 2 * f + up, i, 2)
                                pg = Place(gf, 2 * x_ + up, i, per)
                                if h == 0:
                                    low_made(w)
                                if 2 * x_ + up < RING:
                                    f_o.wait(pe, it - 1, f"o{OUTS - RING + 2 * x_ + up}")
                                elif up:
                                    f_a.wait(pe, u - 1, "silu")
                                else:
                                    f_v.wait(pe, u - 2, "a")
                                parts(banks[pg.slot][:], [(w_hi[:, w.slot, k], w_lo[:, w.slot, k], h2_hi[:, k, half(h)],
                                                           h2_lo[:, k, half(h)]) for k in range(KD)]).then_inc(product, 1)
                    last = i * PAIRS + (b * FI * PAIRS + PAIRS - 1)
                    wd = [Place(nf, 4 + f, i, 2) for f in range(2)]
                    low_made(wd[1])
                    for q in range(OUTS):
                        k, h = q % KD, q // KD
                        po = Place(gf, 4 * HB + q, i, per)
                        if q == 0:
                            f_v.wait(pe, last - 1, "lo")
                        elif q == 1:
                            f_a.wait(pe, last, "silu")
                        elif q == 2:
                            f_v.wait(pe, last, "a")
                        else:
                            f_o.wait(pe, it, f"o{q - RING}")
                        if q == KD:
                            f_v.wait(pe, last, "lo")
                        parts(banks[po.slot][:], [(w_hi[:, wd[f].slot, k], w_lo[:, wd[f].slot, k], act_hi[:, f, half(h)],
                                                   act_lo[:, f, half(h)]) for f in range(2)]).then_inc(product, 1)

                e_v.wait(pe, b, f"ss{KD - 1}")
                for h in range(HB):
                    mm = pe.matmul(side[:, h], ones[:], ssq[:, half(h)], start=True, stop=True)
                e_p.done(mm, "ss")
                e_a.wait(pe, b, f"b{KD - 1}")
                for t in range(TB // P):
                    if t >= 2:
                        e_c.wait(pe, b, f"t{t - 2}")
                    for k in range(KD):
                        mm = pe.transpose(side[:, 2 * (t % 2) + k // 4, (k % 4) * P:(k % 4 + 1) * P],
                                          xacc[:, k, t * P:(t + 1) * P], ident[:])
                    e_p.done(mm, f"t{t}")


def masks():
    j = np.arange(C)[:, None]
    rows = []
    for s in LEVELS:
        i = np.arange(C).reshape(-1, 2 * s)[:, s:].reshape(1, -1)
        keep = (i // (2 * s) == j // (2 * s)) & (j % (2 * s) < s)
        rows.append(np.tile(keep, (1, 4)))
    rows.append(np.tile(np.eye(C, dtype=bool), (1, 4)))
    return np.concatenate(rows, axis=1).astype(np.float32)


_INS = ["x", "c", "w_ada", "b_ada", "g_mix", "w_in", "conv_w", "conv_b", "ln_g", "ln_b", "w_a2", "b_a2",
        "gla_norm_g", "w_out", "g_ffn", "w_ffn_in", "w_ffn_out", "w_ada_final", "b_ada_final", "g_final"]


def kernel(**inputs):
    import concourse.bacc as bacc
    from concourse.bass_utils import run_bass_kernel_spmd

    nc = bacc.Bacc("TRN2", target_bir_lowering=False, num_devices=1)
    arrays, args = {}, {}
    data = {name: np.ascontiguousarray(inputs[name]) for name in _INS}
    data["identity"] = np.eye(P, dtype=np.float32)
    data["level_masks"] = masks()
    for name, a in data.items():
        arrays[f"in_{name}"] = a
        args[name] = nc.dram_tensor(f"in_{name}", a.shape, mybir.dt.from_np(a.dtype), kind="ExternalInput").ap()
    shape = data["x"].shape
    o = nc.dram_tensor("out_0", shape, F32, kind="ExternalOutput").ap()
    block_kernel(nc, **args, out=o)
    r = run_bass_kernel_spmd(nc, [arrays], core_ids=[0])
    return np.asarray(r.results[0]["out_0"])
```

```python
from contextlib import ExitStack

import numpy as np

import concourse.bass as bass
from concourse import mybir

ALU = mybir.AluOpType
ACT = mybir.ActivationFunctionType
F32 = mybir.dt.float32
F32R = mybir.dt.float32r
U8 = mybir.dt.uint8

P = 128
EPS = 1e-6
RING = 3
NT = 512
GATE_TAU = 16.0
C = 128
LEVELS = [64, 32, 16, 8, 4, 2, 1]


class Line:

    def __init__(self, sem, names, ahead=0):
        self.sem, self.names, self.next, self.ahead = sem, list(names), 0, ahead

    def begin(self, engine):
        engine.sem_inc(self.sem, self.ahead * len(self.names))

    def value(self, unit, name):
        return unit * len(self.names) + (self.ahead * len(self.names) + self.names.index(name) + 1)

    def done(self, instruction, name):
        assert self.names[self.next] == name, (self.names[self.next], name)
        self.next = (self.next + 1) % len(self.names)
        instruction.then_inc(self.sem, 1)

    def wait(self, engine, unit, name):
        engine.wait_ge(self.sem, self.value(unit, name))


class Place:

    def __init__(self, base, step, loop, per_loop):
        self.slot = (base + step) % RING
        self.uses = loop * per_loop + (base + step) // RING
        self.number = loop * (RING * per_loop) + (base + step)


def tiles(engine, count, body):
    with engine.Fori(0, count // RING) as i:
        for s in range(RING):
            body(i, s)
    for s in range(count % RING):
        body(count // RING, s)


def block_kernel(nc, x, c, w_ada, b_ada, g_mix, w_in, conv_w, conv_b, ln_g, ln_b, w_a2, b_a2,
                 gla_norm_g, w_out, g_ffn, w_ffn_in, w_ffn_out, w_ada_final, b_ada_final, g_final,
                 identity, level_masks, out):
    T, D = x.shape[1], x.shape[2]
    KD = D // P
    TB = T // 2
    HB = TB // NT
    assert HB == 2
    G = T // NT
    TAPS, DC = conv_w.shape[1], conv_w.shape[2]
    CT = DC // P
    RANK, DK = w_a2.shape[1], w_a2.shape[2]
    KT = DK // P
    DV = gla_norm_g.shape[1]
    HV = D - DC
    VT = HV // P
    HEADS = HV // DV
    HEAD_K = DK // HEADS
    DF = w_ffn_out.shape[1]
    FT = DF // P
    CHUNKS = T // C
    PAD = TAPS - 1
    CV, CG, Q = 0, CT, 2 * CT
    K, V = Q + KT, Q + 2 * KT
    OG = V + VT
    AL = OG + VT
    NA = AL + 1
    assert NA % RING == 0
    assert DV == P and HEAD_K * 2 == P and KD == 8 and VT == HEADS and FT % 2 == 0 and TB % NT == 0

    x2 = x.rearrange("a t d -> (a t) d")
    out2 = out.rearrange("a t d -> (a t) d")
    wada = w_ada.rearrange("a k m -> (a k) m")
    win = w_in.rearrange("a (k p) m -> p (a k) m", p=P)
    wout = w_out.rearrange("a (k p) m -> p (a k) m", p=P)
    wfi = w_ffn_in.rearrange("a (k p) m -> p (a k) m", p=P)
    wfo = w_ffn_out.rearrange("a f m -> (a f) m")

    with ExitStack() as ctx:
        def sem(name):
            return ctx.enter_context(nc.semaphore(name))

        base = (nc.sbuf_base + 63) // 64 * 64
        room = nc.sbuf_usable_end - base - 64
        ctx.enter_context(nc.sbuf_tensor("arena", [P, room // 4], F32))

        def at(name, offset, shape, dtype=F32):
            return nc.alloc_sbuf_tensor_at(name, [P, *shape], dtype, offset=base + offset)

        KB = 1024
        ident = at("ident", 0, [P])
        ones = at("ones", 512, [P])
        pvec = at("pvec", 1024, [112])
        taps = at("taps", 1472, [TAPS * CT])
        modv = at("modv", 1984, [64])
        gain1 = at("gain1", 2240, [KD])
        gain2 = at("gain2", 2272, [KD])
        gainf = at("gainf", 2304, [KD])
        eps = at("eps", 2336, [1])
        cact = at("cact", 2368, [KD])
        ssq4 = at("ssq4", 2432, [4])
        rstd4 = at("rstd4", 2464, [4])
        a2 = at("a2", 2560, [DK])
        WO = 2560 + 4 * DK
        w_raw = at("w_raw", WO, [RING, KD, P])
        w_hi = at("w_hi", WO + 12 * KB, [RING, KD, P], F32R)
        w_lo = at("w_lo", WO + 24 * KB, [RING, KD, P], F32R)
        HA = WO + 36 * KB
        HB_ = HA + 64 * KB
        RO = HA + 128 * KB
        MASKS = (len(LEVELS) + 2) * HEADS * C // 2
        g_mask = at("g_mask", RO + 36 * KB + 512, [MASKS], U8)
        mask_f = at("mask_f", HA, [MASKS])
        rows = at("rows", HA + 16 * KB, [2, P])
        assert RO + 36 * KB + 512 + MASKS <= room, (RO, room)
        m_raw = at("m_raw", RO, [4, KD * P])
        m_acc = at("m_acc", RO + 16 * KB, [KD * P])
        p_tmp = at("p_tmp", RO + 16 * KB, [2, NT])
        p_junk = at("p_junk", RO + 34 * KB + 512, [D], mybir.dt.bfloat16)
        xnat = [at("xnat0", HB_, [4, D]), at("xnat1", HB_ + 16 * KB, [4, D]), at("xnat2", RO, [4, D])]
        xnat.append(xnat[2])
        h_hi = [at("h0_hi", HA, [KD, TB], F32R), at("h1_hi", HB_, [KD, TB], F32R)]
        h_lo = [at("h0_lo", HA + 32 * KB, [KD, TB], F32R), at("h1_lo", HB_ + 32 * KB, [KD, TB], F32R)]
        stage = at("stage", RO + 20 * KB, [RING, NT])
        PW = PAD + NT + 2

        def conv_buffers(tag, o_in, o_acc):
            return (at("cv" + tag, o_in, [PW]), at("cg" + tag, o_in + 4 * PW, [PW]),
                    at("acca" + tag, o_acc, [NT]), at("accb" + tag, o_acc + 4 * NT, [NT]))

        conv_a = conv_buffers("_a", RO + 26 * KB, RO + 26 * KB + 8 * PW)
        conv_d = conv_buffers("_d", RO + 32 * KB, HA + 60 * KB)
        assert 2 * 4 * PW <= 4 * KB + 512
        offset = [HA]

        def gla(name, shape):
            t = at(name, offset[0], shape)
            offset[0] += 4 * int(np.prod(shape))
            return t

        g_lev = gla("g_lev", [len(LEVELS), KT * C])
        g_ql = gla("g_ql", [len(LEVELS), KT, 2, C // 2])
        g_qb = gla("g_qb", [KT, 2, C])
        g_qd = gla("g_qd", [KT, 2, C])
        g_qk = gla("g_qk", [2 * KT, C])
        g_vt = gla("g_vt", [VT, C])
        g_st = gla("g_st", [HEADS, C])
        g_vn = gla("g_vn", [VT * P])
        g_rs = gla("g_rs", [HEADS * C])
        g_kn = gla("g_kn", [KT * P])
        g_state = gla("g_state", [KT, DV])
        g_la = gla("g_la", [KT, C])
        g_cum = gla("g_cum", [KT, C])
        g_ecum = gla("g_ecum", [KT, C])
        g_kd = gla("g_kd", [KT, C])
        g_al = gla("g_al", [C])
        g_one = gla("g_one", [C])
        assert offset[0] <= HA + 36 * KB, offset
        y_hi = at("y_hi", HB_, [KD, TB], F32R)
        y_lo = at("y_lo", HB_ + 32 * KB, [KD, TB], F32R)
        h2_hi = at("h2_hi", HB_, [KD, TB], F32R)
        h2_lo = at("h2_lo", HB_ + 32 * KB, [KD, TB], F32R)
        xacc = at("xacc", RO, [KD, TB])
        ssq = at("ssq", HA, [TB])
        cin = at("cin", HA + 36 * KB, [CT, TB])
        xin = at("xin", HA + 52 * KB, [3, D])
        ln_sq, ln_rs, oin, ogin = ([at(f"{name}{b}", o + k * KB, shape) for b, o in enumerate((RO, HA))]
                                   for name, k, shape in (("ln_sq", 0, [CT, NT]), ("ln_rs", 8, [TB]),
                                                          ("oin", 12, [2, TB]), ("ogin", 20, [2, TB])))
        c_sq = at("c_sq", HA + 36 * KB, [2, NT])
        n_t = at("n_t", HA + 40 * KB, [2, TB])
        n_rs = at("n_rs", HA + 48 * KB, [TB])
        act_hi = at("act_hi", HA + 36 * KB, [2, TB], F32R)
        act_lo = at("act_lo", HA + 44 * KB, [2, TB], F32R)
        sil = at("sil", HA + 52 * KB, [2, NT])
        af = at("af", HA + 56 * KB, [2, NT])
        e_sq = at("e_sq", HB_ + 48 * KB, [2, NT])
        e_rs = at("e_rs", HB_ + 52 * KB, [TB])
        e_out = at("e_out", HB_ + 56 * KB, [2, D])

        banks = [ctx.enter_context(nc.psum_tensor(f"bank{b}", [P, NT], F32)) for b in range(RING)]
        side = ctx.enter_context(nc.psum_tensor("side", [P, 8 - RING, NT], F32))

        proj = nc.dram_tensor("proj", [NA, P, T], F32, kind="Internal").ap()
        convd = nc.dram_tensor("convd", [CT, P, T], F32, kind="Internal").ap()
        od = nc.dram_tensor("od", [VT, P, T], F32, kind="Internal").ap()

        names = [("b_ada", b_ada.rearrange("a (r p) -> (a r) p", p=P)),
                 ("b_fin", b_ada_final.rearrange("(r p) -> r p", p=P)),
                 ("g_mix", g_mix.rearrange("a (r p) -> (a r) p", p=P)),
                 ("g_ffn", g_ffn.rearrange("a (r p) -> (a r) p", p=P)),
                 ("g_fin", g_final.rearrange("(r p) -> r p", p=P)),
                 ("c", c.rearrange("a (r p) -> (a r) p", p=P)),
                 ("conv_b", conv_b.rearrange("a (r p) -> (a r) p", p=P)),
                 ("ln_g", ln_g.rearrange("a (r p) -> (a r) p", p=P)),
                 ("ln_b", ln_b.rearrange("a (r p) -> (a r) p", p=P)),
                 ("b_a2", b_a2.rearrange("a (r p) -> (a r) p", p=P)),
                 ("gla_g", gla_norm_g)]
        col, ncol = {}, 0
        for name, rows_of in names:
            col[name] = ncol
            ncol += rows_of.shape[0]
        assert ncol <= 112

        def vec(name, j=0):
            return pvec[:, col[name] + j:col[name] + j + 1]

        def mod(m, j):
            return modv[:, m * KD + j:m * KD + j + 1]

        def half(h):
            return slice(h * NT, (h + 1) * NT)

        def pairs(ap, s):
            return ap.rearrange("p (r w) -> p r w", w=2 * s)

        const_in = sem("const_in")
        setup_p = Line(sem("setup_p"), ["rows", "taps"])
        setup_v = Line(sem("setup_v"), ["ones", "eps", "pvec", "taps", "mask", "pad"])
        setup_a = Line(sem("setup_a"), ["cact"])
        w_loaded = [sem(f"w_loaded{s}") for s in range(RING)]
        w_high = sem("w_high")
        w_low = sem("w_low")
        product = sem("product")
        SHIFTED = ["t0"] + [f"{s}{k - d}" for k in range(1, KD) for s, d in (("t", 0), ("lo", 1))] + [f"lo{KD - 1}"]
        m_loaded = [sem(f"m_loaded{s}") for s in range(4)]
        m2_loaded = [sem(f"m2_loaded{s}") for s in range(4)]
        mod_v = Line(sem("mod_v"), [f"k{k}" for k in range(KD)] + ["vec"], ahead=1)
        mod_p = Line(sem("mod_p"), ["sum"])
        gains_v = Line(sem("gains_v"), ["g1", "g2", "gf"])
        x_loaded = [sem(f"x_loaded{g}") for g in range(G)]
        prep_a = Line(sem("prep_a"), [f"sq{t}" for t in range(4)] + ["ln", "rstd"] + [f"hi{k}" for k in range(KD)], ahead=1)
        prep_v = Line(sem("prep_v"), [f"xn{t}" for t in range(4)] + SHIFTED, ahead=1)
        prep_p = Line(sem("prep_p"), [f"k{k}" for k in range(KD)])
        staged = Line(sem("staged"), ["copy"], ahead=RING)
        stored = [sem(f"stored{b}") for b in range(RING)]
        cv_loaded = sem("cv_loaded")
        cv_a = Line(sem("cv_a"), ["sig"])
        cv_v = Line(sem("cv_v"), ["u"] + [f"tap{k}" for k in range(TAPS)] + ["sum"], ahead=1)
        cv_stored = sem("cv_stored")
        picks = sem("picks")
        pool_steps = sem("pool_steps")
        g_zero = Line(sem("g_zero"), ["st", "state", "qd", "qb", "ql", "one"])
        g_loaded = sem("g_loaded")
        g_stored = sem("g_stored")
        L = range(len(LEVELS))
        gla_v = Line(sem("gla_v"), ["min", "la", "cum0", "cum1"] + [f"sub{l}" for l in L] + ["qd0", "qd1", "kd"]
                     + [f"{s}{l}" for l in L for s in ("qa", "qb", "k")]
                     + [f"pick{l}" for l in L] + ["pickd", "st0", "st1", "gain", "on"], ahead=1)
        gla_a = Line(sem("gla_a"), ["zb0", "zb1", "zabs", "zexp", "zln", "qb0", "qb1", "abs", "ecum",
                                    "kdec0", "kdec1", "exp", "vn", "kn", "sq", "ln", "rstd"])
        gla_p = Line(sem("gla_p"), ["z", "vn", "kn", "lev", "diag", "o", "state", "ss"], ahead=1)
        c_loaded = sem("c_loaded")
        o_loaded = [sem(f"o_loaded{s}") for s in range(2)]
        x2_loaded = [sem(f"x2_loaded{s}") for s in range(3)]
        ln_p = Line(sem("ln_p"), [f"{s}{h}" for s in ("mean", "var") for h in range(HB)])
        ln_a = Line(sem("ln_a"), [f"q{h}{j}" for h in range(HB) for j in range(CT)]
                    + [f"{s}{h}" for h in range(HB) for s in ("ln", "rstd")]
                    + [f"{s}{h}{j}" for h in range(HB) for s in ("y", "hi") for j in range(CT)])
        ln_v = Line(sem("ln_v"), [f"d{h}{j}" for h in range(HB) for j in range(CT)]
                    + [f"{s}{h}{j}" for h in range(HB) for s in ("n", "lo") for j in range(CT)])
        og_a = Line(sem("og_a"), [f"{s}{j}" for j in range(VT) for s in ("s", "hi")])
        og_v = Line(sem("og_v"), [f"{s}{j}" for j in range(VT) for s in ("m", "lo")])
        TT = TB // P
        xt_p = Line(sem("xt_p"), [f"t{t}" for t in range(TT)])
        xt_a = Line(sem("xt_a"), [f"t{t}" for t in range(TT)])
        res_v = Line(sem("res_v"), ["x", "ss"], ahead=RING)
        res_a = Line(sem("res_a"), ["sq"])
        zero_v = Line(sem("zero_v"), ["ssq"])
        n_p = Line(sem("n_p"), ["ss"])
        n_a = Line(sem("n_a"), ["ln", "rstd"] + [f"hi{k}" for k in range(KD)])
        n_v = Line(sem("n_v"), SHIFTED)
        f_a = Line(sem("f_a"), ["silu", "hi"], ahead=2)
        f_v = Line(sem("f_v"), ["a", "lo"], ahead=2)
        OUTS = KD * HB
        f_o = Line(sem("f_o"), [f"o{q}" for q in range(OUTS)], ahead=1)
        e_a = Line(sem("e_a"), [f"sq{h}{k}" for h in range(HB) for k in range(KD)]
                   + [f"{s}{h}" for h in range(HB) for s in ("ln", "rstd")]
                   + [f"b{h}{k}" for h in range(HB) for k in range(KD)])
        e_v = Line(sem("e_v"), [f"t{h}{k}" for h in range(HB) for k in range(KD)])
        e_p = Line(sem("e_p"), [f"ss{h}{k}" for h in range(HB) for k in range(KD)] + [f"t{t}" for t in range(TT)])
        e_c = Line(sem("e_c"), [f"t{t}" for t in range(TT)])
        out_stored = [sem(f"out_stored{s}") for s in range(2)]

        NAG = NA * HB
        FI = FT // 2
        NC0, GC0 = 2 * NA, 2 * NAG
        NH, GH = KD + 6 * FI, KD * HB + (4 * HB + OUTS) * FI
        PAIRS = 2 * HB
        AI = NA // RING
        CH2 = CHUNKS // 2
        A_T0, A_T1 = 10, 8
        D_T0 = 8

        def a_group(it, s, h):
            if isinstance(it, int) and it == 0:
                return h * RING + s
            return s * HB + h

        def a_order(it):
            if isinstance(it, int) and it == 0:
                return [(s, h) for h in range(HB) for s in range(RING)]
            return [(s, h) for s in range(RING) for h in range(HB)]

        def gla_slots(it):
            return (3, 4, 5, 5) if isinstance(it, int) and it == 0 else (0, 2, 3, 5)

        def a_place(b, it, s, h):
            return Place(b * NAG, a_group(it, s, h), it, NAG // AI // RING)

        def a_tile(it, s):
            t = it * RING + (s - 1)
            if isinstance(it, int) and it * RING + s == 0:
                return AL, (AL - 1) * P + RANK
            return t, t * P

        block = ctx.enter_context(nc.Block())

        @block.sync
        def _(sp):
            def load(place, source):
                sp.wait_ge(w_low, place.number + 1)
                sp.dma_start(w_raw[:, place.slot], source).then_inc(w_loaded[place.slot], 16)

            def mod_rows(m, source):
                for k in range(KD):
                    if m or k >= 4:
                        mod_v.wait(sp, m if k >= 4 else m - 1, f"k{k - 4 if k >= 4 else k + 4}")
                    sp.dma_start(m_raw[:, k % 4], source[k * P:(k + 1) * P, :]).then_inc(m_loaded[k % 4], 16)

            def in_proj(b, it):
                for s in range(RING):
                    load(Place(b * NA, s, it, 1), win[:, :, bass.ds(a_tile(it, s)[1], P)])

            mod_rows(0, wada[:, 0:D])
            sp.dma_start(xnat[0][:], x2[0:NT, :].rearrange("(t p) d -> p t d", p=P)).then_inc(x_loaded[0], 16)
            in_proj(0, 0)
            mod_rows(1, wada[:, D:2 * D])
            sp.dma_start(xnat[1][:], x2[NT:2 * NT, :].rearrange("(t p) d -> p t d", p=P)).then_inc(x_loaded[1], 16)
            for b in range(2):
                if b:
                    in_proj(b, 0)
                with sp.Fori(0, AI - 1) as j:
                    in_proj(b, j + 1)
            for b in range(2):
                n0 = NC0 + b * NH
                tiles(sp, KD, lambda i, s: load(Place(n0, s, i, 1), wout[:, :, bass.ds((i * RING + s) * P, P)]))
                with sp.Fori(0, FI) as i:
                    for f in range(2):
                        for u in range(2):
                            load(Place(n0 + KD, 2 * f + u, i, 2),
                                 wfi[:, :, bass.ds(i * (2 * P) + (f * P + u * DF), P)])
                    for f in range(2):
                        load(Place(n0 + KD, 4 + f, i, 2),
                             wfo[bass.ds(i * (2 * P) + f * P, P), :].rearrange("p (k m) -> p k m", k=KD))

        @block.gpsimd
        def _(pool):
            pool.dma_start(ident[:], identity).then_inc(const_in, 16)
            for name, rows_of in names:
                n = rows_of.shape[0]
                pool.dma_start(rows[col[name]:col[name] + n, 0, :], rows_of).then_inc(const_in, 16)
            pool.dma_start(rows[0:TAPS * CT, 1, :], conv_w.rearrange("a t (j p) -> (a t j) p", p=P)).then_inc(const_in, 16)
            pool.dma_start(a2[0:RANK, :], w_a2.rearrange("a r d -> (a r) d")).then_inc(const_in, 16)
            pool.dma_start(mask_f[:], level_masks).then_inc(const_in, 16)

            def waited():
                pool.sem_inc(pool_steps, 1)

            def mod_rows(m, source):
                for k in range(KD):
                    mod_v.wait(pool, m if k >= 4 else m - 1, f"k{k - 4 if k >= 4 else k + 4}")
                    waited()
                    pool.dma_start(m_raw[:, k % 4], source[k * P:(k + 1) * P, :]).then_inc(m2_loaded[k % 4], 16)

            def conv_load(bufs, unit, j, h):
                cv_v.wait(pool, unit - 1, "sum")
                waited()
                halo = PAD if h else 0
                for buf, t0 in ((bufs[0], CV), (bufs[1], CG)):
                    pool.dma_start(buf[:, PAD - halo:PAD + NT],
                                   proj[bass.ds(j + t0, 1), :, h * NT - halo:(h + 1) * NT]
                                   .rearrange("a p t -> p (a t)")).then_inc(cv_loaded, 16)

            def conv_store(bufs, unit, j, h):
                cv_v.wait(pool, unit, "sum")
                waited()
                pool.dma_start(convd[bass.ds(j, 1), :, h * NT:(h + 1) * NT].rearrange("a p t -> p (a t)"),
                               bufs[2][:]).then_inc(cv_stored, 16)

            def gla_load(n):
                gla_p.wait(pool, n - 1, "diag")
                gla_v.wait(pool, n - 1, f"k{L[-1]}")
                waited()
                tok = bass.ds(n * C, C)
                pool.dma_start(g_al[0:RANK, :], proj[AL, P - RANK:P, tok]).then_inc(g_loaded, 16)
                pool.dma_start(g_qk[:], proj[Q:Q + 2 * KT, :, tok].rearrange("a p t -> p a t")).then_inc(g_loaded, 16)
                pool.dma_start(g_vt[:], proj[V:V + VT, :, tok].rearrange("a p t -> p a t")).then_inc(g_loaded, 16)

            def gla_store(n):
                gla_v.wait(pool, n, "on")
                waited()
                pool.dma_start(od[:, :, bass.ds(n * C, C)].rearrange("a p t -> p a t"),
                               g_rs[:].rearrange("p (h t) -> p h t", h=HEADS)).then_inc(g_stored, 16)

            for m in range(2, 4):
                mod_rows(m, wada[:, m * D:(m + 1) * D])
            for part, source in ((0, wada[:, 4 * D:6 * D]), (1, w_ada_final)):
                with pool.Fori(0, 2) as j:
                    unit = j + 2 * part
                    for s in range(RING):
                        pool.wait_ge(stored[s], j * (2 * 16) + (16 + (part * 2 + 2) * 2 * 16))
                    conv_load(conv_a, unit, unit, 0)
                    mod_rows(unit + 4, source[:, bass.ds(j * D, D)])
                    conv_store(conv_a, unit, unit, 0)
            mod_v.wait(pool, 7, f"k{KD - 1}")
            for g in range(2, 4):
                if g == 3:
                    prep_p.wait(pool, 2, f"k{KD - 1}")
                pool.dma_start(xnat[g][:], x2[g * NT:(g + 1) * NT, :].rearrange("(t p) d -> p t d", p=P)).then_inc(x_loaded[g], 16)

            for s in range(RING):
                pool.wait_ge(stored[s], 16 + NAG // RING * 16)
            pool.wait_ge(product, NAG)
            gla_load(0)
            gla_load(1)
            gla_store(0)
            with pool.Fori(0, CT) as j:
                conv_load(conv_a, j + CT, j, 1)
                gla_load(j + 2)
                conv_store(conv_a, j + CT, j, 1)
                gla_store(j + 1)
            with pool.Fori(0, AI - 1 - CT) as j:
                gla_load(j + (CT + 2))
                gla_store(j + (CT + 1))

            def c_begin(b):
                tok = slice(b * TB, (b + 1) * TB)
                if b:
                    pool.wait_ge(product, GC0 + GH)
                pool.wait_ge(cv_stored, 16 * 2 * CT * (b + 1))
                pool.dma_start(cin[:], convd[:, :, tok].rearrange("a p t -> p a t")).then_inc(c_loaded, 16)
                for t in range(3):
                    pool.dma_start(xin[:, t], x2[b * TB + t * P:b * TB + (t + 1) * P, :]).then_inc(x2_loaded[t], 16)

            def og_load(b, j):
                tok = slice(b * TB, (b + 1) * TB)
                if j >= 2:
                    og_v.wait(pool, b, f"lo{j - 2}")
                pool.dma_start(oin[b][:, j % 2], od[j, :, tok]).then_inc(o_loaded[j % 2], 16)
                pool.dma_start(ogin[b][:, j % 2], proj[OG + j, :, tok]).then_inc(o_loaded[j % 2], 16)

            def c_rest(b):
                for j in range(2, VT):
                    og_load(b, j)
                for t in range(3, TT):
                    xt_p.wait(pool, b, f"t{t - 3}")
                    pool.dma_start(xin[:, t % 3], x2[b * TB + t * P:b * TB + (t + 1) * P, :]).then_inc(x2_loaded[t % 3], 16)

            def results(b):
                for t in range(TT):
                    e_c.wait(pool, b, f"t{t}")
                    pool.dma_start(out2[b * TB + t * P:b * TB + (t + 1) * P, :], e_out[:, t % 2]).then_inc(out_stored[t % 2], 16)

            c_begin(0)
            gla_store(CH2 - 1)
            for s in range(RING):
                pool.wait_ge(stored[s], 16 + 2 * NAG // RING * 16)
            pool.wait_ge(g_stored, 16 * CH2)
            for j in range(2):
                og_load(0, j)
            gla_load(CH2)
            c_rest(0)

            for h, loops in ((2, CT), (3, CT - 1)):
                with pool.Fori(0, loops) as j:
                    n, unit = j + (CH2 + (h - 2) * CT), j + h * CT
                    conv_load(conv_d, unit, j, h)
                    gla_load(n + 1)
                    conv_store(conv_d, unit, j, h)
                    gla_store(n)
            conv_load(conv_d, 4 * CT - 1, CT - 1, 3)
            conv_store(conv_d, 4 * CT - 1, CT - 1, 3)
            gla_store(CHUNKS - 1)
            c_begin(1)
            pool.wait_ge(g_stored, 16 * CHUNKS)
            for j in range(2):
                og_load(1, j)
            results(0)
            c_rest(1)
            results(1)
            for s in range(2):
                pool.wait_ge(out_stored[s], 16 * TT)

        @block.scalar
        def _(act):
            for line in (prep_a, staged, f_a):
                line.begin(act)
            for s in stored:
                act.sem_inc(s, 16)

            def high(place, used):
                act.wait_ge(w_loaded[place.slot], place.uses * 16 + 16)
                if used is not None:
                    act.wait_ge(product, used)
                act.activation(w_hi[:, place.slot], w_raw[:, place.slot], ACT.Copy).then_inc(w_high, 1)

            def prep_norm(g):
                act.wait_ge(x_loaded[g], 16)
                for t in range(4):
                    prep_a.wait(act, g - 1 if t == 0 else g, "rstd" if t == 0 else f"sq{t - 1}")
                    prep_a.done(act.activation(p_junk[:], xnat[g][:, t], ACT.Square, accum_out=ssq4[:, t:t + 1]), f"sq{t}")
                prep_a.wait(act, g, "sq3")
                prep_v.wait(act, g - 1, "xn3")
                prep_a.done(act.activation(rstd4[:], ssq4[:], ACT.Ln, scale=1.0 / D, bias=eps[:]), "ln")
                prep_a.wait(act, g, "ln")
                prep_a.done(act.activation(rstd4[:], rstd4[:], ACT.Exp, scale=-0.5), "rstd")

            def prep_high(g):
                for k in range(KD):
                    prep_v.wait(act, g, f"t{k}")
                    prep_a.done(act.activation(h_hi[g // 2][:, k, half(g % 2)], p_tmp[:, k % 2], ACT.Copy), f"hi{k}")

            def sigmoid(bufs, unit, h):
                act.wait_ge(cv_loaded, unit * 32 + 32)
                part = slice(0 if h else PAD, PAD + NT)
                cv_a.done(act.activation(bufs[1][:, part], bufs[1][:, part], ACT.Sigmoid), "sig")

            def gla_gate(n):
                if isinstance(n, int) and n == 0:
                    g_zero.wait(act, 0, "one")
                for f in range(KT):
                    if f == 0:
                        gla_p.wait(act, n, "z")
                    gla_a.done(act.activation(g_kd[:, f], side[:, 3, f * C:(f + 1) * C], ACT.Identity,
                                              bias=vec("b_a2", f)), f"zb{f}")
                gla_a.wait(act, n, f"zb{KT - 1}")
                gla_v.wait(act, n - 1, "st1")
                gla_a.done(act.activation(g_ecum[:], g_kd[:], ACT.Abs), "zabs")
                gla_a.wait(act, n, "zabs")
                gla_a.done(act.activation(g_ecum[:], g_ecum[:], ACT.Exp, scale=-1.0), "zexp")
                gla_a.wait(act, n, "zexp")
                gla_a.done(act.activation(g_ecum[:], g_ecum[:], ACT.Ln, bias=ones[:, 0:1]), "zln")

            def gla_decays(n):
                act.wait_ge(g_loaded, n * 48 + 48)
                for e in range(2):
                    r = slice(e * HEAD_K, (e + 1) * HEAD_K)
                    gla_a.done(act.activation(g_qb[r, :, e], g_qk[r, 0:KT], ACT.Copy), f"qb{e}")
                gla_v.wait(act, n, f"sub{L[-1]}")
                gla_a.done(act.activation(g_lev[:], g_lev[:], ACT.Abs), "abs")
                gla_a.done(act.activation(g_ecum[:], g_cum[:], ACT.Exp), "ecum")
                for f in range(KT):
                    gla_a.done(act.activation(g_kd[:, f], g_cum[:, f], ACT.Exp, scale=-1.0,
                                              bias=g_cum[:, f, C - 1:C]), f"kdec{f}")
                gla_a.wait(act, n, "abs")
                gla_a.done(act.activation(g_lev[:], g_lev[:], ACT.Exp, scale=-1.0), "exp")

            def gla_turned(n):
                gla_p.wait(act, n, "vn")
                gla_a.done(act.activation(g_vn[:], side[:, 0], ACT.Copy), "vn")
                gla_p.wait(act, n, "kn")
                gla_a.done(act.activation(g_kn[:], side[:, 1, 0:KT * P], ACT.Copy), "kn")

            def gla_squares(n):
                gla_p.wait(act, n, "o")
                act.wait_ge(g_stored, n * 16)
                gla_a.done(act.activation(g_rs[:], side[:, 0], ACT.Square), "sq")

            def gla_rstd(n):
                gla_p.wait(act, n, "ss")
                gla_a.done(act.activation(g_rs[:], side[:, 2], ACT.Ln, scale=1.0 / (DV * HEAD_K), bias=eps[:]), "ln")
                gla_a.wait(act, n, "ln")
                gla_a.done(act.activation(g_rs[:], g_rs[:], ACT.Exp, scale=-0.5), "rstd")

            def in_proj(b, it, chunk=None, conv=None, prep=None):
                for n, (s, h) in enumerate(a_order(it)):
                    if n == 0 and prep is not None:
                        prep_norm(prep)
                        prep_high(prep)
                    if n == gla_slots(it)[0] and chunk is not None:
                        gla_gate(chunk)
                    if n == 0 and conv is not None and chunk is None:
                        sigmoid(conv_a, *conv)
                    p = a_place(b, it, s, h)
                    act.wait_ge(product, p.number + 1)
                    act.wait_ge(stored[p.slot], p.uses * 16 + 16)
                    staged.done(act.activation(stage[:, p.slot], banks[p.slot][:], ACT.Copy), "copy")
                    if h == HB - 1:
                        high(Place(b * NA + RING, s, it, 1), p.number + 1)
                    staged.wait(act, p.number, "copy")
                    act.dma_start(proj[bass.ds(a_tile(it, s)[0], 1), :, b * TB + h * NT:b * TB + (h + 1) * NT]
                                  .rearrange("a p t -> p (a t)"), stage[:, p.slot]).then_inc(stored[p.slot], 16)
                    if chunk is not None:
                        if n == gla_slots(it)[0]:
                            gla_decays(chunk)
                            if conv is not None:
                                sigmoid(conv_a, *conv)
                        if n == gla_slots(it)[1]:
                            gla_turned(chunk)
                        if n == gla_slots(it)[3]:
                            gla_squares(chunk)
                            gla_rstd(chunk)

            setup_v.wait(act, 0, "pvec")
            setup_a.done(act.activation(cact[:], pvec[:, col["c"]:col["c"] + KD], ACT.Silu), "cact")
            prep_norm(0)
            for s in range(RING):
                high(Place(0, s, 0, 1), None)
            prep_high(0)
            in_proj(0, 0, prep=1)
            in_proj(0, 1)
            with act.Fori(0, CT) as j:
                in_proj(0, j + 2, conv=(j, 0))
            in_proj(0, AI - 1, prep=2)
            in_proj(1, 0, prep=3, chunk=0)
            with act.Fori(0, CT) as j:
                in_proj(1, j + 1, chunk=j + 1, conv=(j + CT, 1))
            with act.Fori(0, AI - 1 - CT) as j:
                in_proj(1, j + (CT + 1), chunk=j + (CT + 1))
            for part in (gla_gate, gla_decays, gla_turned, gla_squares, gla_rstd):
                part(CH2 - 1)

            for b in range(2):
                n0, g0 = NC0 + b * NH, GC0 + b * GH
                act.wait_ge(c_loaded, 16 * (b + 1))
                for h in range(HB):
                    for j in range(CT):
                        ln_v.wait(act, b, f"d{h}{j}")
                        if h:
                            ln_p.wait(act, b, "var0")
                        ln_a.done(act.activation(ln_sq[b][:, j], cin[:, j, half(h)], ACT.Square), f"q{h}{j}")
                for h in range(HB):
                    ln_p.wait(act, b, f"var{h}")
                    ln_a.done(act.activation(ln_rs[b][:, half(h)], banks[h][:], ACT.Ln, scale=1.0 / DC, bias=eps[:]), f"ln{h}")
                    ln_a.wait(act, b, f"ln{h}")
                    ln_a.done(act.activation(ln_rs[b][:, half(h)], ln_rs[b][:, half(h)], ACT.Exp, scale=-0.5), f"rstd{h}")

                def silu_gate(j):
                    act.wait_ge(o_loaded[j % 2], 32 * (b * VT // 2 + j // 2 + 1))
                    og_a.done(act.activation(ogin[b][:, j % 2], ogin[b][:, j % 2], ACT.Silu), f"s{j}")

                def gated_high(j):
                    og_v.wait(act, b, f"m{j}")
                    og_a.done(act.activation(y_hi[:, CT + j], oin[b][:, j % 2], ACT.Copy), f"hi{j}")

                silu_gate(0)
                for h in range(HB):
                    for j in range(CT):
                        ln_v.wait(act, b, f"n{h}{j}")
                        ln_a.done(act.activation(cin[:, j, half(h)], cin[:, j, half(h)], ACT.Silu, scale=vec("ln_g", j),
                                                 bias=vec("ln_b", j)), f"y{h}{j}")
                    for j in range(CT):
                        ln_a.wait(act, b, f"y{h}{j}")
                        ln_a.done(act.activation(y_hi[:, j, half(h)], cin[:, j, half(h)], ACT.Copy), f"hi{h}{j}")
                    gated_high(h)
                    silu_gate(h + 1)
                gated_high(2)
                silu_gate(3)
                gated_high(3)

                og_v.wait(act, b, f"lo{VT - 1}")
                def turned(t0, t1):
                    for t in range(t0, t1):
                        xt_p.wait(act, b, f"t{t}")
                        w = 2 * (t % 2)
                        xt_a.done(act.activation(xacc[:, :, t * P:(t + 1) * P],
                                                 side[:, w:w + 2].rearrange("p a (k t) -> p (a k) t", t=P), ACT.Copy), f"t{t}")

                turned(0, 4)
                for s in range(KD):
                    for h in range(HB):
                        if s == 0:
                            turned(4 + 2 * h, 6 + 2 * h)
                        u = b * KD * HB + s * HB + h
                        res_v.wait(act, u - 2, "ss")
                        res_v.wait(act, u, "x")
                        res_a.done(act.activation(c_sq[:, h], xacc[:, s, half(h)], ACT.Square), "sq")
                    high(Place(n0 + RING + s, 0, 0, 1), g0 + (s + 1) * HB)
                n_p.wait(act, b, "ss")
                n_a.done(act.activation(n_rs[:], side[:, 0:HB], ACT.Ln, scale=1.0 / D, bias=eps[:]), "ln")
                n_a.wait(act, b, "ln")
                n_a.done(act.activation(n_rs[:], n_rs[:], ACT.Exp, scale=-0.5), "rstd")
                for k in range(KD):
                    n_v.wait(act, b, f"t{k}")
                    n_a.done(act.activation(h2_hi[:, k], n_t[:, k % 2], ACT.Identity, bias=mod(3, k)), f"hi{k}")

                nf, gf = n0 + KD, g0 + KD * HB

                def ffn(i, last=False, chunk=None, conv=None):
                    i0 = i * (4 * HB + OUTS) + gf
                    if chunk is not None:
                        gla_gate(chunk)
                    for f in range(2):
                        for h in range(HB):
                            u = i * PAIRS + (b * FI * PAIRS + f * HB + h)
                            pg = Place(gf, 2 * (f * HB + h), i, (4 * HB + OUTS) // RING)
                            act.wait_ge(product, pg.number + 1)
                            f_v.wait(act, u - 2, "a")
                            f_a.done(act.activation(sil[:, h], banks[pg.slot][:], ACT.Silu), "silu")
                            if (f, h) == (1, HB - 1):
                                high(Place(nf + RING, 2, i, 2), i0 + (4 * HB - 1))
                            f_v.wait(act, u, "a")
                            f_a.done(act.activation(act_hi[:, f, half(h)], af[:, h], ACT.Copy), "hi")
                            if (f, h) == (0, 0) and chunk is not None:
                                gla_decays(chunk)
                                sigmoid(conv_d, *conv)
                        if f == 0:
                            high(Place(nf + RING, 0, i, 2), i0 + 2 * HB)
                            high(Place(nf + RING, 1, i, 2), i0 + 2 * HB)
                            if chunk is not None:
                                gla_turned(chunk)
                    if not last:
                        high(Place(nf + RING, 3, i, 2), i0 + 4 * HB)
                    if chunk is not None:
                        gla_squares(chunk)
                        gla_rstd(chunk)
                    if not last:
                        high(Place(nf + RING, 4, i, 2), i0 + (4 * HB + OUTS))
                        high(Place(nf + RING, 5, i, 2), i0 + (4 * HB + OUTS))

                if b == 0:
                    for h in range(2, 4):
                        with act.Fori(0, CT) as j:
                            ffn(j + (h - 2) * CT, chunk=j + (CH2 + (h - 2) * CT), conv=(j + h * CT, h))
                    with act.Fori(0, FI - 2 * CT) as j:
                        ffn(j + 2 * CT)
                else:
                    with act.Fori(0, FI - 1) as i:
                        ffn(i)
                    ffn(FI - 1, last=True)

                for h in range(HB):
                    for k in range(KD):
                        f_o.wait(act, (b + 1) * FI - 1, f"o{h * KD + k}")
                        if h or k >= 2:
                            e_p.wait(act, b, f"ss{h}{k - 2}" if k >= 2 else f"ss{h - 1}{KD - 2 + k}")
                        e_a.done(act.activation(e_sq[:, k % 2], xacc[:, k, half(h)], ACT.Square), f"sq{h}{k}")
                for h in range(HB):
                    e_p.wait(act, b, f"ss{h}{KD - 1}")
                    e_a.done(act.activation(e_rs[:, half(h)], side[:, 4 - h], ACT.Ln, scale=1.0 / D, bias=eps[:]), f"ln{h}")
                    e_a.wait(act, b, f"ln{h}")
                    e_a.done(act.activation(e_rs[:, half(h)], e_rs[:, half(h)], ACT.Exp, scale=-0.5), f"rstd{h}")
                for h in range(HB):
                    for k in range(KD):
                        e_v.wait(act, b, f"t{h}{k}")
                        e_a.done(act.activation(xacc[:, k, half(h)], xacc[:, k, half(h)], ACT.Identity, bias=mod(6, k)), f"b{h}{k}")
                    for t in range(h * NT // P, (h + 1) * NT // P):
                        e_p.wait(act, b, f"t{t}")
                        if b or t >= 2:
                            act.wait_ge(out_stored[t % 2], 16 * ((b * TT + t) // 2))
                        e_c.done(act.activation(e_out[:, t % 2], side[:, 2 * (t % 2):2 * (t % 2) + 2], ACT.Copy), f"t{t}")

        @block.vector
        def _(dve):
            dve.sem_inc(w_low, RING)
            for line in (mod_v, prep_v, cv_v, gla_v, res_v, f_v, f_o):
                line.begin(dve)

            def low(place):
                dve.wait_ge(w_high, place.number + 1)
                dve.tensor_tensor(w_lo[:, place.slot], w_raw[:, place.slot], w_hi[:, place.slot].bitcast(F32),
                                  ALU.subtract).then_inc(w_low, 1)

            def mod_sum(m):
                for k in range(KD):
                    if isinstance(m, int) and m < 2:
                        dve.wait_ge(m_loaded[k % 4], m * 32 + 16 * (k // 4 + 1))
                    else:
                        dve.wait_ge(m2_loaded[k % 4], (m - 2) * 32 + 16 * (k // 4 + 1))
                    if k == 0:
                        ins = dve.tensor_scalar(m_acc[:], m_raw[:, 0], cact[:, 0:1], None, ALU.mult)
                    else:
                        mod_v.wait(dve, m, f"k{k - 1}")
                        ins = dve.scalar_tensor_tensor(m_acc[:], m_raw[:, k % 4], cact[:, k:k + 1], m_acc[:],
                                                       ALU.mult, ALU.add)
                    mod_v.done(ins, f"k{k}")

            def mod_vec(m):
                mod_p.wait(dve, m, "sum")
                mod_v.done(dve.tensor_tensor(modv[:, bass.ds(m * KD, KD)], side[:, 4, 0:KD],
                                             pvec[:, bass.ds(m * KD, KD)], ALU.add), "vec")

            def prep_rows(g):
                prep_a.wait(dve, g, "rstd")
                for t in range(4):
                    prep_v.done(dve.tensor_scalar(xnat[g][:, t], xnat[g][:, t], rstd4[:, t:t + 1], None, ALU.mult), f"xn{t}")

            def prep_low(g):
                for k in range(KD):
                    prep_p.wait(dve, g, f"k{k}")
                    prep_a.wait(dve, g if k >= 2 else g - 1, f"hi{(k - 2) % KD}")
                    if k >= 2:
                        prep_v.wait(dve, g, f"lo{k - 2}")
                    prep_v.done(dve.tensor_scalar(p_tmp[:, k % 2], side[:, k % 4], gain1[:, k:k + 1], mod(0, k),
                                                  ALU.mult, ALU.add), f"t{k}")
                    if k:
                        prep_lo(g, k - 1)
                prep_lo(g, KD - 1)

            def prep_lo(g, k):
                prep_a.wait(dve, g, f"hi{k}")
                prep_v.done(dve.tensor_tensor(h_lo[g // 2][:, k, half(g % 2)], p_tmp[:, k % 2],
                                              h_hi[g // 2][:, k, half(g % 2)].bitcast(F32), ALU.subtract), f"lo{k}")

            def conv_in(bufs, unit, j, h):
                cv, cg = bufs[0:2]
                part = slice(0 if h else PAD, PAD + NT)
                dve.wait_ge(cv_loaded, unit * 32 + 32)
                cv_a.wait(dve, unit, "sig")
                cv_v.wait(dve, unit - 1, "sum")
                cv_v.done(dve.tensor_tensor(cv[:, part], cv[:, part], cg[:, part], ALU.mult), "u")
                dve.wait_ge(cv_stored, unit * 16)

            def conv_taps(first, count, bufs, unit, j, h):
                for k in range(first, min(first + count, TAPS)):
                    a, tap = bufs[2 + k % 2], taps[:, bass.ds(j + k * CT, 1)]
                    cv_v.wait(dve, unit, f"tap{k - 2}" if k >= 2 else "u")
                    if k == 0:
                        ins = dve.tensor_scalar(a[:], bufs[0][:, 0:NT], tap, pvec[:, bass.ds(j + col["conv_b"], 1)],
                                                ALU.mult, ALU.add)
                    elif k == 1:
                        ins = dve.tensor_scalar(a[:], bufs[0][:, 1:1 + NT], tap, None, ALU.mult)
                    else:
                        ins = dve.scalar_tensor_tensor(a[:], bufs[0][:, k:k + NT], tap, a[:], ALU.mult, ALU.add)
                    cv_v.done(ins, f"tap{k}")

            def conv_out(bufs, unit, j, h):
                cv_v.wait(dve, unit, f"tap{TAPS - 1}")
                cv_v.wait(dve, unit, f"tap{TAPS - 2}")
                cv_v.done(dve.tensor_tensor(bufs[2][:], bufs[2][:], bufs[3][:], ALU.add), "sum")

            def gla_zero():
                g_zero.done(dve.memset(g_st[:], 0.0), "st")
                g_zero.done(dve.memset(g_state[:], 0.0), "state")
                g_zero.done(dve.memset(g_qd[:], 0.0), "qd")
                g_zero.done(dve.memset(g_qb[:], 0.0), "qb")
                g_zero.done(dve.memset(g_ql[:], 0.0), "ql")
                g_zero.done(dve.memset(g_one[:], 1.0), "one")

            def gla_cum(n):
                cum_all = g_cum[:].rearrange("p a t -> p (a t)")
                gla_a.wait(dve, n, f"zb{KT - 1}")
                gla_v.done(dve.tensor_scalar(g_la[:], g_kd[:], 0.0, 1.0 / GATE_TAU, ALU.min, ALU.mult), "min")
                gla_a.wait(dve, n, "zln")
                gla_v.wait(dve, n, "min")
                gla_v.done(dve.scalar_tensor_tensor(g_la[:], g_ecum[:], -1.0 / GATE_TAU, g_la[:], ALU.mult, ALU.add), "la")
                gla_v.wait(dve, n, "la")
                for f in range(KT):
                    gla_v.done(dve.tensor_tensor_scan(g_cum[:, f], g_one[:], g_la[:, f], 0.0, ALU.mult, ALU.add), f"cum{f}")
                gla_v.wait(dve, n, "cum1")
                for l, s in enumerate(LEVELS):
                    c3 = pairs(cum_all, s)
                    gla_v.done(dve.tensor_tensor(pairs(g_lev[:, l], s), c3,
                                                 c3[:, :, s - 1:s].to_broadcast([P, KT * C // (2 * s), 2 * s]),
                                                 ALU.subtract), f"sub{l}")

            def gla_levels(n):
                k_all = g_qk[:, KT:2 * KT].rearrange("p a t -> p (a t)")
                dve.wait_ge(g_loaded, n * 48 + 48)
                gla_a.wait(dve, n, f"kdec{KT - 1}")
                for e in range(2):
                    r = slice(e * HEAD_K, (e + 1) * HEAD_K)
                    gla_v.done(dve.tensor_tensor(g_qd[r, :, e], g_ecum[r], g_qk[r, 0:KT], ALU.mult), f"qd{e}")
                gla_v.done(dve.tensor_tensor(g_kd[:], g_kd[:], g_qk[:, KT:2 * KT], ALU.mult), "kd")
                gla_a.wait(dve, n, "exp")
                for l, s in enumerate(LEVELS):
                    e3 = pairs(g_lev[:, l], s)
                    for e in range(2):
                        r = slice(e * HEAD_K, (e + 1) * HEAD_K)
                        gla_v.done(dve.tensor_tensor(
                            g_ql[r, l, :, e].rearrange("p a (r w) -> p a r w", w=s),
                            g_lev[r, l].rearrange("p (a r w) -> p a r w", a=KT, w=2 * s)[:, :, :, s:2 * s],
                            g_qk[r, 0:KT].rearrange("p a (r w) -> p a r w", w=2 * s)[:, :, :, s:2 * s],
                            ALU.mult), f"q{'ab'[e]}{l}")
                    gla_v.done(dve.tensor_tensor(e3[:, :, 0:s], e3[:, :, 0:s], pairs(k_all, s)[:, :, 0:s],
                                                 ALU.mult), f"k{l}")

            def gla_picks(n):
                gla_p.wait(dve, n, "lev")
                st_all = g_st[:].rearrange("p h t -> p (h t)")
                for l, s in enumerate(LEVELS):
                    w = HEADS * C // 2
                    if l:
                        gla_v.wait(dve, n, f"pick{l - 1}")
                    dve.sem_inc(picks, 1)
                    data = side[:, l // 2, (l % 2) * w:(l % 2 + 1) * w]
                    gla_v.done(dve.copy_predicated(pairs(st_all, s)[:, :, s:2 * s],
                                                   g_mask[:, l * w:(l + 1) * w].rearrange("p (r w) -> p r w", w=s),
                                                   data.rearrange("p (r w) -> p r w", w=s)), f"pick{l}")
                gla_p.wait(dve, n, "diag")
                gla_v.wait(dve, n, f"pick{L[-1]}")
                dve.sem_inc(picks, 1)
                gla_v.done(dve.copy_predicated(st_all, g_mask[:, len(LEVELS) * HEADS * C // 2:], side[:, 4]), "pickd")

            def gla_out(n):
                gla_p.wait(dve, n, "state")
                for f in range(KT):
                    gla_v.done(dve.scalar_tensor_tensor(g_state[:, f], g_state[:, f], g_ecum[:, f, C - 1:C],
                                                        side[:, 1, f * DV:(f + 1) * DV], ALU.mult, ALU.add), f"st{f}")
                gla_a.wait(dve, n, "rstd")
                gla_v.done(dve.tensor_scalar(g_rs[:], g_rs[:], vec("gla_g"), HEAD_K ** -0.5, ALU.mult, ALU.mult), "gain")
                gla_v.wait(dve, n, "gain")
                gla_v.done(dve.tensor_tensor(g_rs[:], side[:, 0], g_rs[:], ALU.mult), "on")

            def in_proj(b, it, chunk=None, conv=None, prep=None, mods=()):
                if prep is not None:
                    prep_rows(prep)
                    prep_low(prep)
                first = isinstance(it, int) and it == 0
                if chunk is not None:
                    if first:
                        dve.wait_ge(product, NAG)
                        gla_zero()
                        g_zero.wait(dve, 0, "one")
                    gla_cum(chunk)
                    if first:
                        gla_levels(chunk)
                if conv:
                    conv_in(conv_a, *conv)
                    conv_taps(0, A_T0, conv_a, *conv)
                if mods and not conv:
                    mod_sum(mods[0])
                low(Place(b * NA + RING, 0, it, 1))
                if mods and conv:
                    mod_sum(mods[0])
                if mods and not conv:
                    mod_vec(mods[0])
                    mod_sum(mods[1])
                if chunk is not None and not first:
                    gla_levels(chunk)
                if conv:
                    conv_taps(A_T0, A_T1, conv_a, *conv)
                low(Place(b * NA + RING, 1, it, 1))
                if mods:
                    mod_vec(mods[-1])
                if chunk is not None:
                    gla_picks(chunk)
                if conv:
                    conv_taps(A_T0 + A_T1, TAPS, conv_a, *conv)
                    conv_out(conv_a, *conv)
                low(Place(b * NA + RING, 2, it, 1))
                if chunk is not None:
                    gla_out(chunk)

            setup_v.done(dve.memset(ones[:], 1.0), "ones")
            setup_v.done(dve.memset(eps[:], EPS), "eps")
            setup_p.wait(dve, 0, "rows")
            setup_v.done(dve.tensor_copy(pvec[:, 0:ncol], side[:, 0, 0:ncol]), "pvec")
            setup_p.wait(dve, 0, "taps")
            setup_v.done(dve.tensor_copy(taps[:], side[:, 1, 0:TAPS * CT]), "taps")
            setup_v.done(dve.tensor_copy(g_mask[:], mask_f[:]), "mask")
            setup_v.done(dve.memset(conv_a[0][:, 0:PAD], 0.0), "pad")
            setup_a.wait(dve, 0, "cact")
            mod_sum(0)
            mod_vec(0)
            prep_rows(0)
            for s in range(RING):
                low(Place(0, s, 0, 1))
            mod_sum(1)
            mod_vec(1)
            mod_v.wait(dve, 1, "vec")
            gains_v.done(dve.scalar_tensor_tensor(gain1[:], modv[:, KD:2 * KD], 1.0,
                                                  pvec[:, col["g_mix"]:col["g_mix"] + KD], ALU.add, ALU.mult), "g1")
            gains_v.wait(dve, 0, "g1")
            prep_low(0)
            in_proj(0, 0, prep=1)
            in_proj(0, 1, mods=(2, 3))
            with dve.Fori(0, CT) as j:
                in_proj(0, j + 2, conv=(j, j, 0), mods=(j + 4,))
            in_proj(0, AI - 1, prep=2)
            mod_v.wait(dve, 7, "vec")
            gains_v.done(dve.scalar_tensor_tensor(gain2[:], modv[:, 4 * KD:5 * KD], 1.0,
                                                  pvec[:, col["g_ffn"]:col["g_ffn"] + KD], ALU.add, ALU.mult), "g2")
            gains_v.done(dve.scalar_tensor_tensor(gainf[:], modv[:, 7 * KD:8 * KD], 1.0,
                                                  pvec[:, col["g_fin"]:col["g_fin"] + KD], ALU.add, ALU.mult), "gf")
            in_proj(1, 0, prep=3, chunk=0)
            with dve.Fori(0, CT) as j:
                in_proj(1, j + 1, chunk=j + 1, conv=(j + CT, j, 1))
            with dve.Fori(0, AI - 1 - CT) as j:
                in_proj(1, j + (CT + 1), chunk=j + (CT + 1))
            for part in (gla_cum, gla_levels, gla_picks, gla_out):
                part(CH2 - 1)

            for b in range(2):
                n0 = NC0 + b * NH
                dve.wait_ge(c_loaded, 16 * (b + 1))
                for h in range(HB):
                    ln_p.wait(dve, b, f"mean{h}")
                    for j in range(CT):
                        ln_v.done(dve.scalar_tensor_tensor(cin[:, j, half(h)], banks[h][:], -1.0 / DC, cin[:, j, half(h)],
                                                           ALU.mult, ALU.add), f"d{h}{j}")

                def gated(j):
                    og_a.wait(dve, b, f"s{j}")
                    og_v.done(dve.tensor_tensor(oin[b][:, j % 2], oin[b][:, j % 2], ogin[b][:, j % 2], ALU.mult), f"m{j}")

                def gated_low(j):
                    og_a.wait(dve, b, f"hi{j}")
                    if b and j == 0:
                        for s in range(2):
                            dve.wait_ge(out_stored[s], 16 * (TB // P) // 2)
                    og_v.done(dve.tensor_tensor(y_lo[:, CT + j], oin[b][:, j % 2], y_hi[:, CT + j].bitcast(F32),
                                                ALU.subtract), f"lo{j}")

                for h in range(HB):
                    ln_a.wait(dve, b, f"rstd{h}")
                    for j in range(CT):
                        ln_v.done(dve.tensor_tensor(cin[:, j, half(h)], cin[:, j, half(h)], ln_rs[b][:, half(h)], ALU.mult),
                                  f"n{h}{j}")
                    if h:
                        gated_low(0)
                    gated(h)
                    for j in range(CT):
                        ln_a.wait(dve, b, f"hi{h}{j}")
                        ln_v.done(dve.tensor_tensor(y_lo[:, j, half(h)], cin[:, j, half(h)],
                                                    y_hi[:, j, half(h)].bitcast(F32), ALU.subtract), f"lo{h}{j}")
                gated_low(1)
                gated(2)
                gated_low(2)
                gated(3)
                gated_low(3)
                zero_v.done(dve.memset(ssq[:], 0.0), "ssq")
                zero_v.wait(dve, b, "ssq")

                for s in range(KD):
                    for h in range(HB):
                        p = Place(GC0 + b * GH + s * HB + h, 0, 0, 1)
                        u = b * KD * HB + s * HB + h
                        dve.wait_ge(product, p.number + 1)
                        if s == 0:
                            xt_a.wait(dve, b, f"t{4 * h + 3}")
                        res_v.done(dve.scalar_tensor_tensor(xacc[:, s, half(h)], banks[p.slot][:], mod(2, s),
                                                            xacc[:, s, half(h)], ALU.mult, ALU.add), "x")
                        if h:
                            low(Place(n0 + RING + s, 0, 0, 1))
                        res_a.wait(dve, u, "sq")
                        res_v.done(dve.tensor_tensor(ssq[:, half(h)], ssq[:, half(h)], c_sq[:, h], ALU.add), "ss")

                n_a.wait(dve, b, "rstd")
                for k in range(KD):
                    if k >= 2:
                        n_a.wait(dve, b, f"hi{k - 2}")
                        n_v.wait(dve, b, f"lo{k - 2}")
                    n_v.done(dve.scalar_tensor_tensor(n_t[:, k % 2], xacc[:, k], gain2[:, k:k + 1], n_rs[:],
                                                      ALU.mult, ALU.mult), f"t{k}")
                    for d in (k - 1,) if k < KD - 1 else (k - 1, k):
                        if d >= 0:
                            n_a.wait(dve, b, f"hi{d}")
                            n_v.done(dve.scalar_tensor_tensor(h2_lo[:, d], n_t[:, d % 2], mod(3, d),
                                                              h2_hi[:, d].bitcast(F32), ALU.add, ALU.subtract), f"lo{d}")

                nf, gf = n0 + KD, GC0 + b * GH + KD * HB

                def ffn(i, last=False, chunk=None, conv=None):
                    if chunk is not None:
                        gla_cum(chunk)
                    for f in range(2):
                        for h in range(HB):
                            u = i * PAIRS + (b * FI * PAIRS + f * HB + h)
                            pu = Place(gf, 2 * (f * HB + h) + 1, i, (4 * HB + OUTS) // RING)
                            f_a.wait(dve, u, "silu")
                            f_a.wait(dve, u - 2, "hi")
                            if (f, h) == (1, HB - 1):
                                low(Place(nf + RING, 2, i, 2))
                            dve.wait_ge(product, pu.number + 1)
                            f_v.done(dve.tensor_tensor(af[:, h], banks[pu.slot][:], sil[:, h], ALU.mult), "a")
                            f_a.wait(dve, u, "hi")
                            f_v.done(dve.tensor_tensor(act_lo[:, f, half(h)], af[:, h],
                                                       act_hi[:, f, half(h)].bitcast(F32), ALU.subtract), "lo")
                            if (f, h) == (0, 0) and chunk is not None:
                                gla_levels(chunk)
                            if (f, h) == (1, 0) and chunk is not None:
                                gla_picks(chunk)
                        if f == 0:
                            low(Place(nf + RING, 0, i, 2))
                            low(Place(nf + RING, 1, i, 2))
                            if conv:
                                conv_in(conv_d, *conv)
                                conv_taps(0, D_T0, conv_d, *conv)
                    if not last:
                        low(Place(nf + RING, 3, i, 2))
                    for q in range(OUTS):
                        po = Place(gf, 4 * HB + q, i, (4 * HB + OUTS) // RING)
                        k, h = q % KD, q // KD
                        dve.wait_ge(product, po.number + 1)
                        f_o.done(dve.scalar_tensor_tensor(xacc[:, k, half(h)], banks[po.slot][:], mod(5, k),
                                                          xacc[:, k, half(h)], ALU.mult, ALU.add), f"o{q}")
                        if conv:
                            conv_taps(D_T0 + q, 1, conv_d, *conv)
                    if not last:
                        low(Place(nf + RING, 4, i, 2))
                        low(Place(nf + RING, 5, i, 2))
                    if conv:
                        conv_taps(D_T0 + OUTS, TAPS, conv_d, *conv)
                        conv_out(conv_d, *conv)
                    if chunk is not None:
                        gla_out(chunk)

                if b == 0:
                    for h in range(2, 4):
                        with dve.Fori(0, CT) as j:
                            ffn(j + (h - 2) * CT, chunk=j + (CH2 + (h - 2) * CT), conv=(j + h * CT, j, h))
                    with dve.Fori(0, FI - 2 * CT) as j:
                        ffn(j + 2 * CT)
                else:
                    with dve.Fori(0, FI - 1) as i:
                        ffn(i)
                    ffn(FI - 1, last=True)

                for h in range(HB):
                    e_a.wait(dve, b, f"rstd{h}")
                    for k in range(KD):
                        e_v.done(dve.scalar_tensor_tensor(xacc[:, k, half(h)], xacc[:, k, half(h)], gainf[:, k:k + 1],
                                                          e_rs[:, half(h)], ALU.mult, ALU.mult), f"t{h}{k}")

        @block.tensor
        def _(pe):
            gla_p.begin(pe)

            def parts(out_ap, terms):
                for n, (w1, w2, r1, r2) in enumerate(terms):
                    pe.matmul(out_ap, w1, r1, start=(n == 0), stop=False)
                    pe.matmul(out_ap, w1, r2, start=False, stop=False)
                    mm = pe.matmul(out_ap, w2, r1, start=False, stop=(n == len(terms) - 1))
                return mm

            def low_made(place):
                pe.wait_ge(w_low, place.number + (RING + 1))

            def mod_add(m):
                mod_v.wait(pe, m, f"k{KD - 1}")
                mod_v.wait(pe, m - 1, "vec")
                for j in range(KD):
                    mm = pe.matmul(side[:, 4, j:j + 1], m_acc[:, j * P:(j + 1) * P], ones[:, 0:1], start=True, stop=True)
                mod_p.done(mm, "sum")

            def prep_turn(g, k0, k1):
                for k in range(k0, k1):
                    prep_v.wait(pe, g, "xn3")
                    prep_v.wait(pe, g if k >= 4 else g - 1, f"t{(k - 4) % KD}")
                    for t in range(4):
                        mm = pe.transpose(side[:, k % 4, t * P:(t + 1) * P], xnat[g][:, t, k * P:(k + 1) * P], ident[:])
                    prep_p.done(mm, f"k{k}")

            def gla_z(n):
                pe.wait_ge(g_loaded, n * 48 + 48)
                for f in range(KT):
                    mm = pe.matmul(side[:, 3, f * C:(f + 1) * C], a2[0:RANK, f * P:(f + 1) * P], g_al[0:RANK, :],
                                   start=True, stop=True)
                gla_p.done(mm, "z")

            def gla_turn(n):
                gla_v.wait(pe, n - 1, "on")
                for h in range(HEADS):
                    mm = pe.transpose(side[:, 0, h * C:(h + 1) * C], g_vt[:, h], ident[:])
                gla_p.done(mm, "vn")
                gla_v.wait(pe, n, "kd")
                for f in range(KT):
                    mm = pe.transpose(side[:, 1, f * P:(f + 1) * P], g_kd[:, f], ident[:])
                gla_p.done(mm, "kn")

            def gla_scores(n):
                w = HEADS * C // 2
                gla_v.wait(pe, n, f"k{L[-1]}")
                gla_a.wait(pe, n, "kn")
                for l in L:
                    for f in range(KT):
                        o = (l % 2) * w + f * C
                        mm = pe.matmul(side[:, l // 2, o:o + C], g_lev[:, l, f * C:(f + 1) * C],
                                       g_ql[:, l, f].rearrange("p e t -> p (e t)"), start=True, stop=True)
                gla_p.done(mm, "lev")
                for f in range(KT):
                    mm = pe.matmul(side[:, 4, f * 2 * C:(f + 1) * 2 * C], g_qk[:, KT + f],
                                   g_qb[:, f].rearrange("p e t -> p (e t)"), start=True, stop=True)
                gla_p.done(mm, "diag")

            def gla_apply(n):
                gla_v.wait(pe, n, "pickd")
                gla_v.wait(pe, n - 1, "st1")
                for f in range(KT):
                    pe.matmul(side[:, 0, f * 2 * C:(f + 1) * 2 * C], g_state[:, f],
                              g_qd[:, f].rearrange("p e t -> p (e t)"), start=True, stop=True, skip_group_check=True)
                    for h in range(2 * f, 2 * f + 2):
                        mm = pe.matmul(side[:, 0, h * C:(h + 1) * C], g_vn[:, h * DV:(h + 1) * DV], g_st[:, h],
                                       start=False, stop=True, skip_group_check=True)
                gla_p.done(mm, "o")
                for h in range(HEADS):
                    f, r = h // 2, slice((h % 2) * HEAD_K, (h % 2 + 1) * HEAD_K)
                    mm = pe.matmul(side[r, 1, f * DV:(f + 1) * DV], g_kn[:, h * HEAD_K:(h + 1) * HEAD_K],
                                   g_vn[:, h * DV:(h + 1) * DV], start=True, stop=True)
                gla_p.done(mm, "state")

            def gla_norm(n):
                gla_a.wait(pe, n, "sq")
                gla_p.done(pe.matmul(side[:, 2], ones[:], g_rs[:], start=True, stop=True), "ss")

            def in_proj(b, it, chunk=None, prep=None, mods=()):
                for n, (s, h) in enumerate(a_order(it)):
                    if prep is not None:
                        if n == 0:
                            prep_turn(prep, 0, 4)
                        if n == 2:
                            prep_turn(prep, 4, KD)
                    if h == 0:
                        low_made(Place(b * NA, s, it, 1))
                    if isinstance(it, int) and it == 0:
                        prep_v.wait(pe, 2 * b + h, f"lo{KD - 1}")
                    if chunk is not None and n == gla_slots(it)[0]:
                        gla_z(chunk)
                    p = a_place(b, it, s, h)
                    staged.wait(pe, p.number - RING, "copy")
                    parts(banks[p.slot][:], [(w_hi[:, s, k], w_lo[:, s, k], h_hi[b][:, k, half(h)], h_lo[b][:, k, half(h)])
                                             for k in range(KD)]).then_inc(product, 1)
                    if chunk is not None:
                        if n == gla_slots(it)[1]:
                            gla_turn(chunk)
                        if n == gla_slots(it)[2]:
                            gla_scores(chunk)
                        if n == gla_slots(it)[3]:
                            gla_apply(chunk)
                            gla_norm(chunk)
                    if mods and n == (2 if len(mods) == 2 else 4):
                        mod_add(mods[0])
                    if len(mods) == 2 and n == 5:
                        mod_add(mods[1])

            pe.wait_ge(const_in, 16 * (1 + len(names) + 3))
            setup_p.done(pe.transpose(side[:, 0, 0:ncol], rows[0:ncol, 0, :], ident[0:ncol, 0:ncol]), "rows")
            setup_p.done(pe.transpose(side[:, 1, 0:TAPS * CT], rows[0:TAPS * CT, 1, :],
                                      ident[0:TAPS * CT, 0:TAPS * CT]), "taps")
            setup_v.wait(pe, 0, "taps")
            for m in range(2):
                mod_add(m)
            prep_turn(0, 0, KD)
            in_proj(0, 0, prep=1)
            in_proj(0, 1, mods=(2, 3))
            with pe.Fori(0, CT) as j:
                in_proj(0, j + 2, mods=(j + 4,))
            in_proj(0, AI - 1, prep=2)
            in_proj(1, 0, prep=3, chunk=0)
            with pe.Fori(0, AI - 1) as j:
                in_proj(1, j + 1, chunk=j + 1)
            for part in (gla_z, gla_turn, gla_scores, gla_apply, gla_norm):
                part(CH2 - 1)

            for b in range(2):
                n0, g0 = NC0 + b * NH, GC0 + b * GH
                if b == 0:
                    staged.wait(pe, 2 * NAG - 1, "copy")
                else:
                    f_o.wait(pe, FI - 1, f"o{OUTS - 1}")
                pe.wait_ge(c_loaded, 16 * (b + 1))
                for h in range(HB):
                    for j in range(CT):
                        mm = pe.matmul(banks[h][:], ones[:], cin[:, j, half(h)], start=(j == 0), stop=(j == CT - 1))
                    ln_p.done(mm, f"mean{h}")
                for h in range(HB):
                    ln_v.wait(pe, b, f"d{h}{CT - 1}")
                    for j in range(CT):
                        ln_a.wait(pe, b, f"q{h}{j}")
                        mm = pe.matmul(banks[h][:], ones[:], ln_sq[b][:, j], start=(j == 0), stop=(j == CT - 1))
                    ln_p.done(mm, f"var{h}")
                if b == 0:
                    gla_v.wait(pe, CH2 - 1, "on")
                else:
                    e_c.wait(pe, 0, f"t{TT - 1}")

                def turn(t):
                    pe.wait_ge(x2_loaded[t % 3], 16 * (b * ((TT - t % 3 + 2) // 3) + t // 3 + 1))
                    if t >= 2:
                        xt_a.wait(pe, b, f"t{t - 2}")
                    for k in range(KD):
                        mm = pe.transpose(side[:, 2 * (t % 2) + k // 4, (k % 4) * P:(k % 4 + 1) * P],
                                          xin[:, t % 3, k * P:(k + 1) * P], ident[:])
                    xt_p.done(mm, f"t{t}")

                turn(0)
                turn(1)
                ln_v.wait(pe, b, f"lo{HB - 1}{CT - 1}")
                og_v.wait(pe, b, f"lo{VT - 1}")

                for s in range(KD):
                    for h in range(HB):
                        p = Place(n0 + s, 0, 0, 1)
                        low_made(p)
                        pb = Place(g0 + s * HB + h, 0, 0, 1)
                        u = b * KD * HB + s * HB + h
                        if b or s * HB + h >= RING:
                            res_v.wait(pe, u - RING, "x")
                        parts(banks[pb.slot][:], [(w_hi[:, p.slot, k], w_lo[:, p.slot, k], y_hi[:, k, half(h)],
                                                   y_lo[:, k, half(h)]) for k in range(KD)]).then_inc(product, 1)
                        if s * HB + h < (TT - 2) // 2:
                            turn(2 + 2 * (s * HB + h))
                            turn(3 + 2 * (s * HB + h))
                xt_a.wait(pe, b, f"t{TT - 1}")
                res_v.wait(pe, (b + 1) * KD * HB - 1, "ss")
                for h in range(HB):
                    mm = pe.matmul(side[:, h], ones[:], ssq[:, half(h)], start=True, stop=True)
                n_p.done(mm, "ss")
                n_v.wait(pe, b, f"lo{KD - 1}")

                nf, gf = n0 + KD, g0 + KD * HB
                per = (4 * HB + OUTS) // RING

                def ffn(i, chunk=None):
                    it = i + b * FI
                    if chunk is not None:
                        gla_z(chunk)
                    for f in range(2):
                        for h in range(HB):
                            x_ = f * HB + h
                            u = i * PAIRS + (b * FI * PAIRS + x_)
                            for up in range(2):
                                w = Place(nf, 2 * f + up, i, 2)
                                pg = Place(gf, 2 * x_ + up, i, per)
                                if h == 0:
                                    low_made(w)
                                if 2 * x_ + up < RING:
                                    f_o.wait(pe, it - 1, f"o{OUTS - RING + 2 * x_ + up}")
                                elif up:
                                    f_a.wait(pe, u - 1, "silu")
                                else:
                                    f_v.wait(pe, u - 2, "a")
                                parts(banks[pg.slot][:], [(w_hi[:, w.slot, k], w_lo[:, w.slot, k], h2_hi[:, k, half(h)],
                                                           h2_lo[:, k, half(h)]) for k in range(KD)]).then_inc(product, 1)
                                if chunk is not None:
                                    if 2 * x_ + up == 3:
                                        gla_turn(chunk)
                                    if 2 * x_ + up == 5:
                                        gla_scores(chunk)
                    if chunk is not None:
                        gla_apply(chunk)
                    last = i * PAIRS + (b * FI * PAIRS + PAIRS - 1)
                    wd = [Place(nf, 4 + f, i, 2) for f in range(2)]
                    low_made(wd[1])
                    for q in range(OUTS):
                        k, h = q % KD, q // KD
                        po = Place(gf, 4 * HB + q, i, per)
                        if q == 0:
                            f_v.wait(pe, last - 1, "lo")
                        elif q == 1:
                            f_a.wait(pe, last, "silu")
                        elif q == 2:
                            f_v.wait(pe, last, "a")
                        else:
                            f_o.wait(pe, it, f"o{q - RING}")
                        if q == KD:
                            f_v.wait(pe, last, "lo")
                        parts(banks[po.slot][:], [(w_hi[:, wd[f].slot, k], w_lo[:, wd[f].slot, k], act_hi[:, f, half(h)],
                                                   act_lo[:, f, half(h)]) for f in range(2)]).then_inc(product, 1)
                        if q == RING and chunk is not None:
                            gla_norm(chunk)

                if b == 0:
                    with pe.Fori(0, 2 * CT) as i:
                        ffn(i, chunk=i + CH2)
                    with pe.Fori(0, FI - 2 * CT) as i:
                        ffn(i + 2 * CT)
                else:
                    with pe.Fori(0, FI) as i:
                        ffn(i)

                for h in range(HB):
                    for k in range(KD):
                        e_a.wait(pe, b, f"sq{h}{k}")
                        e_p.done(pe.matmul(side[:, 4 - h], ones[:], e_sq[:, k % 2], start=(k == 0), stop=(k == KD - 1)),
                                 f"ss{h}{k}")
                for t in range(TT):
                    e_a.wait(pe, b, f"b{t // (TT // HB)}{KD - 1}")
                    if t >= 2:
                        e_c.wait(pe, b, f"t{t - 2}")
                    for k in range(KD):
                        mm = pe.transpose(side[:, 2 * (t % 2) + k // 4, (k % 4) * P:(k % 4 + 1) * P],
                                          xacc[:, k, t * P:(t + 1) * P], ident[:])
                    e_p.done(mm, f"t{t}")


def masks():
    j = np.arange(C)[:, None]
    rows = []
    for s in LEVELS:
        i = np.arange(C).reshape(-1, 2 * s)[:, s:].reshape(1, -1)
        keep = (i // (2 * s) == j // (2 * s)) & (j % (2 * s) < s)
        rows.append(np.tile(keep, (1, 4)))
    rows.append(np.tile(np.eye(C, dtype=bool), (1, 4)))
    return np.concatenate(rows, axis=1).astype(np.float32)


_INS = ["x", "c", "w_ada", "b_ada", "g_mix", "w_in", "conv_w", "conv_b", "ln_g", "ln_b", "w_a2", "b_a2",
        "gla_norm_g", "w_out", "g_ffn", "w_ffn_in", "w_ffn_out", "w_ada_final", "b_ada_final", "g_final"]


def kernel(**inputs):
    import concourse.bacc as bacc
    from concourse.bass_utils import run_bass_kernel_spmd

    nc = bacc.Bacc("TRN2", target_bir_lowering=False, num_devices=1)
    arrays, args = {}, {}
    data = {name: np.ascontiguousarray(inputs[name]) for name in _INS}
    data["identity"] = np.eye(P, dtype=np.float32)
    data["level_masks"] = masks()
    for name, a in data.items():
        arrays[f"in_{name}"] = a
        args[name] = nc.dram_tensor(f"in_{name}", a.shape, mybir.dt.from_np(a.dtype), kind="ExternalInput").ap()
    shape = data["x"].shape
    o = nc.dram_tensor("out_0", shape, F32, kind="ExternalOutput").ap()
    block_kernel(nc, **args, out=o)
    r = run_bass_kernel_spmd(nc, [arrays], core_ids=[0])
    return np.asarray(r.results[0]["out_0"])
```

```python
from contextlib import ExitStack

import numpy as np

import concourse.bass as bass
from concourse import mybir

ALU = mybir.AluOpType
ACT = mybir.ActivationFunctionType
F32 = mybir.dt.float32
F32R = mybir.dt.float32r
U8 = mybir.dt.uint8

P = 128
EPS = 1e-6
RING = 3
NT = 512
GATE_TAU = 16.0
C = 128
LEVELS = [64, 32, 16, 8, 4, 2, 1]


class Line:

    def __init__(self, sem, names, ahead=0):
        self.sem, self.names, self.next, self.ahead = sem, list(names), 0, ahead

    def begin(self, engine):
        engine.sem_inc(self.sem, self.ahead * len(self.names))

    def value(self, unit, name):
        return unit * len(self.names) + (self.ahead * len(self.names) + self.names.index(name) + 1)

    def done(self, instruction, name):
        assert self.names[self.next] == name, (self.names[self.next], name)
        self.next = (self.next + 1) % len(self.names)
        instruction.then_inc(self.sem, 1)

    def wait(self, engine, unit, name):
        engine.wait_ge(self.sem, self.value(unit, name))


class Place:

    def __init__(self, base, step, loop, per_loop):
        self.slot = (base + step) % RING
        self.uses = loop * per_loop + (base + step) // RING
        self.number = loop * (RING * per_loop) + (base + step)


def tiles(engine, count, body):
    with engine.Fori(0, count // RING) as i:
        for s in range(RING):
            body(i, s)
    for s in range(count % RING):
        body(count // RING, s)


def block_kernel(nc, x, c, w_ada, b_ada, g_mix, w_in, conv_w, conv_b, ln_g, ln_b, w_a2, b_a2,
                 gla_norm_g, w_out, g_ffn, w_ffn_in, w_ffn_out, w_ada_final, b_ada_final, g_final,
                 identity, level_masks, out):
    T, D = x.shape[1], x.shape[2]
    KD = D // P
    TB = T // 2
    HB = TB // NT
    assert HB == 2
    G = T // NT
    TAPS, DC = conv_w.shape[1], conv_w.shape[2]
    CT = DC // P
    RANK, DK = w_a2.shape[1], w_a2.shape[2]
    KT = DK // P
    DV = gla_norm_g.shape[1]
    HV = D - DC
    VT = HV // P
    HEADS = HV // DV
    HEAD_K = DK // HEADS
    DF = w_ffn_out.shape[1]
    FT = DF // P
    CHUNKS = T // C
    PAD = TAPS - 1
    CV, CG, Q = 0, CT, 2 * CT
    K, V = Q + KT, Q + 2 * KT
    OG = V + VT
    AL = OG + VT
    NA = AL + 1
    assert NA % RING == 0
    assert DV == P and HEAD_K * 2 == P and KD == 8 and VT == HEADS and FT % 2 == 0 and TB % NT == 0

    x2 = x.rearrange("a t d -> (a t) d")
    out2 = out.rearrange("a t d -> (a t) d")
    wada = w_ada.rearrange("a k m -> (a k) m")
    win = w_in.rearrange("a (k p) m -> p (a k) m", p=P)
    wout = w_out.rearrange("a (k p) m -> p (a k) m", p=P)
    wfi = w_ffn_in.rearrange("a (k p) m -> p (a k) m", p=P)
    wfo = w_ffn_out.rearrange("a f m -> (a f) m")

    with ExitStack() as ctx:
        def sem(name):
            return ctx.enter_context(nc.semaphore(name))

        base = (nc.sbuf_base + 63) // 64 * 64
        room = nc.sbuf_usable_end - base - 64
        ctx.enter_context(nc.sbuf_tensor("arena", [P, room // 4], F32))

        def at(name, offset, shape, dtype=F32):
            return nc.alloc_sbuf_tensor_at(name, [P, *shape], dtype, offset=base + offset)

        KB = 1024
        ident = at("ident", 0, [P])
        ones = at("ones", 512, [P])
        pvec = at("pvec", 1024, [112])
        taps = at("taps", 1472, [TAPS * CT])
        modv = at("modv", 1984, [64])
        gain1 = at("gain1", 2240, [KD])
        gain2 = at("gain2", 2272, [KD])
        gainf = at("gainf", 2304, [KD])
        eps = at("eps", 2336, [1])
        cact = at("cact", 2368, [KD])
        ssq4 = at("ssq4", 2432, [4])
        rstd4 = at("rstd4", 2464, [4])
        a2 = at("a2", 2560, [DK])
        WO = 2560 + 4 * DK
        w_raw = at("w_raw", WO, [RING, KD, P])
        w_hi = at("w_hi", WO + 12 * KB, [RING, KD, P], F32R)
        w_lo = at("w_lo", WO + 24 * KB, [RING, KD, P], F32R)
        HA = WO + 36 * KB
        HB_ = HA + 64 * KB
        RO = HA + 128 * KB
        MASKS = (len(LEVELS) + 2) * HEADS * C // 2
        g_mask = at("g_mask", RO + 36 * KB + 512, [MASKS], U8)
        mask_f = at("mask_f", RO + 25 * KB, [MASKS])
        rows = at("rows", HA + 16 * KB, [2, P])
        assert RO + 36 * KB + 512 + MASKS <= room, (RO, room)
        m_raw = at("m_raw", RO, [4, KD * P])
        m_first = [at("m_first0", HA + 32 * KB, [KD, KD * P]), at("m_first1", HB_ + 32 * KB, [KD, KD * P])]
        m_acc = at("m_acc", RO + 16 * KB, [KD * P])
        m_acc1 = at("m_acc1", RO + 20 * KB, [KD * P])
        p_tmp = at("p_tmp", RO + 26 * KB, [4, NT])
        p_few = at("p_few", RO + 16 * KB, [2, NT])
        p_junk = at("p_junk", RO + 34 * KB + 512, [D], mybir.dt.bfloat16)
        xnat = [at("xnat0", HB_, [4, D]), at("xnat1", HB_ + 16 * KB, [4, D]), at("xnat2", RO, [4, D])]
        xnat.append(xnat[2])
        h_hi = [at("h0_hi", HA, [KD, TB], F32R), at("h1_hi", HB_, [KD, TB], F32R)]
        h_lo = [at("h0_lo", HA + 32 * KB, [KD, TB], F32R), at("h1_lo", HB_ + 32 * KB, [KD, TB], F32R)]
        stage = at("stage", RO + 20 * KB, [RING, NT])
        PW = PAD + NT + 2

        def conv_buffers(tag, o_in, o_acc):
            return (at("cv" + tag, o_in, [PW]), at("cg" + tag, o_in + 4 * PW, [PW]),
                    at("acca" + tag, o_acc, [NT]), at("accb" + tag, o_acc + 4 * NT, [NT]))

        conv_a = conv_buffers("_a", RO + 26 * KB, RO + 26 * KB + 8 * PW)
        conv_d = conv_buffers("_d", RO + 32 * KB, HA + 60 * KB)
        assert 2 * 4 * PW <= 4 * KB + 512
        offset = [HA]

        def gla(name, shape):
            t = at(name, offset[0], shape)
            offset[0] += 4 * int(np.prod(shape))
            return t

        g_lev = gla("g_lev", [len(LEVELS), KT * C])
        g_qk = gla("g_qk", [2 * KT, C])
        g_vt = gla("g_vt", [VT, C])
        g_vn = gla("g_vn", [VT * P])
        g_kn = gla("g_kn", [KT * P])
        g_la = gla("g_la", [KT, C])
        g_cum = gla("g_cum", [KT, C])
        g_ecum = gla("g_ecum", [KT, C])
        g_kd = gla("g_kd", [KT, C])
        g_rs = gla("g_rs", [HEADS * C])
        g_ql = gla("g_ql", [len(LEVELS), KT, 2, C // 2])
        g_qb = gla("g_qb", [KT, 2, C])
        g_qd = gla("g_qd", [KT, 2, C])
        g_st = gla("g_st", [HEADS, C])
        g_state = gla("g_state", [KT, DV])
        g_al = gla("g_al", [C])
        g_one = gla("g_one", [C])
        assert offset[0] <= HA + 36 * KB, offset
        y_hi = at("y_hi", HB_, [KD, TB], F32R)
        y_lo = at("y_lo", HB_ + 32 * KB, [KD, TB], F32R)
        h2_hi = at("h2_hi", HB_, [KD, TB], F32R)
        h2_lo = at("h2_lo", HB_ + 32 * KB, [KD, TB], F32R)
        xacc = at("xacc", RO, [KD, TB])
        def per_half(name, offsets, shape):
            return [at(f"{name}{b}", o, shape) for b, o in enumerate(offsets)]

        cin = per_half("cin", (HA + 36 * KB, HA), [HB, CT, NT])
        o_late = per_half("o_late", (HA, HA + 16 * KB), [VT, NT])
        og_late = per_half("og_late", (HA + 8 * KB, HA + 24 * KB), [VT, NT])
        o_early = at("o_early", HB_ + 48 * KB, [VT, TB])
        og_early = at("og_early", HB_ + 16 * KB, [VT, TB])
        oin = [[o_early[:, :, NT:TB], o_late[0][:]], [o_late[1][:], o_late[1][:]]]
        ogin = [[og_early[:, :, NT:TB], og_late[0][:]], [og_late[1][:], og_late[1][:]]]
        ln_rs = per_half("ln_rs", (HB_ + 44 * KB, HA + 32 * KB), [TB])
        ln_sq = per_half("ln_sq", (RO, RO + 32 * KB), [2, NT])
        xin = [[at(f"xin{b}{t}", HA + o * KB, [2, NT])[:] for t, o in enumerate(places)]
               for b, places in enumerate(((52, 56, 60), (44, 48, 60)))]
        x_fourth = at("x_fourth", HB_, [2, TB])[:, :, NT:TB]
        c_sq = per_half("c_sq", (HA + 36 * KB, HA), [2, NT])
        n_t = per_half("n_t", (HA + 40 * KB, HA + 4 * KB), [2, NT])
        n_rs = per_half("n_rs", (HA + 44 * KB, HA + 8 * KB), [TB])
        ssq = at("ssq", RO + 32 * KB, [NT])
        act_hi = at("act_hi", HA + 36 * KB, [2, TB], F32R)
        act_lo = at("act_lo", HA + 44 * KB, [2, TB], F32R)
        sil = at("sil", HA + 52 * KB, [2, NT])
        af = at("af", HA + 56 * KB, [2, NT])
        e_out = at("e_out", HA + 36 * KB, [2, D])
        e_sq = at("e_sq", HA + 52 * KB, [2, NT])
        e_rs = at("e_rs", HA + 56 * KB, [TB])

        banks = [ctx.enter_context(nc.psum_tensor(f"bank{b}", [P, NT], F32)) for b in range(RING)]
        side = ctx.enter_context(nc.psum_tensor("side", [P, 8 - RING, NT], F32))

        proj = nc.dram_tensor("proj", [NA, P, T], F32, kind="Internal").ap()
        convd = nc.dram_tensor("convd", [CT, P, T], F32, kind="Internal").ap()
        od = nc.dram_tensor("od", [VT, P, T], F32, kind="Internal").ap()

        names = [("b_ada", b_ada.rearrange("a (r p) -> (a r) p", p=P)),
                 ("b_fin", b_ada_final.rearrange("(r p) -> r p", p=P)),
                 ("g_mix", g_mix.rearrange("a (r p) -> (a r) p", p=P)),
                 ("g_ffn", g_ffn.rearrange("a (r p) -> (a r) p", p=P)),
                 ("g_fin", g_final.rearrange("(r p) -> r p", p=P)),
                 ("c", c.rearrange("a (r p) -> (a r) p", p=P)),
                 ("conv_b", conv_b.rearrange("a (r p) -> (a r) p", p=P)),
                 ("ln_g", ln_g.rearrange("a (r p) -> (a r) p", p=P)),
                 ("ln_b", ln_b.rearrange("a (r p) -> (a r) p", p=P)),
                 ("b_a2", b_a2.rearrange("a (r p) -> (a r) p", p=P)),
                 ("gla_g", gla_norm_g)]
        col, ncol = {}, 0
        for name, rows_of in names:
            col[name] = ncol
            ncol += rows_of.shape[0]
        assert ncol <= 112

        def vec(name, j=0):
            return pvec[:, col[name] + j:col[name] + j + 1]

        def mod(m, j):
            return modv[:, m * KD + j:m * KD + j + 1]

        def half(h):
            return slice(h * NT, (h + 1) * NT)

        def pairs(ap, s):
            return ap.rearrange("p (r w) -> p r w", w=2 * s)

        const_in = sem("const_in")
        mask_in = sem("mask_in")
        setup_p = Line(sem("setup_p"), ["rows", "taps"])
        setup_v = Line(sem("setup_v"), ["ones", "eps", "pvec", "taps", "mask", "pad"])
        setup_a = Line(sem("setup_a"), ["cact"])
        w_loaded = [sem(f"w_loaded{s}") for s in range(RING)]
        w_high = sem("w_high")
        w_low = sem("w_low")
        product = sem("product")
        SHIFTED = ["t0"] + [f"{s}{k - d}" for k in range(1, KD) for s, d in (("t", 0), ("lo", 1))] + [f"lo{KD - 1}"]
        m_first_loaded = [[sem(f"m_first_loaded{m}{q}") for q in range(4)] for m in range(2)]
        m_loaded = [sem(f"m_loaded{s}") for s in range(4)]
        mod_v = Line(sem("mod_v"), [f"k{k}" for k in range(KD)], ahead=1)
        vec_v = Line(sem("vec_v"), ["vec"])
        mod_p = Line(sem("mod_p"), ["sum"])
        gains_v = Line(sem("gains_v"), ["g1", "g2", "gf"])
        x_loaded = [sem(f"x_loaded{g}") for g in range(G)]
        prep_a = Line(sem("prep_a"), [f"sq{t}" for t in range(4)] + ["ln", "rstd"] + [f"xn{t}" for t in range(4)]
                      + ["t0"] + [f"{s}{k - d}" for k in range(1, KD) for s, d in (("t", 0), ("hi", 1))]
                      + [f"hi{KD - 1}"], ahead=1)
        prep_v = Line(sem("prep_v"), [f"lo{k}" for k in range(KD)], ahead=1)
        prep_p = Line(sem("prep_p"), [f"k{k}" for k in range(KD)])
        staged = Line(sem("staged"), ["copy"], ahead=RING)
        stored = [sem(f"stored{b}") for b in range(RING)]
        cv_loaded = sem("cv_loaded")
        cv_a = Line(sem("cv_a"), ["sig"])
        cv_v = Line(sem("cv_v"), ["u"] + [f"tap{k}" for k in range(TAPS)] + ["sum"], ahead=1)
        cv_stored = sem("cv_stored")
        picks = sem("picks")
        pool_steps = sem("pool_steps")
        g_zero = Line(sem("g_zero"), ["st", "state", "qd", "qb", "ql", "one"])
        g_loaded = sem("g_loaded")
        g_stored = sem("g_stored")
        L = range(len(LEVELS))
        gla_v = Line(sem("gla_v"), ["min", "la", "cum0", "cum1"] + [f"sub{l}" for l in L] + ["qd0", "qd1", "kd"]
                     + [f"{s}{l}" for l in L for s in ("qa", "qb", "k")]
                     + [f"pick{l}" for l in L] + ["pickd", "st0", "st1", "gain", "on"], ahead=1)
        gla_a = Line(sem("gla_a"), ["zb0", "zb1", "zabs", "zexp", "zln", "qb0", "qb1", "abs", "ecum",
                                    "kdec0", "kdec1", "exp", "vn", "kn", "sq", "ln", "rstd"])
        gla_p = Line(sem("gla_p"), ["z", "vn", "kn", "lev", "diag", "o", "state", "ss"], ahead=1)
        c_loaded = [sem(f"c_loaded{h}") for h in range(HB)]
        o_loaded = sem("o_loaded")
        x2_loaded = [sem(f"x2_loaded{s}") for s in range(4)]
        ln_p = Line(sem("ln_p"), [f"mean{h}" for h in range(HB)] + [f"v{h}{j}" for h in range(HB) for j in range(CT)])
        ln_a = Line(sem("ln_a"), [f"q{j}-{h}" for h in range(HB) for j in range(CT)]
                    + [f"{s}{h}" for s in ("ln", "rstd") for h in range(HB)])
        ln_v = Line(sem("ln_v"), [f"d{h}{j}" for h in range(HB) for j in range(CT)])
        y_a = Line(sem("y_a"), [f"{s}{h}{j}" for h in range(HB) for s in ("y", "hi") for j in range(CT)])
        y_v = Line(sem("y_v"), [f"{s}{h}{j}" for h in range(HB) for s in ("n", "lo") for j in range(CT)])
        og_a = Line(sem("og_a"), [f"{s}{h}" for h in range(HB) for s in ("s", "hi")])
        og_v = Line(sem("og_v"), [f"{s}{h}" for h in range(HB) for s in ("m", "lo")])
        TT = TB // P
        xt_p = Line(sem("xt_p"), [f"t{t}" for t in range(TT)])
        xt_a = Line(sem("xt_a"), [f"t{t}" for t in range(TT)])
        res_v = Line(sem("res_v"), ["x", "ss"], ahead=RING)
        res_a = Line(sem("res_a"), ["sq"])
        n_p = Line(sem("n_p"), [f"ss{h}" for h in range(HB)])
        n_a = Line(sem("n_a"), [f"{s}{h}" for h in range(HB) for s in ["ln", "rstd"] + [f"hi{k}-" for k in range(KD)]])
        n_v = Line(sem("n_v"), [f"{s}-{h}" for h in range(HB) for s in SHIFTED])
        f_a = Line(sem("f_a"), ["silu", "hi"], ahead=2)
        f_v = Line(sem("f_v"), ["a", "lo"], ahead=2)
        OUTS = KD * HB
        f_o = Line(sem("f_o"), [f"o{q}" for q in range(OUTS)], ahead=1)
        e_a = Line(sem("e_a"), [f"sq0{k}" for k in range(KD)] + ["ln0", "rstd0"]
                   + [f"sq1{k}" for k in range(KD)] + ["ln1", "rstd1"]
                   + [f"b{k}" for k in range(KD)])
        e_v = Line(sem("e_v"), [f"t{h}{k}" for h in range(HB) for k in range(KD)] + [f"b{k}" for k in range(KD)])
        e_p = Line(sem("e_p"), [f"ss{h}{k}" for h in range(HB) for k in range(KD)] + [f"t{t}" for t in range(TT)])
        e_c = Line(sem("e_c"), [f"t{t}" for t in range(TT)])
        out_stored = [sem(f"out_stored{s}") for s in range(2)]

        NAG = NA * HB
        FI = FT // 2
        NC0, GC0 = 2 * NA, 2 * NAG
        NH, GH = KD * HB + 6 * FI, KD * HB + (4 * HB + OUTS) * FI
        PAIRS = 2 * HB
        AI = NA // RING
        CH2 = CHUNKS // 2
        D_T0 = 8

        SPLIT = KD * HB

        def a_group(it, s, h):
            if isinstance(it, int) and it == 0:
                return h * RING + s
            return s * HB + h

        def a_order(it):
            if isinstance(it, int) and it == 0:
                return [(s, h) for h in range(HB) for s in range(RING)]
            return [(s, h) for s in range(RING) for h in range(HB)]

        PREP_AT = {1: 2, 2: 2, 3: 2}

        X_SLOT = (0, 1, 2, 3, 0, 1, 2, 0)

        def x_slot(b, t):
            return (xin[b] + [x_fourth])[X_SLOT[t]]

        def prep_slots(g):
            return (p_few, 2) if g == 2 else (p_tmp, 4)

        def gla_slots(it):
            return (3, 4, 5, 5) if isinstance(it, int) and it == 0 else (0, 2, 3, 5)

        def a_place(b, it, s, h):
            return Place(b * NAG, a_group(it, s, h), it, NAG // AI // RING)

        def a_tile(it, s):
            t = it * RING + (s - 1)
            if isinstance(it, int) and it * RING + s == 0:
                return AL, (AL - 1) * P + RANK
            return t, t * P

        def stat(b, h):
            return side[:, 3 + h] if b else banks[h][:]

        block = ctx.enter_context(nc.Block())

        @block.sync
        def _(sp):
            def load(place, source):
                sp.wait_ge(w_low, place.number + 1)
                sp.dma_start(w_raw[:, place.slot], source).then_inc(w_loaded[place.slot], 16)

            def mod_first(m):
                for q in range(4):
                    sp.dma_start(m_first[m][:, 2 * q:2 * q + 2],
                                 wada[2 * q * P:(2 * q + 2) * P, m * D:(m + 1) * D].rearrange("(k p) d -> p k d", p=P)
                                 ).then_inc(m_first_loaded[m][q], 16)

            def in_proj(b, it, m=None, source=None):
                for s in range(RING):
                    if m is not None and s == 2:
                        mod_rows(m, source, 0, 4)
                    load(Place(b * NA, s, it, 1), win[:, :, bass.ds(a_tile(it, s)[1], P)])
                if m is not None:
                    mod_rows(m, source, 4, KD)

            def mod_rows(m, source, k0, k1):
                for k in range(k0, k1):
                    mod_v.wait(sp, m if k >= 4 else m - 1, f"k{k - 4 if k >= 4 else k + 4}")
                    sp.dma_start(m_raw[:, k % 4], source[k * P:(k + 1) * P, :]).then_inc(m_loaded[k % 4], 16)

            sp.wait_ge(const_in, 16 * (1 + len(names) + 2))
            mod_first(0)
            sp.dma_start(xnat[0][:], x2[0:NT, :].rearrange("(t p) d -> p t d", p=P)).then_inc(x_loaded[0], 16)
            mod_first(1)
            in_proj(0, 0)
            sp.dma_start(xnat[1][:], x2[NT:2 * NT, :].rearrange("(t p) d -> p t d", p=P)).then_inc(x_loaded[1], 16)
            with sp.Fori(0, 4) as j:
                in_proj(0, j + 1, j + 2, wada[:, bass.ds(j * D + 2 * D, D)])
            with sp.Fori(0, AI - 5) as j:
                in_proj(0, j + 5, j + 6, w_ada_final[:, bass.ds(j * D, D)])
            mod_v.wait(sp, 7, f"k{KD - 1}")
            sp.dma_start(xnat[2][:], x2[2 * NT:3 * NT, :].rearrange("(t p) d -> p t d", p=P)).then_inc(x_loaded[2], 16)
            in_proj(1, 0)
            with sp.Fori(0, AI - 1) as j:
                in_proj(1, j + 1)
            for b in range(2):
                n0 = NC0 + b * NH
                for h in range(HB):
                    tiles(sp, KD, lambda i, s: load(Place(n0 + h * KD, s, i, 1), wout[:, :, bass.ds((i * RING + s) * P, P)]))
                nf = n0 + SPLIT
                with sp.Fori(0, FI) as i:
                    for f in range(2):
                        for u in range(2):
                            load(Place(nf, 2 * f + u, i, 2), wfi[:, :, bass.ds(i * (2 * P) + (f * P + u * DF), P)])
                    for f in range(2):
                        load(Place(nf, 4 + f, i, 2),
                             wfo[bass.ds(i * (2 * P) + f * P, P), :].rearrange("p (k m) -> p k m", k=KD))

        @block.gpsimd
        def _(pool):
            def waited():
                pool.sem_inc(pool_steps, 1)

            def conv_load(bufs, unit, j, h):
                cv_v.wait(pool, unit - 1, "sum")
                waited()
                halo = PAD if h else 0
                for buf, t0 in ((bufs[0], CV), (bufs[1], CG)):
                    pool.dma_start(buf[:, PAD - halo:PAD + NT],
                                   proj[bass.ds(j + t0, 1), :, h * NT - halo:(h + 1) * NT]
                                   .rearrange("a p t -> p (a t)")).then_inc(cv_loaded, 16)

            def conv_store(bufs, unit, j, h):
                cv_v.wait(pool, unit, "sum")
                waited()
                pool.dma_start(convd[bass.ds(j, 1), :, h * NT:(h + 1) * NT].rearrange("a p t -> p (a t)"),
                               bufs[2][:]).then_inc(cv_stored, 16)

            def gla_load(n):
                gla_p.wait(pool, n - 1, "diag")
                gla_v.wait(pool, n - 1, f"k{L[-1]}")
                waited()
                tok = bass.ds(n * C, C)
                pool.dma_start(g_al[0:RANK, :], proj[AL, P - RANK:P, tok]).then_inc(g_loaded, 16)
                pool.dma_start(g_qk[:], proj[Q:Q + 2 * KT, :, tok].rearrange("a p t -> p a t")).then_inc(g_loaded, 16)
                pool.dma_start(g_vt[:], proj[V:V + VT, :, tok].rearrange("a p t -> p a t")).then_inc(g_loaded, 16)

            def gla_store(n):
                gla_v.wait(pool, n, "on")
                waited()
                pool.dma_start(od[:, :, bass.ds(n * C, C)].rearrange("a p t -> p a t"),
                               g_rs[:].rearrange("p (h t) -> p h t", h=HEADS)).then_inc(g_stored, 16)

            def tokens(b, h):
                return slice(b * TB + h * NT, b * TB + (h + 1) * NT)

            def cin_load(b, h):
                pool.wait_ge(cv_stored, 16 * (CT + 1 if b == h == 0 else CT * (2 * b + h + 1)))
                pool.dma_start(cin[b][:, h], convd[:, :, tokens(b, h)].rearrange("a p t -> p a t")).then_inc(c_loaded[h], 16)

            def og_load(b, h):
                if b and h:
                    og_v.wait(pool, b, f"lo{h - 1}")
                pool.dma_start(oin[b][h], od[:, :, tokens(b, h)].rearrange("a p t -> p a t")).then_inc(o_loaded, 16)
                pool.dma_start(ogin[b][h], proj[OG:OG + VT, :, tokens(b, h)].rearrange("a p t -> p a t")).then_inc(o_loaded, 16)

            def x_load(b, t):
                before = [u for u in range(t) if X_SLOT[u] == X_SLOT[t]]
                if before:
                    xt_p.wait(pool, b, f"t{before[-1]}")
                pool.dma_start(x_slot(b, t), x2[b * TB + t * P:b * TB + (t + 1) * P, :].rearrange("p (a d) -> p a d", a=2)
                               ).then_inc(x2_loaded[X_SLOT[t]], 16)

            def results(b):
                for t in range(TT):
                    e_c.wait(pool, b, f"t{t}")
                    pool.dma_start(out2[b * TB + t * P:b * TB + (t + 1) * P, :], e_out[:, t % 2]).then_inc(out_stored[t % 2], 16)

            with pool.Fori(0, CT) as j:
                for s in range(RING):
                    pool.wait_ge(stored[s], j * 32 + (16 + 2 * 32))
                conv_load(conv_a, j, j, 0)
                conv_store(conv_a, j, j, 0)
            conv_load(conv_a, CT, 0, 1)
            prep_p.wait(pool, 2, f"k{KD - 1}")
            pool.dma_start(xnat[3][:], x2[3 * NT:4 * NT, :].rearrange("(t p) d -> p t d", p=P)).then_inc(x_loaded[3], 16)

            conv_store(conv_a, CT, 0, 1)

            for s in range(RING):
                pool.wait_ge(stored[s], 16 + NAG // RING * 16)
            pool.wait_ge(product, NAG)
            gla_load(0)
            gla_load(1)
            gla_store(0)
            prep_v.wait(pool, 3, f"lo{KD - 1}")
            cin_load(0, 0)
            for t in range(3):
                x_load(0, t)
            with pool.Fori(0, CT - 1) as j:
                n, unit, tile = j * 2 + 1, j + (CT + 1), j + 1
                conv_load(conv_a, unit, tile, 1)
                gla_load(n + 1)
                gla_store(n)
                gla_load(n + 2)
                conv_store(conv_a, unit, tile, 1)
                gla_store(n + 1)
            cin_load(0, 1)
            pool.wait_ge(product, 2 * NAG)
            for s in range(RING):
                pool.wait_ge(stored[s], 16 + 2 * NAG // RING * 16)
            pool.wait_ge(g_stored, 16 * (CH2 - 1))
            og_load(0, 0)
            x_load(0, 3)
            gla_store(CH2 - 1)
            pool.wait_ge(g_stored, 16 * CH2)
            og_load(0, 1)
            for t in range(4, TT):
                x_load(0, t)
            og_v.wait(pool, 0, f"lo{HB - 1}")
            gla_load(CH2)

            n_p.wait(pool, 0, f"ss{HB - 1}")
            for h, loops in ((2, CT), (3, CT - 1)):
                with pool.Fori(0, loops) as j:
                    n, unit = j + (CH2 + (h - 2) * CT), j + h * CT
                    conv_load(conv_d, unit, j, h)
                    gla_load(n + 1)
                    conv_store(conv_d, unit, j, h)
                    gla_store(n)
            conv_load(conv_d, 4 * CT - 1, CT - 1, 3)
            conv_store(conv_d, 4 * CT - 1, CT - 1, 3)
            gla_store(CHUNKS - 1)
            pool.wait_ge(g_stored, 16 * CHUNKS)
            for h in range(HB):
                cin_load(1, h)
            og_load(1, 0)
            pool.wait_ge(product, GC0 + GH)
            for t in range(4):
                x_load(1, t)
            og_load(1, 1)
            results(0)
            for t in range(4, TT):
                x_load(1, t)
            results(1)
            for s in range(2):
                pool.wait_ge(out_stored[s], 16 * TT)

        @block.scalar
        def _(act):
            for line in (prep_a, staged, f_a):
                line.begin(act)
            for s in stored:
                act.sem_inc(s, 16)

            def high(place, used):
                act.wait_ge(w_loaded[place.slot], place.uses * 16 + 16)
                if used is not None:
                    act.wait_ge(product, used)
                act.activation(w_hi[:, place.slot], w_raw[:, place.slot], ACT.Copy).then_inc(w_high, 1)

            def prep_rstd(g):
                act.wait_ge(x_loaded[g], 16)
                for t in range(4):
                    prep_a.wait(act, g - 1 if t == 0 else g, "xn3" if t == 0 else f"sq{t - 1}")
                    prep_a.done(act.activation(p_junk[:], xnat[g][:, t], ACT.Square, accum_out=ssq4[:, t:t + 1]), f"sq{t}")
                prep_a.wait(act, g, "sq3")
                prep_a.done(act.activation(rstd4[:], ssq4[:], ACT.Ln, scale=1.0 / D, bias=eps[:]), "ln")
                prep_a.wait(act, g, "ln")
                prep_a.done(act.activation(rstd4[:], rstd4[:], ACT.Exp, scale=-0.5), "rstd")

            def prep_rows(g):
                prep_a.wait(act, g, "rstd")
                for t in range(4):
                    prep_a.done(act.activation(xnat[g][:, t], xnat[g][:, t], ACT.Copy, scale=rstd4[:, t:t + 1]), f"xn{t}")

            def prep_high(g, k0, k1):
                shifted, slots = prep_slots(g)

                def hi(k):
                    prep_a.wait(act, g, f"t{k}")
                    prep_a.done(act.activation(h_hi[g // 2][:, k, half(g % 2)], shifted[:, k % slots], ACT.Copy), f"hi{k}")

                if g == 0 and k0 == 0:
                    gains_v.wait(act, 0, "g1")
                    setup_v.wait(act, 0, "mask")
                if g == 2 and k0 == 0:
                    vec_v.wait(act, 7, "vec")
                if g == 3 and k0 == 0:
                    act.wait_ge(cv_stored, 16 * (CT + 1))
                for k in range(k0, k1):
                    prep_p.wait(act, g, f"k{k}")
                    prep_v.wait(act, g if k >= slots else g - 1, f"lo{(k - slots) % KD}")
                    prep_a.wait(act, g if k >= slots else g - 1, f"hi{(k - slots) % KD}")
                    prep_a.done(act.activation(shifted[:, k % slots], side[:, k % 4], ACT.Identity, scale=gain1[:, k:k + 1],
                                               bias=mod(0, k)), f"t{k}")
                    if k:
                        hi(k - 1)
                if k1 == KD:
                    hi(KD - 1)

            def sigmoid(bufs, unit, h):
                act.wait_ge(cv_loaded, unit * 32 + 32)
                part = slice(0 if h else PAD, PAD + NT)
                cv_a.done(act.activation(bufs[1][:, part], bufs[1][:, part], ACT.Sigmoid), "sig")

            def gla_gate(n):
                if isinstance(n, int) and n == 0:
                    g_zero.wait(act, 0, "one")
                for f in range(KT):
                    if f == 0:
                        gla_p.wait(act, n, "z")
                    gla_a.done(act.activation(g_kd[:, f], side[:, 3, f * C:(f + 1) * C], ACT.Identity,
                                              bias=vec("b_a2", f)), f"zb{f}")
                gla_a.wait(act, n, f"zb{KT - 1}")
                gla_v.wait(act, n - 1, "st1")
                gla_a.done(act.activation(g_ecum[:], g_kd[:], ACT.Abs), "zabs")
                gla_a.wait(act, n, "zabs")
                gla_a.done(act.activation(g_ecum[:], g_ecum[:], ACT.Exp, scale=-1.0), "zexp")
                gla_a.wait(act, n, "zexp")
                gla_a.done(act.activation(g_ecum[:], g_ecum[:], ACT.Ln, bias=ones[:, 0:1]), "zln")

            def gla_decays(n):
                act.wait_ge(g_loaded, n * 48 + 48)
                for e in range(2):
                    r = slice(e * HEAD_K, (e + 1) * HEAD_K)
                    gla_a.done(act.activation(g_qb[r, :, e], g_qk[r, 0:KT], ACT.Copy), f"qb{e}")
                gla_v.wait(act, n, f"sub{L[-1]}")
                gla_a.done(act.activation(g_lev[:], g_lev[:], ACT.Abs), "abs")
                gla_a.done(act.activation(g_ecum[:], g_cum[:], ACT.Exp), "ecum")
                for f in range(KT):
                    gla_a.done(act.activation(g_kd[:, f], g_cum[:, f], ACT.Exp, scale=-1.0,
                                              bias=g_cum[:, f, C - 1:C]), f"kdec{f}")
                gla_a.wait(act, n, "abs")
                gla_a.done(act.activation(g_lev[:], g_lev[:], ACT.Exp, scale=-1.0), "exp")

            def gla_turned(n):
                gla_p.wait(act, n, "vn")
                gla_a.done(act.activation(g_vn[:], side[:, 0], ACT.Copy), "vn")
                gla_p.wait(act, n, "kn")
                gla_a.done(act.activation(g_kn[:], side[:, 1, 0:KT * P], ACT.Copy), "kn")

            def gla_squares(n):
                gla_p.wait(act, n, "o")
                act.wait_ge(g_stored, n * 16)
                gla_a.done(act.activation(g_rs[:], side[:, 0], ACT.Square), "sq")

            def gla_rstd(n):
                gla_p.wait(act, n, "ss")
                gla_a.done(act.activation(g_rs[:], side[:, 2], ACT.Ln, scale=1.0 / (DV * HEAD_K), bias=eps[:]), "ln")
                gla_a.wait(act, n, "ln")
                gla_a.done(act.activation(g_rs[:], g_rs[:], ACT.Exp, scale=-0.5), "rstd")

            def in_proj(b, it, chunk=None, conv=None, prep=None):
                for n, (s, h) in enumerate(a_order(it)):
                    if prep is not None:
                        if n == PREP_AT[prep] - 2:
                            prep_rstd(prep)
                        if n == PREP_AT[prep] - 1:
                            prep_rows(prep)
                        if n == PREP_AT[prep]:
                            prep_high(prep, 0, 4)
                        if n == PREP_AT[prep] + 1:
                            prep_high(prep, 4, KD)
                    if n == gla_slots(it)[0] and chunk is not None:
                        gla_gate(chunk)
                    if n == (4 if prep else 0) and conv is not None and chunk is None:
                        sigmoid(conv_a, *conv)
                    p = a_place(b, it, s, h)
                    act.wait_ge(product, p.number + 1)
                    act.wait_ge(stored[p.slot], p.uses * 16 + 16)
                    staged.done(act.activation(stage[:, p.slot], banks[p.slot][:], ACT.Copy), "copy")
                    if h == HB - 1:
                        high(Place(b * NA + RING, s, it, 1), p.number + 1)
                    staged.wait(act, p.number, "copy")
                    act.dma_start(proj[bass.ds(a_tile(it, s)[0], 1), :, b * TB + h * NT:b * TB + (h + 1) * NT]
                                  .rearrange("a p t -> p (a t)"), stage[:, p.slot]).then_inc(stored[p.slot], 16)
                    if chunk is not None:
                        if n == gla_slots(it)[0]:
                            gla_decays(chunk)
                        if n == 0 and conv is not None:
                            sigmoid(conv_a, *conv)
                        if n == gla_slots(it)[1]:
                            gla_turned(chunk)
                        if n == gla_slots(it)[3]:
                            gla_squares(chunk)
                            gla_rstd(chunk)

            act.dma_start(ident[:], identity).then_inc(const_in, 16)
            for name, rows_of in names:
                n = rows_of.shape[0]
                act.dma_start(rows[col[name]:col[name] + n, 0, :], rows_of).then_inc(const_in, 16)
            act.dma_start(rows[0:TAPS * CT, 1, :], conv_w.rearrange("a t (j p) -> (a t j) p", p=P)).then_inc(const_in, 16)
            act.dma_start(a2[0:RANK, :], w_a2.rearrange("a r d -> (a r) d")).then_inc(const_in, 16)
            act.dma_start(mask_f[:], level_masks).then_inc(mask_in, 16)
            setup_v.wait(act, 0, "pvec")
            setup_a.done(act.activation(cact[:], pvec[:, col["c"]:col["c"] + KD], ACT.Silu), "cact")
            prep_rstd(0)
            prep_rows(0)
            for s in range(RING):
                high(Place(0, s, 0, 1), None)
            prep_high(0, 0, KD)
            in_proj(0, 0, prep=1)
            in_proj(0, 1)
            with act.Fori(0, CT) as j:
                in_proj(0, j + 2, conv=(j, 0))
            in_proj(0, AI - 1, prep=2, conv=(CT, 1))
            in_proj(1, 0, prep=3, chunk=0)
            with act.Fori(0, CT - 1) as j:
                n = j * 2 + 1
                in_proj(1, n, chunk=n, conv=(j + (CT + 1), 1))
                in_proj(1, n + 1, chunk=n + 1)
            def ln_stat(b):
                for h in range(HB):
                    for j in range(CT):
                        ln_v.wait(act, b, f"d{h}{j}")
                        if h or j >= 2:
                            ln_p.wait(act, b, f"v{h}{j - 2}" if j >= 2 else f"v{h - 1}{CT - 2 + j}")
                        ln_a.done(act.activation(ln_sq[b][:, j % 2], cin[b][:, h, j], ACT.Square), f"q{j}-{h}")
                for h in range(HB):
                    ln_p.wait(act, b, f"v{h}{CT - 1}")
                    ln_a.done(act.activation(ln_rs[b][:, half(h)], stat(b, h), ACT.Ln, scale=1.0 / DC, bias=eps[:]), f"ln{h}")
                for h in range(HB):
                    ln_a.wait(act, b, f"ln{h}")
                    ln_a.done(act.activation(ln_rs[b][:, half(h)], ln_rs[b][:, half(h)], ACT.Exp, scale=-0.5), f"rstd{h}")

            def silu_gate(b, h):
                act.wait_ge(o_loaded, 32 * (b * HB + h + 1))
                og_a.done(act.activation(ogin[b][h], ogin[b][h], ACT.Silu), f"s{h}")

            def gated_high(b, h):
                og_v.wait(act, b, f"m{h}")
                og_a.done(act.activation(y_hi[:, CT:KD, half(h)], oin[b][h], ACT.Copy), f"hi{h}")

            def y_silu(b, h, j):
                y_v.wait(act, b, f"n{h}{j}")
                y_a.done(act.activation(cin[b][:, h, j], cin[b][:, h, j], ACT.Silu, scale=vec("ln_g", j),
                                        bias=vec("ln_b", j)), f"y{h}{j}")

            def y_high(b, h, j):
                y_a.wait(act, b, f"y{h}{j}")
                y_a.done(act.activation(y_hi[:, j, half(h)], cin[b][:, h, j], ACT.Copy), f"hi{h}{j}")

            def turned(b, t):
                xt_p.wait(act, b, f"t{t}")
                w = 2 * (t % 2)
                xt_a.done(act.activation(xacc[:, :, t * P:(t + 1) * P],
                                         side[:, w:w + 2].rearrange("p a (k t) -> p (a k) t", t=P), ACT.Copy), f"t{t}")

            def norm_rstd(b, h):
                n_p.wait(act, b, f"ss{h}")
                n_a.done(act.activation(n_rs[b][:, half(h)], side[:, 4], ACT.Ln, scale=1.0 / D, bias=eps[:]), f"ln{h}")
                n_a.wait(act, b, f"ln{h}")
                n_a.done(act.activation(n_rs[b][:, half(h)], n_rs[b][:, half(h)], ACT.Exp, scale=-0.5), f"rstd{h}")

            def norm_high(b, h, k):
                n_v.wait(act, b, f"t{k}-{h}")
                n_a.done(act.activation(h2_hi[:, k, half(h)], n_t[b][:, k % 2], ACT.Identity, bias=mod(3, k)), f"hi{k}-{h}")

            def beside_projection(b, h, s):
                if h == 0:
                    if s == 0:
                        silu_gate(b, 1)
                    if s in (1, 2):
                        y_silu(b, 1, 2 * s - 2)
                        y_silu(b, 1, 2 * s - 1)
                    if s in (3, 4):
                        y_high(b, 1, 2 * s - 6)
                        y_high(b, 1, 2 * s - 5)
                    if s == 4:
                        gated_high(b, 1)
                    if 3 <= s < 7:
                        turned(b, s + 1)
                elif s == 0:
                    norm_rstd(b, 0)
                elif s >= 2:
                    norm_high(b, 0, s - 2)

            def final_squares(b, h):
                for k in range(KD):
                    f_o.wait(act, (b + 1) * FI - 1, f"o{h * KD + k}")
                    if h or k >= 2:
                        e_p.wait(act, b, f"ss{h}{k - 2}" if k >= 2 else f"ss{h - 1}{KD - 2 + k}")
                    e_a.done(act.activation(e_sq[:, k % 2], xacc[:, k, half(h)], ACT.Square), f"sq{h}{k}")

            def final_rstd(b, h):
                e_p.wait(act, b, f"ss{h}{KD - 1}")
                e_a.done(act.activation(e_rs[:, half(h)], side[:, 4], ACT.Ln, scale=1.0 / D, bias=eps[:]), f"ln{h}")
                e_a.wait(act, b, f"ln{h}")
                e_a.done(act.activation(e_rs[:, half(h)], e_rs[:, half(h)], ACT.Exp, scale=-0.5), f"rstd{h}")

            def final_shift(b):
                for k in range(KD):
                    e_v.wait(act, b, f"t0{k}")
                    e_a.done(act.activation(xacc[:, k, half(0)], xacc[:, k, half(0)], ACT.Identity, bias=mod(6, k)), f"b{k}")

            def final_out(b, h):
                for t in range(h * NT // P, (h + 1) * NT // P):
                    e_p.wait(act, b, f"t{t}")
                    if b or t >= 2:
                        act.wait_ge(out_stored[t % 2], 16 * ((b * TT + t) // 2))
                    e_c.done(act.activation(e_out[:, t % 2], side[:, 2 * (t % 2):2 * (t % 2) + 2], ACT.Copy), f"t{t}")

            def final(b):
                final_rstd(b, 0)
                final_squares(b, 1)
                final_rstd(b, 1)
                final_shift(b)
                for h in range(HB):
                    final_out(b, h)

            for b in range(2):
                n0, g0 = NC0 + b * NH, GC0 + b * GH
                if b == 0:
                    gla_gate(CH2 - 1)
                    gla_decays(CH2 - 1)
                    ln_stat(b)
                    gla_turned(CH2 - 1)
                    silu_gate(b, 0)
                    for j in range(CT):
                        y_silu(b, 0, j)
                    for j in range(CT):
                        y_high(b, 0, j)
                    gated_high(b, 0)
                    gla_squares(CH2 - 1)
                    gla_rstd(CH2 - 1)
                else:
                    final(0)
                for t in range(4):
                    turned(b, t)

                for h in range(HB):
                    for s in range(KD):
                        u = b * SPLIT + h * KD + s
                        high(Place(n0 + RING + h * KD + s, 0, 0, 1), g0 + h * KD + s + 1)
                        res_v.wait(act, u - 2, "ss")
                        res_v.wait(act, u, "x")
                        res_a.done(act.activation(c_sq[b][:, s % 2], xacc[:, s, half(h)], ACT.Square), "sq")
                        beside_projection(b, h, s)
                for k in range(KD - 2, KD):
                    norm_high(b, 0, k)
                norm_rstd(b, 1)
                for k in range(KD):
                    norm_high(b, 1, k)

                nf, gf = n0 + SPLIT, g0 + KD * HB

                def ffn(i, last=False, chunk=None, conv=None, next_y=False):
                    i0 = i * (4 * HB + OUTS) + gf
                    if chunk is not None:
                        gla_gate(chunk)
                    for f in range(2):
                        for h in range(HB):
                            u = i * PAIRS + (b * FI * PAIRS + f * HB + h)
                            pg = Place(gf, 2 * (f * HB + h), i, (4 * HB + OUTS) // RING)
                            act.wait_ge(product, pg.number + 1)
                            f_v.wait(act, u - 2, "a")
                            f_a.done(act.activation(sil[:, h], banks[pg.slot][:], ACT.Silu), "silu")
                            if h == HB - 1:
                                high(Place(nf + RING, 2 * f, i, 2), i0 + (f * 2 * HB + 2 * HB - 1))
                            f_v.wait(act, u, "a")
                            f_a.done(act.activation(act_hi[:, f, half(h)], af[:, h], ACT.Copy), "hi")
                            if (f, h) == (0, 0) and chunk is not None:
                                gla_decays(chunk)
                            if (f, h) == (1, 0) and next_y:
                                for j in range(CT):
                                    y_silu(1, 0, j)
                        if f == 0:
                            high(Place(nf + RING, 1, i, 2), i0 + 2 * HB)
                            if chunk is not None:
                                gla_turned(chunk)
                                sigmoid(conv_d, *conv)
                            if next_y:
                                ln_stat(1)
                                silu_gate(1, 0)
                    if not last:
                        high(Place(nf + RING, 3, i, 2), i0 + 4 * HB)
                    if chunk is not None:
                        gla_squares(chunk)
                        gla_rstd(chunk)
                    if next_y:
                        for j in range(CT):
                            y_high(1, 0, j)
                        gated_high(1, 0)
                    if isinstance(i, int):
                        final_squares(b, 0)
                    if not last:
                        high(Place(nf + RING, 4, i, 2), i0 + (4 * HB + OUTS))
                        high(Place(nf + RING, 5, i, 2), i0 + (4 * HB + OUTS))

                if b == 0:
                    for h in range(2, 4):
                        with act.Fori(0, CT) as j:
                            ffn(j + (h - 2) * CT, chunk=j + (CH2 + (h - 2) * CT), conv=(j + h * CT, h))
                    with act.Fori(0, FI - 1 - 2 * CT) as j:
                        ffn(j + 2 * CT)
                    ffn(FI - 1, next_y=True)
                else:
                    with act.Fori(0, FI - 1) as i:
                        ffn(i)
                    ffn(FI - 1, last=True)
            final(1)

        @block.vector
        def _(dve):
            dve.sem_inc(w_low, RING)
            for line in (mod_v, prep_v, cv_v, gla_v, res_v, f_v, f_o):
                line.begin(dve)

            def low(place):
                dve.wait_ge(w_high, place.number + 1)
                dve.tensor_tensor(w_lo[:, place.slot], w_raw[:, place.slot], w_hi[:, place.slot].bitcast(F32),
                                  ALU.subtract).then_inc(w_low, 1)

            def mod_sum(m, acc=None):
                acc = m_acc if acc is None else acc
                for k in range(KD):
                    if isinstance(m, int) and m < 2:
                        dve.wait_ge(m_first_loaded[m][k // 2], 16)
                        raw = m_first[m][:, k]
                    else:
                        dve.wait_ge(m_loaded[k % 4], (m - 2) * 32 + 16 * (k // 4 + 1))
                        raw = m_raw[:, k % 4]
                    if k == 0:
                        ins = dve.tensor_scalar(acc[:], raw, cact[:, 0:1], None, ALU.mult)
                    else:
                        mod_v.wait(dve, m, f"k{k - 1}")
                        ins = dve.scalar_tensor_tensor(acc[:], raw, cact[:, k:k + 1], acc[:], ALU.mult, ALU.add)
                    mod_v.done(ins, f"k{k}")

            def mod_vec(m):
                mod_p.wait(dve, m, "sum")
                vec_v.done(dve.tensor_tensor(modv[:, bass.ds(m * KD, KD)], side[:, 4, 0:KD],
                                             pvec[:, bass.ds(m * KD, KD)], ALU.add), "vec")

            def prep_low(g, k0, k1):
                shifted, slots = prep_slots(g)
                for k in range(k0, k1):
                    prep_a.wait(dve, g, f"hi{k}")
                    prep_v.done(dve.tensor_tensor(h_lo[g // 2][:, k, half(g % 2)], shifted[:, k % slots],
                                                  h_hi[g // 2][:, k, half(g % 2)].bitcast(F32), ALU.subtract), f"lo{k}")

            def conv_in(bufs, unit, j, h):
                cv, cg = bufs[0:2]
                part = slice(0 if h else PAD, PAD + NT)
                dve.wait_ge(cv_loaded, unit * 32 + 32)
                cv_a.wait(dve, unit, "sig")
                cv_v.wait(dve, unit - 1, "sum")
                cv_v.done(dve.tensor_tensor(cv[:, part], cv[:, part], cg[:, part], ALU.mult), "u")
                dve.wait_ge(cv_stored, unit * 16)

            def conv_taps(first, count, bufs, unit, j, h):
                for k in range(first, min(first + count, TAPS)):
                    a, tap = bufs[2 + k % 2], taps[:, bass.ds(j + k * CT, 1)]
                    cv_v.wait(dve, unit, f"tap{k - 2}" if k >= 2 else "u")
                    if k == 0:
                        ins = dve.tensor_scalar(a[:], bufs[0][:, 0:NT], tap, pvec[:, bass.ds(j + col["conv_b"], 1)],
                                                ALU.mult, ALU.add)
                    elif k == 1:
                        ins = dve.tensor_scalar(a[:], bufs[0][:, 1:1 + NT], tap, None, ALU.mult)
                    else:
                        ins = dve.scalar_tensor_tensor(a[:], bufs[0][:, k:k + NT], tap, a[:], ALU.mult, ALU.add)
                    cv_v.done(ins, f"tap{k}")

            def conv_out(bufs, unit, j, h):
                cv_v.wait(dve, unit, f"tap{TAPS - 1}")
                cv_v.wait(dve, unit, f"tap{TAPS - 2}")
                cv_v.done(dve.tensor_tensor(bufs[2][:], bufs[2][:], bufs[3][:], ALU.add), "sum")

            def gla_zero():
                g_zero.done(dve.memset(g_st[:], 0.0), "st")
                g_zero.done(dve.memset(g_state[:], 0.0), "state")
                g_zero.done(dve.memset(g_qd[:], 0.0), "qd")
                g_zero.done(dve.memset(g_qb[:], 0.0), "qb")
                g_zero.done(dve.memset(g_ql[:], 0.0), "ql")
                g_zero.done(dve.memset(g_one[:], 1.0), "one")

            def gla_cum(n):
                cum_all = g_cum[:].rearrange("p a t -> p (a t)")
                gla_a.wait(dve, n, f"zb{KT - 1}")
                gla_v.done(dve.tensor_scalar(g_la[:], g_kd[:], 0.0, 1.0 / GATE_TAU, ALU.min, ALU.mult), "min")
                gla_a.wait(dve, n, "zln")
                gla_v.wait(dve, n, "min")
                gla_v.done(dve.scalar_tensor_tensor(g_la[:], g_ecum[:], -1.0 / GATE_TAU, g_la[:], ALU.mult, ALU.add), "la")
                gla_v.wait(dve, n, "la")
                for f in range(KT):
                    gla_v.done(dve.tensor_tensor_scan(g_cum[:, f], g_one[:], g_la[:, f], 0.0, ALU.mult, ALU.add), f"cum{f}")
                gla_v.wait(dve, n, "cum1")
                for l, s in enumerate(LEVELS):
                    c3 = pairs(cum_all, s)
                    gla_v.done(dve.tensor_tensor(pairs(g_lev[:, l], s), c3,
                                                 c3[:, :, s - 1:s].to_broadcast([P, KT * C // (2 * s), 2 * s]),
                                                 ALU.subtract), f"sub{l}")

            def gla_levels(n):
                k_all = g_qk[:, KT:2 * KT].rearrange("p a t -> p (a t)")
                dve.wait_ge(g_loaded, n * 48 + 48)
                gla_a.wait(dve, n, f"kdec{KT - 1}")
                for e in range(2):
                    r = slice(e * HEAD_K, (e + 1) * HEAD_K)
                    gla_v.done(dve.tensor_tensor(g_qd[r, :, e], g_ecum[r], g_qk[r, 0:KT], ALU.mult), f"qd{e}")
                gla_v.done(dve.tensor_tensor(g_kd[:], g_kd[:], g_qk[:, KT:2 * KT], ALU.mult), "kd")
                gla_a.wait(dve, n, "exp")
                for l, s in enumerate(LEVELS):
                    e3 = pairs(g_lev[:, l], s)
                    for e in range(2):
                        r = slice(e * HEAD_K, (e + 1) * HEAD_K)
                        gla_v.done(dve.tensor_tensor(
                            g_ql[r, l, :, e].rearrange("p a (r w) -> p a r w", w=s),
                            g_lev[r, l].rearrange("p (a r w) -> p a r w", a=KT, w=2 * s)[:, :, :, s:2 * s],
                            g_qk[r, 0:KT].rearrange("p a (r w) -> p a r w", w=2 * s)[:, :, :, s:2 * s],
                            ALU.mult), f"q{'ab'[e]}{l}")
                    gla_v.done(dve.tensor_tensor(e3[:, :, 0:s], e3[:, :, 0:s], pairs(k_all, s)[:, :, 0:s],
                                                 ALU.mult), f"k{l}")

            def gla_picks(n):
                gla_p.wait(dve, n, "lev")
                st_all = g_st[:].rearrange("p h t -> p (h t)")
                for l, s in enumerate(LEVELS):
                    w = HEADS * C // 2
                    if l:
                        gla_v.wait(dve, n, f"pick{l - 1}")
                    dve.sem_inc(picks, 1)
                    data = side[:, l // 2, (l % 2) * w:(l % 2 + 1) * w]
                    gla_v.done(dve.copy_predicated(pairs(st_all, s)[:, :, s:2 * s],
                                                   g_mask[:, l * w:(l + 1) * w].rearrange("p (r w) -> p r w", w=s),
                                                   data.rearrange("p (r w) -> p r w", w=s)), f"pick{l}")
                gla_p.wait(dve, n, "diag")
                gla_v.wait(dve, n, f"pick{L[-1]}")
                dve.sem_inc(picks, 1)
                gla_v.done(dve.copy_predicated(st_all, g_mask[:, len(LEVELS) * HEADS * C // 2:], side[:, 4]), "pickd")

            def gla_new_state(n):
                gla_p.wait(dve, n, "state")
                for f in range(KT):
                    gla_v.done(dve.scalar_tensor_tensor(g_state[:, f], g_state[:, f], g_ecum[:, f, C - 1:C],
                                                        side[:, 1, f * DV:(f + 1) * DV], ALU.mult, ALU.add), f"st{f}")

            def gla_out(n):
                gla_a.wait(dve, n, "rstd")
                gla_v.done(dve.tensor_scalar(g_rs[:], g_rs[:], vec("gla_g"), HEAD_K ** -0.5, ALU.mult, ALU.mult), "gain")
                gla_v.wait(dve, n, "gain")
                gla_v.done(dve.tensor_tensor(g_rs[:], side[:, 0], g_rs[:], ALU.mult), "on")

            def in_proj(b, it, chunk=None, taps=(None, None, None), prep=None, mod_block=None):
                first = isinstance(it, int) and it == 0
                if prep is not None and prep != 2:
                    prep_low(prep, 0, KD)
                if chunk is not None:
                    if first:
                        dve.wait_ge(product, NAG)
                        gla_zero()
                        g_zero.wait(dve, 0, "one")
                    gla_cum(chunk)
                    if first:
                        gla_levels(chunk)
                if mod_block is not None:
                    mod_sum(mod_block)
                if mod_block is None and taps[0]:
                    taps[0]()
                if chunk is not None and not first:
                    gla_levels(chunk)
                low(Place(b * NA + RING, 0, it, 1))
                if mod_block is not None and taps[0]:
                    taps[0]()
                if prep == 2:
                    prep_low(prep, 0, KD)
                low(Place(b * NA + RING, 1, it, 1))
                if taps[1] and chunk is None:
                    taps[1]()
                if mod_block is not None:
                    mod_vec(mod_block)
                if chunk is not None:
                    gla_picks(chunk)
                    if taps[1]:
                        taps[1]()
                low(Place(b * NA + RING, 2, it, 1))
                if chunk is not None:
                    gla_new_state(chunk)
                if taps[2]:
                    taps[2]()
                if chunk is not None:
                    gla_out(chunk)

            def conv_part(first, count, unit, j, h):
                def run():
                    if first == 0:
                        conv_in(conv_a, unit, j, h)
                    conv_taps(first, count, conv_a, unit, j, h)
                    if first + count >= TAPS:
                        conv_out(conv_a, unit, j, h)

                return run

            setup_v.done(dve.memset(ones[:], 1.0), "ones")
            setup_v.done(dve.memset(eps[:], EPS), "eps")
            setup_p.wait(dve, 0, "rows")
            setup_v.done(dve.tensor_copy(pvec[:, 0:ncol], side[:, 0, 0:ncol]), "pvec")
            setup_p.wait(dve, 0, "taps")
            setup_v.done(dve.tensor_copy(taps[:], side[:, 1, 0:TAPS * CT]), "taps")
            setup_a.wait(dve, 0, "cact")
            mod_sum(0, m_acc)
            mod_sum(1, m_acc1)
            for s in range(RING):
                low(Place(0, s, 0, 1))
            mod_vec(0)
            mod_vec(1)
            vec_v.wait(dve, 1, "vec")
            gains_v.done(dve.scalar_tensor_tensor(gain1[:], modv[:, KD:2 * KD], 1.0,
                                                  pvec[:, col["g_mix"]:col["g_mix"] + KD], ALU.add, ALU.mult), "g1")
            dve.wait_ge(mask_in, 16)
            setup_v.done(dve.tensor_copy(g_mask[:], mask_f[:]), "mask")
            prep_low(0, 0, KD)
            in_proj(0, 0, prep=1, mod_block=2)
            prep_v.wait(dve, 1, f"lo{KD - 1}")
            setup_v.done(dve.memset(conv_a[0][:, 0:PAD], 0.0), "pad")
            in_proj(0, 1, mod_block=3)
            with dve.Fori(0, CT) as j:
                in_proj(0, j + 2, mod_block=j + 4, taps=(conv_part(0, 14, j, j, 0), conv_part(14, 8, j, j, 0),
                                                         conv_part(22, TAPS, j, j, 0)))
            in_proj(0, AI - 1, prep=2, taps=(None, conv_part(0, 15, CT, 0, 1),
                                             conv_part(15, TAPS, CT, 0, 1)))
            vec_v.wait(dve, 7, "vec")
            gains_v.done(dve.scalar_tensor_tensor(gain2[:], modv[:, 4 * KD:5 * KD], 1.0,
                                                  pvec[:, col["g_ffn"]:col["g_ffn"] + KD], ALU.add, ALU.mult), "g2")
            gains_v.done(dve.scalar_tensor_tensor(gainf[:], modv[:, 7 * KD:8 * KD], 1.0,
                                                  pvec[:, col["g_fin"]:col["g_fin"] + KD], ALU.add, ALU.mult), "gf")
            in_proj(1, 0, prep=3, chunk=0)
            with dve.Fori(0, CT - 1) as j:
                n, u, tile = j * 2 + 1, j + (CT + 1), j + 1
                in_proj(1, n, chunk=n, taps=(None, conv_part(0, 11, u, tile, 1), conv_part(11, 4, u, tile, 1)))
                in_proj(1, n + 1, chunk=n + 1, taps=(conv_part(15, 8, u, tile, 1), conv_part(23, 8, u, tile, 1), None))

            def centre(b):
                for h in range(HB):
                    dve.wait_ge(c_loaded[h], 16 * b + 16)
                    ln_p.wait(dve, b, f"mean{h}")
                    for j in range(CT):
                        ln_v.done(dve.scalar_tensor_tensor(cin[b][:, h, j], stat(b, h), -1.0 / DC, cin[b][:, h, j],
                                                           ALU.mult, ALU.add), f"d{h}{j}")

            def normed(b, h, j):
                ln_a.wait(dve, b, f"rstd{h}")
                ln_v.wait(dve, b, f"d{h}{j}")
                y_v.done(dve.tensor_tensor(cin[b][:, h, j], cin[b][:, h, j], ln_rs[b][:, half(h)], ALU.mult), f"n{h}{j}")

            def y_low(b, h, j):
                y_a.wait(dve, b, f"hi{h}{j}")
                y_v.done(dve.tensor_tensor(y_lo[:, j, half(h)], cin[b][:, h, j], y_hi[:, j, half(h)].bitcast(F32),
                                           ALU.subtract), f"lo{h}{j}")

            def gated(b, h):
                og_a.wait(dve, b, f"s{h}")
                og_v.done(dve.tensor_tensor(oin[b][h], oin[b][h], ogin[b][h], ALU.mult), f"m{h}")

            def gated_low(b, h):
                og_a.wait(dve, b, f"hi{h}")
                og_v.done(dve.tensor_tensor(y_lo[:, CT:KD, half(h)], oin[b][h], y_hi[:, CT:KD, half(h)].bitcast(F32),
                                            ALU.subtract), f"lo{h}")

            def norm_scale(b, h, k):
                n_a.wait(dve, b, f"rstd{h}")
                if h or k >= 2:
                    hk = (h, k - 2) if k >= 2 else (h - 1, KD - 2 + k)
                    n_a.wait(dve, b, f"hi{hk[1]}-{hk[0]}")
                    n_v.wait(dve, b, f"lo{hk[1]}-{hk[0]}")
                n_v.done(dve.scalar_tensor_tensor(n_t[b][:, k % 2], xacc[:, k, half(h)], gain2[:, k:k + 1],
                                                  n_rs[b][:, half(h)], ALU.mult, ALU.mult), f"t{k}-{h}")
                for d in (k - 1,) if k < KD - 1 else (k - 1, k):
                    if d >= 0:
                        n_a.wait(dve, b, f"hi{d}-{h}")
                        n_v.done(dve.scalar_tensor_tensor(h2_lo[:, d, half(h)], n_t[b][:, d % 2], mod(3, d),
                                                          h2_hi[:, d, half(h)].bitcast(F32), ALU.add, ALU.subtract),
                                 f"lo{d}-{h}")

            def beside_projection(b, h, s):
                if h == 0:
                    if s in (0, 1):
                        normed(b, 1, 2 * s)
                        normed(b, 1, 2 * s + 1)
                    if s == 2:
                        gated(b, 1)
                    if s in (3, 4):
                        y_low(b, 1, 2 * s - 6)
                        y_low(b, 1, 2 * s - 5)
                    if s == 5:
                        gated_low(b, 1)
                elif s:
                    norm_scale(b, 0, s - 1)

            def final(b):
                for h in range(HB):
                    e_a.wait(dve, b, f"rstd{h}")
                    for k in range(KD):
                        e_v.done(dve.scalar_tensor_tensor(xacc[:, k, half(h)], xacc[:, k, half(h)], gainf[:, k:k + 1],
                                                          e_rs[:, half(h)], ALU.mult, ALU.mult), f"t{h}{k}")
                for k in range(KD):
                    e_v.wait(dve, b, f"t1{k}")
                    e_v.done(dve.tensor_scalar(xacc[:, k, half(1)], xacc[:, k, half(1)], mod(6, k), None, ALU.add), f"b{k}")

            gla_cum(CH2 - 1)
            centre(0)
            gla_levels(CH2 - 1)
            for b in range(2):
                n0 = NC0 + b * NH
                if b == 0:
                    for j in range(CT):
                        normed(b, 0, j)
                    gla_picks(CH2 - 1)
                    gated(b, 0)
                    for j in range(CT):
                        y_low(b, 0, j)
                    gated_low(b, 0)
                    gla_new_state(CH2 - 1)
                    gla_out(CH2 - 1)
                else:
                    final(0)

                for h in range(HB):
                    for s in range(KD):
                        idx = h * KD + s
                        p = Place(GC0 + b * GH + idx, 0, 0, 1)
                        u = b * SPLIT + idx
                        dve.wait_ge(product, p.number + 1)
                        if s == 0:
                            xt_a.wait(dve, b, f"t{4 * h + 3}")
                        res_v.done(dve.scalar_tensor_tensor(xacc[:, s, half(h)], banks[p.slot][:], mod(2, s),
                                                            xacc[:, s, half(h)], ALU.mult, ALU.add), "x")
                        low(Place(n0 + RING + idx, 0, 0, 1))
                        res_a.wait(dve, u, "sq")
                        if s == 0:
                            if idx or b:
                                n_p.wait(dve, b if h else b - 1, f"ss{1 - h}")
                            res_v.done(dve.tensor_copy(ssq[:], c_sq[b][:, 0]), "ss")
                        else:
                            res_v.wait(dve, u - 1, "ss")
                            res_v.done(dve.tensor_tensor(ssq[:], ssq[:], c_sq[b][:, s % 2], ALU.add), "ss")
                        beside_projection(b, h, s)
                norm_scale(b, 0, KD - 1)
                for k in range(KD):
                    norm_scale(b, 1, k)

                nf, gf = n0 + SPLIT, GC0 + b * GH + KD * HB

                def ffn(i, last=False, chunk=None, conv=None, next_y=False):
                    if chunk is not None:
                        gla_cum(chunk)
                    if next_y:
                        centre(1)
                    for f in range(2):
                        for h in range(HB):
                            u = i * PAIRS + (b * FI * PAIRS + f * HB + h)
                            pu = Place(gf, 2 * (f * HB + h) + 1, i, (4 * HB + OUTS) // RING)
                            f_a.wait(dve, u, "silu")
                            f_a.wait(dve, u - 2, "hi")
                            if h == HB - 1:
                                low(Place(nf + RING, 2 * f, i, 2))
                            dve.wait_ge(product, pu.number + 1)
                            f_v.done(dve.tensor_tensor(af[:, h], banks[pu.slot][:], sil[:, h], ALU.mult), "a")
                            f_a.wait(dve, u, "hi")
                            f_v.done(dve.tensor_tensor(act_lo[:, f, half(h)], af[:, h],
                                                       act_hi[:, f, half(h)].bitcast(F32), ALU.subtract), "lo")
                            if (f, h) == (0, 0) and chunk is not None:
                                gla_levels(chunk)
                            if (f, h) == (1, 0) and chunk is not None:
                                gla_picks(chunk)
                        if f == 0:
                            low(Place(nf + RING, 1, i, 2))
                            if conv:
                                conv_in(conv_d, *conv)
                                conv_taps(0, D_T0, conv_d, *conv)
                            if next_y:
                                for j in range(CT):
                                    normed(1, 0, j)
                    if not last:
                        low(Place(nf + RING, 3, i, 2))
                    if next_y:
                        gated(1, 0)
                    for q in range(OUTS):
                        po = Place(gf, 4 * HB + q, i, (4 * HB + OUTS) // RING)
                        k, h = q % KD, q // KD
                        dve.wait_ge(product, po.number + 1)
                        f_o.done(dve.scalar_tensor_tensor(xacc[:, k, half(h)], banks[po.slot][:], mod(5, k),
                                                          xacc[:, k, half(h)], ALU.mult, ALU.add), f"o{q}")
                        if conv:
                            conv_taps(D_T0 + q, 1, conv_d, *conv)
                        if q == 10 and chunk is not None:
                            gla_new_state(chunk)
                            gla_out(chunk)
                        if next_y and 4 <= q < 4 + CT:
                            y_low(1, 0, q - 4)
                        if next_y and q == 4 + CT:
                            gated_low(1, 0)
                    if not last:
                        low(Place(nf + RING, 4, i, 2))
                        low(Place(nf + RING, 5, i, 2))
                    if conv:
                        conv_taps(D_T0 + OUTS, TAPS, conv_d, *conv)
                        conv_out(conv_d, *conv)

                if b == 0:
                    for h in range(2, 4):
                        with dve.Fori(0, CT) as j:
                            ffn(j + (h - 2) * CT, chunk=j + (CH2 + (h - 2) * CT), conv=(j + h * CT, j, h))
                    with dve.Fori(0, FI - 1 - 2 * CT) as j:
                        ffn(j + 2 * CT)
                    ffn(FI - 1, next_y=True)
                else:
                    with dve.Fori(0, FI - 1) as i:
                        ffn(i)
                    ffn(FI - 1, last=True)
            final(1)

        @block.tensor
        def _(pe):
            gla_p.begin(pe)

            def parts(out_ap, terms, made=None):
                for n, (w1, w2, r1, r2) in enumerate(terms):
                    if made is not None:
                        made(n)
                    pe.matmul(out_ap, w1, r1, start=(n == 0), stop=False)
                    pe.matmul(out_ap, w1, r2, start=False, stop=False)
                    mm = pe.matmul(out_ap, w2, r1, start=False, stop=(n == len(terms) - 1))
                return mm

            def low_made(place):
                pe.wait_ge(w_low, place.number + (RING + 1))

            def mod_add(m, acc=None):
                acc = m_acc if acc is None else acc
                mod_v.wait(pe, m, f"k{KD - 1}")
                if not isinstance(m, int) or m:
                    vec_v.wait(pe, m - 1, "vec")
                for j in range(KD):
                    mm = pe.matmul(side[:, 4, j:j + 1], acc[:, j * P:(j + 1) * P], ones[:, 0:1], start=True, stop=True)
                mod_p.done(mm, "sum")

            def prep_turn(g, k0, k1):
                for k in range(k0, k1):
                    prep_a.wait(pe, g, "xn3")
                    prep_a.wait(pe, g if k >= 4 else g - 1, f"t{(k - 4) % KD}")
                    for t in range(4):
                        mm = pe.transpose(side[:, k % 4, t * P:(t + 1) * P], xnat[g][:, t, k * P:(k + 1) * P], ident[:])
                    prep_p.done(mm, f"k{k}")

            def gla_z(n):
                if isinstance(n, int) and n == 0:
                    prep_a.wait(pe, 3, f"t{KD - 1}")
                pe.wait_ge(g_loaded, n * 48 + 48)
                for f in range(KT):
                    mm = pe.matmul(side[:, 3, f * C:(f + 1) * C], a2[0:RANK, f * P:(f + 1) * P], g_al[0:RANK, :],
                                   start=True, stop=True)
                gla_p.done(mm, "z")

            def gla_turn(n):
                gla_v.wait(pe, n - 1, "on")
                for h in range(HEADS):
                    mm = pe.transpose(side[:, 0, h * C:(h + 1) * C], g_vt[:, h], ident[:])
                gla_p.done(mm, "vn")
                gla_v.wait(pe, n, "kd")
                for f in range(KT):
                    mm = pe.transpose(side[:, 1, f * P:(f + 1) * P], g_kd[:, f], ident[:])
                gla_p.done(mm, "kn")

            def gla_scores(n):
                w = HEADS * C // 2
                gla_v.wait(pe, n, f"k{L[-1]}")
                gla_a.wait(pe, n, "kn")
                for l in L:
                    for f in range(KT):
                        o = (l % 2) * w + f * C
                        mm = pe.matmul(side[:, l // 2, o:o + C], g_lev[:, l, f * C:(f + 1) * C],
                                       g_ql[:, l, f].rearrange("p e t -> p (e t)"), start=True, stop=True)
                gla_p.done(mm, "lev")
                for f in range(KT):
                    mm = pe.matmul(side[:, 4, f * 2 * C:(f + 1) * 2 * C], g_qk[:, KT + f],
                                   g_qb[:, f].rearrange("p e t -> p (e t)"), start=True, stop=True)
                gla_p.done(mm, "diag")

            def gla_apply(n):
                gla_v.wait(pe, n, "pickd")
                gla_v.wait(pe, n - 1, "st1")
                for f in range(KT):
                    pe.matmul(side[:, 0, f * 2 * C:(f + 1) * 2 * C], g_state[:, f],
                              g_qd[:, f].rearrange("p e t -> p (e t)"), start=True, stop=True, skip_group_check=True)
                    for h in range(2 * f, 2 * f + 2):
                        mm = pe.matmul(side[:, 0, h * C:(h + 1) * C], g_vn[:, h * DV:(h + 1) * DV], g_st[:, h],
                                       start=False, stop=True, skip_group_check=True)
                gla_p.done(mm, "o")
                for h in range(HEADS):
                    f, r = h // 2, slice((h % 2) * HEAD_K, (h % 2 + 1) * HEAD_K)
                    mm = pe.matmul(side[r, 1, f * DV:(f + 1) * DV], g_kn[:, h * HEAD_K:(h + 1) * HEAD_K],
                                   g_vn[:, h * DV:(h + 1) * DV], start=True, stop=True)
                gla_p.done(mm, "state")

            def gla_norm(n):
                gla_a.wait(pe, n, "sq")
                gla_p.done(pe.matmul(side[:, 2], ones[:], g_rs[:], start=True, stop=True), "ss")

            def in_proj(b, it, chunk=None, prep=None, mods=()):
                for n, (s, h) in enumerate(a_order(it)):
                    if prep is not None:
                        if n == PREP_AT[prep]:
                            prep_turn(prep, 0, 4)
                        if n == PREP_AT[prep] + 1:
                            prep_turn(prep, 4, KD)
                    if h == 0:
                        low_made(Place(b * NA, s, it, 1))
                    first = isinstance(it, int) and it == 0 and s == 0
                    if chunk is not None and n == gla_slots(it)[0]:
                        gla_z(chunk)
                    p = a_place(b, it, s, h)
                    staged.wait(pe, p.number - RING, "copy")
                    parts(banks[p.slot][:], [(w_hi[:, s, k], w_lo[:, s, k], h_hi[b][:, k, half(h)], h_lo[b][:, k, half(h)])
                                             for k in range(KD)],
                          (lambda k: prep_v.wait(pe, 2 * b + h, f"lo{k}")) if first else None).then_inc(product, 1)
                    if chunk is not None:
                        if n == gla_slots(it)[1]:
                            gla_turn(chunk)
                        if n == gla_slots(it)[2]:
                            gla_scores(chunk)
                        if n == gla_slots(it)[3]:
                            gla_apply(chunk)
                            gla_norm(chunk)
                    if mods and n == 4:
                        mod_add(mods[0])

            pe.wait_ge(const_in, 16 * (1 + len(names) + 2))
            setup_p.done(pe.transpose(side[:, 0, 0:ncol], rows[0:ncol, 0, :], ident[0:ncol, 0:ncol]), "rows")
            setup_p.done(pe.transpose(side[:, 1, 0:TAPS * CT], rows[0:TAPS * CT, 1, :],
                                      ident[0:TAPS * CT, 0:TAPS * CT]), "taps")
            setup_v.wait(pe, 0, "taps")
            mod_add(0)
            prep_turn(0, 0, 4)
            mod_add(1, m_acc1)
            prep_turn(0, 4, KD)
            in_proj(0, 0, prep=1, mods=(2,))
            in_proj(0, 1, mods=(3,))
            with pe.Fori(0, CT) as j:
                in_proj(0, j + 2, mods=(j + 4,))
            in_proj(0, AI - 1, prep=2)
            in_proj(1, 0, prep=3, chunk=0)
            with pe.Fori(0, AI - 1) as j:
                in_proj(1, j + 1, chunk=j + 1)

            def means(b):
                for h in range(HB):
                    pe.wait_ge(c_loaded[h], 16 * b + 16)
                    for j in range(CT):
                        mm = pe.matmul(stat(b, h), ones[:], cin[b][:, h, j], start=(j == 0), stop=(j == CT - 1))
                    ln_p.done(mm, f"mean{h}")

            def variance(b, h):
                ln_v.wait(pe, b, f"d{h}{CT - 1}")
                for j in range(CT):
                    ln_a.wait(pe, b, f"q{j}-{h}")
                    ln_p.done(pe.matmul(stat(b, h), ones[:], ln_sq[b][:, j % 2], start=(j == 0), stop=(j == CT - 1)),
                              f"v{h}{j}")

            def turn(b, t):
                slot = X_SLOT[t]
                pe.wait_ge(x2_loaded[slot], 16 * (b * X_SLOT.count(slot) + X_SLOT[:t + 1].count(slot)))
                if t >= 2:
                    xt_a.wait(pe, b, f"t{t - 2}")
                for k in range(KD):
                    mm = pe.transpose(side[:, 2 * (t % 2) + k // 4, (k % 4) * P:(k % 4 + 1) * P],
                                      x_slot(b, t)[:, k // 4, (k % 4) * P:(k % 4 + 1) * P], ident[:])
                xt_p.done(mm, f"t{t}")

            def norm_sum(b, h):
                res_v.wait(pe, b * SPLIT + (h + 1) * KD - 1, "ss")
                if h:
                    n_a.wait(pe, b, "ln0")
                n_p.done(pe.matmul(side[:, 4], ones[:], ssq[:], start=True, stop=True), f"ss{h}")

            def final_sum(b, h, k):
                if h and k == 0:
                    e_a.wait(pe, b, "ln0")
                e_a.wait(pe, b, f"sq{h}{k}")
                e_p.done(pe.matmul(side[:, 4], ones[:], e_sq[:, k % 2], start=(k == 0), stop=(k == KD - 1)), f"ss{h}{k}")

            def final_turn(b, h):
                for t in range(h * NT // P, (h + 1) * NT // P):
                    (e_v if h else e_a).wait(pe, b, f"b{KD - 1}")
                    if t >= 2:
                        e_c.wait(pe, b, f"t{t - 2}")
                    for k in range(KD):
                        mm = pe.transpose(side[:, 2 * (t % 2) + k // 4, (k % 4) * P:(k % 4 + 1) * P],
                                          xacc[:, k, t * P:(t + 1) * P], ident[:])
                    e_p.done(mm, f"t{t}")

            gla_z(CH2 - 1)
            staged.wait(pe, 2 * NAG - 1, "copy")
            means(0)
            for h in range(HB):
                variance(0, h)
            gla_turn(CH2 - 1)
            gla_scores(CH2 - 1)
            gla_apply(CH2 - 1)
            for b in range(2):
                n0, g0 = NC0 + b * NH, GC0 + b * GH
                if b:
                    for k in range(KD):
                        final_sum(0, 1, k)

                for h in range(HB):
                    def y_made(k):
                        if k < CT:
                            y_v.wait(pe, b, f"lo{h}{k}")
                        elif k == CT:
                            og_v.wait(pe, b, f"lo{h}")

                    for s in range(KD):
                        idx = h * KD + s
                        p, pb = Place(n0 + idx, 0, 0, 1), Place(g0 + idx, 0, 0, 1)
                        u = b * SPLIT + idx
                        low_made(p)
                        if idx >= RING:
                            res_v.wait(pe, u - RING, "x")
                        parts(banks[pb.slot][:], [(w_hi[:, p.slot, k], w_lo[:, p.slot, k], y_hi[:, k, half(h)],
                                                   y_lo[:, k, half(h)]) for k in range(KD)],
                              y_made if s == 0 else None).then_inc(product, 1)
                        if b and idx < HB:
                            final_turn(0, idx)
                        if b == 0 and idx == 0:
                            gla_norm(CH2 - 1)
                        if b == 0 and idx == 1:
                            gla_v.wait(pe, CH2 - 1, "on")
                            turn(b, 0)
                            turn(b, 1)
                        if idx == 2:
                            if b:
                                e_c.wait(pe, 0, f"t{TT - 1}")
                            for t in range(0 if b else 2, 4):
                                turn(b, t)
                        if 3 <= idx < 7:
                            turn(b, idx + 1)
                        if idx == KD:
                            norm_sum(b, 0)
                norm_sum(b, 1)

                nf, gf = n0 + SPLIT, g0 + KD * HB
                per = (4 * HB + OUTS) // RING

                def ffn(i, chunk=None, next_y=False):
                    it = i + b * FI
                    if chunk is not None:
                        gla_z(chunk)
                    if next_y:
                        means(1)
                    for f in range(2):
                        for h in range(HB):
                            x_ = f * HB + h
                            u = i * PAIRS + (b * FI * PAIRS + x_)
                            for up in range(2):
                                w = Place(nf, 2 * f + up, i, 2)
                                pg = Place(gf, 2 * x_ + up, i, per)
                                if h == 0:
                                    low_made(w)
                                if 2 * x_ + up < RING:
                                    f_o.wait(pe, it - 1, f"o{OUTS - RING + 2 * x_ + up}")
                                elif up:
                                    f_a.wait(pe, u - 1, "silu")
                                else:
                                    f_v.wait(pe, u - 2, "a")
                                parts(banks[pg.slot][:], [(w_hi[:, w.slot, k], w_lo[:, w.slot, k], h2_hi[:, k, half(h)],
                                                           h2_lo[:, k, half(h)]) for k in range(KD)],
                                      (lambda k: n_v.wait(pe, b, f"lo{k}-{h}")) if f == up == 0 else None).then_inc(product, 1)
                                if chunk is not None:
                                    if 2 * x_ + up == 3:
                                        gla_turn(chunk)
                                    if 2 * x_ + up == 5:
                                        gla_scores(chunk)
                        if f == 0 and next_y:
                            for h in range(HB):
                                variance(1, h)
                    if chunk is not None:
                        gla_apply(chunk)
                    last = i * PAIRS + (b * FI * PAIRS + PAIRS - 1)
                    wd = [Place(nf, 4 + f, i, 2) for f in range(2)]
                    low_made(wd[1])
                    for q in range(OUTS):
                        k, h = q % KD, q // KD
                        po = Place(gf, 4 * HB + q, i, per)
                        if q == 0:
                            f_v.wait(pe, last - 1, "lo")
                        elif q == 1:
                            f_a.wait(pe, last, "silu")
                        elif q == 2:
                            f_v.wait(pe, last, "a")
                        else:
                            f_o.wait(pe, it, f"o{q - RING}")
                        if q == KD:
                            f_v.wait(pe, last, "lo")
                        parts(banks[po.slot][:], [(w_hi[:, wd[f].slot, k], w_lo[:, wd[f].slot, k], act_hi[:, f, half(h)],
                                                   act_lo[:, f, half(h)]) for f in range(2)]).then_inc(product, 1)
                        if q == RING and chunk is not None:
                            gla_norm(chunk)
                        if isinstance(i, int) and q > KD:
                            final_sum(b, 0, q - KD - 1)
                    if isinstance(i, int):
                        final_sum(b, 0, KD - 1)

                if b == 0:
                    with pe.Fori(0, 2 * CT) as i:
                        ffn(i, chunk=i + CH2)
                    with pe.Fori(0, FI - 1 - 2 * CT) as i:
                        ffn(i + 2 * CT)
                    ffn(FI - 1, next_y=True)
                else:
                    with pe.Fori(0, FI - 1) as i:
                        ffn(i)
                    ffn(FI - 1)

            for k in range(KD):
                final_sum(1, 1, k)
            for h in range(HB):
                final_turn(1, h)


def masks():
    j = np.arange(C)[:, None]
    rows = []
    for s in LEVELS:
        i = np.arange(C).reshape(-1, 2 * s)[:, s:].reshape(1, -1)
        keep = (i // (2 * s) == j // (2 * s)) & (j % (2 * s) < s)
        rows.append(np.tile(keep, (1, 4)))
    rows.append(np.tile(np.eye(C, dtype=bool), (1, 4)))
    return np.concatenate(rows, axis=1).astype(np.float32)


_INS = ["x", "c", "w_ada", "b_ada", "g_mix", "w_in", "conv_w", "conv_b", "ln_g", "ln_b", "w_a2", "b_a2",
        "gla_norm_g", "w_out", "g_ffn", "w_ffn_in", "w_ffn_out", "w_ada_final", "b_ada_final", "g_final"]


def kernel(**inputs):
    import concourse.bacc as bacc
    from concourse.bass_utils import run_bass_kernel_spmd

    nc = bacc.Bacc("TRN2", target_bir_lowering=False, num_devices=1)
    arrays, args = {}, {}
    data = {name: np.ascontiguousarray(inputs[name]) for name in _INS}
    data["identity"] = np.eye(P, dtype=np.float32)
    data["level_masks"] = masks()
    for name, a in data.items():
        arrays[f"in_{name}"] = a
        args[name] = nc.dram_tensor(f"in_{name}", a.shape, mybir.dt.from_np(a.dtype), kind="ExternalInput").ap()
    shape = data["x"].shape
    o = nc.dram_tensor("out_0", shape, F32, kind="ExternalOutput").ap()
    block_kernel(nc, **args, out=o)
    r = run_bass_kernel_spmd(nc, [arrays], core_ids=[0])
    return np.asarray(r.results[0]["out_0"])
```
